# Optimizing a Trainium2 kernel written in Bass

```python
import jax, jax.numpy as jnp
from jax import lax
import numpy as np

D_MODEL = 1024
BATCH = 1
SEQ = 1024
DEPTH = 2
DEC_BATCH = 8
DEC_SEQ = 16
PAST_LEN = 256

CHUNK = 64
N_A_LAYERS = DEPTH // 2
N_B_LAYERS = DEPTH - N_A_LAYERS
EPS = 1e-6
GLA_HEADS = 4
GLA_DK = D_MODEL // 2 // GLA_HEADS
GLA_DV = D_MODEL // GLA_HEADS
GLA_GATE_RANK = 16
GLA_TAU = 16.0
GLA_BLOCK = 64
GLA_IN = 2 * GLA_HEADS * GLA_DK + 2 * GLA_HEADS * GLA_DV + GLA_GATE_RANK
ATT_HEADS = 16
ATT_DH = D_MODEL // ATT_HEADS
N_PAST_CHUNKS = 8
BAND_PAST = N_PAST_CHUNKS * CHUNK
BAND = BAND_PAST + CHUNK
REL_CLIP = 128
NEG_INF = -1e30
D_FF = -(-8 * D_MODEL // (3 * 256)) * 256

kernel_name = "yoco_gla_chunkband_stream_step"

def _rmsnorm(x, g):
    xf = x.astype(jnp.float32)
    y = xf * lax.rsqrt(jnp.mean(xf * xf, axis=-1, keepdims=True) + EPS)
    return (y * g.astype(jnp.float32)).astype(x.dtype)

def _swiglu(h, wg, wu, wd):
    return (jax.nn.silu(h @ wg) * (h @ wu)) @ wd

def _gla_block(q, k, v, la, s):
    L = q.shape[1]
    b = jnp.cumsum(la, axis=1)
    qd = q * jnp.exp(b)
    kd = k * jnp.exp(-b)
    a = jnp.einsum('blhk,bshk->bhls', qd, kd)
    a = jnp.where(jnp.tril(jnp.ones((L, L), dtype=bool)), a, 0.0)
    o = jnp.einsum('blhk,bhkv->blhv', qd, s) + jnp.einsum('bhls,bshv->blhv', a, v)
    b_last = b[:, -1]
    s_new = s * jnp.exp(b_last)[..., None] + jnp.einsum(
        'bshk,bshv->bhkv', k * jnp.exp(b_last[:, None] - b), v)
    return o, s_new

def _gla_mixer(hn, s0, w_in, w_gate2, b_gate, norm_g, w_out):
    B, T, _ = hn.shape
    nk, nv = GLA_HEADS * GLA_DK, GLA_HEADS * GLA_DV
    z = hn @ w_in
    q, k, v, g, a = jnp.split(z, [nk, 2 * nk, 2 * nk + nv, 2 * nk + 2 * nv], axis=-1)
    q = q.reshape(B, T, GLA_HEADS, GLA_DK).astype(jnp.float32) * (GLA_DK ** -0.5)
    k = k.reshape(B, T, GLA_HEADS, GLA_DK).astype(jnp.float32)
    v = v.reshape(B, T, GLA_HEADS, GLA_DV).astype(jnp.float32)
    logit = (a @ w_gate2 + b_gate).astype(jnp.float32)
    la = (jax.nn.log_sigmoid(logit) / GLA_TAU).reshape(B, T, GLA_HEADS, GLA_DK)
    blk = GLA_BLOCK if T % GLA_BLOCK == 0 else T
    nb = T // blk

    def to_blocks(t):
        return t.reshape(B, nb, blk, *t.shape[2:]).swapaxes(0, 1)

    def body(s, xs):
        o_b, s = _gla_block(xs[0], xs[1], xs[2], xs[3], s)
        return s, o_b

    s_fin, o = lax.scan(body, s0, (to_blocks(q), to_blocks(k), to_blocks(v), to_blocks(la)))
    o = o.swapaxes(0, 1).reshape(B, T, GLA_HEADS, GLA_DV)
    o = o * lax.rsqrt(jnp.mean(o * o, axis=-1, keepdims=True) + EPS)
    o = o * norm_g.astype(jnp.float32).reshape(GLA_HEADS, GLA_DV)
    o = o.reshape(B, T, nv).astype(hn.dtype)
    return (o * jax.nn.silu(g)) @ w_out, s_fin

def _shared_kv(h, kv_norm, w_kv):
    B, T, _ = h.shape
    z = _rmsnorm(h, kv_norm) @ w_kv
    k, v = jnp.split(z, 2, axis=-1)
    return (k.reshape(B, T, ATT_HEADS, ATT_DH), v.reshape(B, T, ATT_HEADS, ATT_DH))

def _rel_bias(table, n_q, n_k, offset):
    a = jnp.arange(n_q)[:, None]
    j = jnp.arange(n_k)[None, :]
    idx = jnp.clip(offset + a - j, -REL_CLIP, REL_CLIP) + REL_CLIP
    return table[:, idx].astype(jnp.float32)

def _attend(q, k, v, bias, valid):
    s = jnp.einsum('bqhd,bkhd->bhqk', q, k, preferred_element_type=jnp.float32)
    s = s * (ATT_DH ** -0.5) + bias[None]
    if valid is not None:
        s = jnp.where(valid, s, NEG_INF)
    p = jax.nn.softmax(s, axis=-1)
    return jnp.einsum('bhqk,bkhd->bqhd', p.astype(v.dtype), v)

def _band_prompt(hn, k, v, w_q, table, w_out):
    B, T, _ = hn.shape
    nc = T // CHUNK
    q = (hn @ w_q).reshape(B, T, ATT_HEADS, ATT_DH)
    pad = ((0, 0), (BAND_PAST, 0), (0, 0), (0, 0))
    kp, vp = jnp.pad(k, pad), jnp.pad(v, pad)
    bias = _rel_bias(table, CHUNK, BAND, BAND_PAST)
    r = jnp.arange(BAND)

    def one_chunk(c):
        start = c * CHUNK
        qc = lax.dynamic_slice_in_dim(q, start, CHUNK, axis=1)
        kc = lax.dynamic_slice_in_dim(kp, start, BAND, axis=1)
        vc = lax.dynamic_slice_in_dim(vp, start, BAND, axis=1)
        valid = (r >= BAND_PAST - start)[None, None, None, :]
        return _attend(qc, kc, vc, bias, valid)

    o = lax.map(one_chunk, jnp.arange(nc))
    o = o.swapaxes(0, 1).reshape(B, T, ATT_HEADS * ATT_DH)
    return o @ w_out

def _band_sample(hn, k_all, v_all, n_past, w_q, table, w_out):
    B, L, _ = hn.shape
    q = (hn @ w_q).reshape(B, L, ATT_HEADS, ATT_DH)
    bias = _rel_bias(table, L, n_past + L, n_past)
    o = _attend(q, k_all, v_all, bias, None)
    return o.reshape(B, L, ATT_HEADS * ATT_DH) @ w_out

def _trunk(x, state, ck, cv, prompt, norm_mix, norm_ffn, norm_final, gla_w_in, gla_w_gate2,
           gla_b_gate, gla_norm, gla_w_out, kv_norm, w_kv, attn_w_q, attn_rel_bias,
           attn_w_out, ffn_w_gate, ffn_w_up, ffn_w_down):
    bsz, T, _ = x.shape
    h = x
    new_s = []
    for l in range(DEPTH):
        hn = _rmsnorm(h, norm_mix[l])
        if l < N_A_LAYERS:
            if prompt:
                s0 = jnp.zeros((bsz, GLA_HEADS, GLA_DK, GLA_DV), jnp.float32)
            else:
                s0 = state[l].astype(jnp.float32)
            o, s1 = _gla_mixer(hn, s0, gla_w_in[l], gla_w_gate2[l], gla_b_gate[l],
                               gla_norm[l], gla_w_out[l])
            new_s.append(s1.astype(x.dtype))
        else:
            if l == N_A_LAYERS:
                k, v = _shared_kv(h, kv_norm, w_kv)
                if prompt:
                    keep = min(BAND_PAST, T)
                    new_k, new_v = k[:, T - keep:], v[:, T - keep:]
                else:
                    n_past = ck.shape[1]
                    k_all = jnp.concatenate([ck.astype(k.dtype), k], axis=1)
                    v_all = jnp.concatenate([cv.astype(v.dtype), v], axis=1)
                    new_k, new_v = k_all[:, T:], v_all[:, T:]
            i = l - N_A_LAYERS
            if prompt:
                o = _band_prompt(hn, k, v, attn_w_q[i], attn_rel_bias[i], attn_w_out[i])
            else:
                o = _band_sample(hn, k_all, v_all, n_past, attn_w_q[i], attn_rel_bias[i],
                                 attn_w_out[i])
        h = h + o
        h = h + _swiglu(_rmsnorm(h, norm_ffn[l]), ffn_w_gate[l], ffn_w_up[l], ffn_w_down[l])
    return _rmsnorm(h, norm_final), jnp.stack(new_s), new_k, new_v

def setup_inputs(seed: int = 0) -> dict:
    key = jax.random.key(seed)
    ks = jax.random.split(key, 24)
    f32 = jnp.float32
    win = min(BAND_PAST, PAST_LEN)
    nrm = lambda k, shape, s: jax.random.normal(k, shape, f32) * s
    return {
        "x_prompt": nrm(ks[0], (BATCH, SEQ, D_MODEL), 1.0),
        "x_sample": nrm(ks[1], (DEC_BATCH, DEC_SEQ, D_MODEL), 1.0),
        "state_gla": nrm(ks[2], (N_A_LAYERS, DEC_BATCH, GLA_HEADS, GLA_DK, GLA_DV), 1.0),
        "cache_k": nrm(ks[3], (DEC_BATCH, win, ATT_HEADS, ATT_DH), 1.0),
        "cache_v": nrm(ks[4], (DEC_BATCH, win, ATT_HEADS, ATT_DH), 1.0),
        "norm_mix": 1.0 + nrm(ks[5], (DEPTH, D_MODEL), 0.02),
        "norm_ffn": 1.0 + nrm(ks[6], (DEPTH, D_MODEL), 0.02),
        "norm_final": 1.0 + nrm(ks[7], (D_MODEL,), 0.02),
        "gla_w_in": nrm(ks[8], (N_A_LAYERS, D_MODEL, GLA_IN), D_MODEL ** -0.5),
        "gla_w_gate2": nrm(ks[9], (N_A_LAYERS, GLA_GATE_RANK, GLA_HEADS * GLA_DK), GLA_GATE_RANK ** -0.5),
        "gla_b_gate": nrm(ks[10], (N_A_LAYERS, GLA_HEADS * GLA_DK), 0.1),
        "gla_norm": 1.0 + nrm(ks[11], (N_A_LAYERS, GLA_HEADS * GLA_DV), 0.02),
        "gla_w_out": nrm(ks[12], (N_A_LAYERS, GLA_HEADS * GLA_DV, D_MODEL), (GLA_HEADS * GLA_DV) ** -0.5),
        "kv_norm": 1.0 + nrm(ks[13], (D_MODEL,), 0.02),
        "w_kv": nrm(ks[14], (D_MODEL, 2 * ATT_HEADS * ATT_DH), D_MODEL ** -0.5),
        "attn_w_q": nrm(ks[15], (N_B_LAYERS, D_MODEL, ATT_HEADS * ATT_DH), D_MODEL ** -0.5),
        "attn_rel_bias": nrm(ks[16], (N_B_LAYERS, ATT_HEADS, 2 * REL_CLIP + 1), 0.5),
        "attn_w_out": nrm(ks[17], (N_B_LAYERS, ATT_HEADS * ATT_DH, D_MODEL), (ATT_HEADS * ATT_DH) ** -0.5),
        "ffn_w_gate": nrm(ks[18], (DEPTH, D_MODEL, D_FF), D_MODEL ** -0.5),
        "ffn_w_up": nrm(ks[19], (DEPTH, D_MODEL, D_FF), D_MODEL ** -0.5),
        "ffn_w_down": nrm(ks[20], (DEPTH, D_FF, D_MODEL), D_FF ** -0.5),
    }

def reference(x_prompt, x_sample, state_gla, cache_k, cache_v, norm_mix, norm_ffn, norm_final,
              gla_w_in, gla_w_gate2, gla_b_gate, gla_norm, gla_w_out, kv_norm, w_kv,
              attn_w_q, attn_rel_bias, attn_w_out, ffn_w_gate, ffn_w_up, ffn_w_down):
    y_prompt, state_gla_prompt, cache_k_prompt, cache_v_prompt = _trunk(
        x_prompt, None, None, None, True, norm_mix, norm_ffn, norm_final, gla_w_in,
        gla_w_gate2, gla_b_gate, gla_norm, gla_w_out, kv_norm, w_kv, attn_w_q,
        attn_rel_bias, attn_w_out, ffn_w_gate, ffn_w_up, ffn_w_down)
    y_sample, state_gla_sample, cache_k_sample, cache_v_sample = _trunk(
        x_sample, state_gla, cache_k, cache_v, False, norm_mix, norm_ffn, norm_final,
        gla_w_in, gla_w_gate2, gla_b_gate, gla_norm, gla_w_out, kv_norm, w_kv, attn_w_q,
        attn_rel_bias, attn_w_out, ffn_w_gate, ffn_w_up, ffn_w_down)
    return (y_prompt, y_sample, state_gla_prompt, cache_k_prompt, cache_v_prompt,
            state_gla_sample, cache_k_sample, cache_v_sample)


_drawn_inputs = setup_inputs


def setup_inputs(seed=0):
    import zlib

    import numpy as np

    out = dict(_drawn_inputs(seed))
    spreads = {}
    factors = {'norm_ffn': 2.968, 'norm_final': 8.212, 'gla_norm': 4.575, 'kv_norm': 7.534}
    for name, (base, spread) in spreads.items():
        noise = np.random.default_rng([zlib.crc32(name.encode()), seed]).standard_normal(out[name].shape)
        drawn = base * np.exp(spread * noise) if base else spread * noise
        out[name] = __import__('jax').numpy.asarray(drawn.astype(out[name].dtype))
    for name, factor in factors.items():
        out[name] = (out[name] * factor).astype(out[name].dtype)
    return out
```

```python
from contextlib import ExitStack, contextmanager

import concourse.bass as bass
from concourse import mybir

F32 = mybir.dt.float32
F32R = mybir.dt.float32r
I32 = mybir.dt.int32
ALU = mybir.AluOpType
ACT = mybir.ActivationFunctionType

P = 128
D = 1024
DK = D // P
SEQ = 1024
DEC_B, DEC_S = 8, 16
DEC = DEC_B * DEC_S
TOK = SEQ + DEC
NT = TOK // P
GRP = 384
NG = TOK // GRP
EPS = 1e-6
GLA_H, GLA_DK, GLA_DV, GLA_BLOCK, GLA_TAU, RANK = 4, 128, 256, 64, 16.0, 16
NQK, NV = GLA_H * GLA_DK, GLA_H * GLA_DV
GLA_IN = 2 * NQK + 2 * NV + RANK
HEADS, DH = 16, 64
PAIRS = HEADS // 2
PAST = 256
CHUNK = 64
BAND_T = 5
CLIP = 128
D_FF = 2816
MASKED = 1e30
STRIP = 400
STRIP_C = STRIP - (2 * CLIP + 1)

G_MIX0, G_MIX1, G_FFN0, G_FFN1, G_FINAL, G_KV = range(6)


class Ring:

    def __init__(self, slots, stages):
        self.slots, self.stages = slots, stages


class Segment:

    def __init__(self, w, col, units, gain, out, row, skip, base, slots):
        self.w, self.col, self.gain, self.out, self.row, self.skip = (
            w.rearrange("(k p) n -> p k n", p=P), col, gain, out, row, skip)
        self.per = min(slots, units)
        self.trips = units // self.per
        self.base, self.turn = base, base // slots
        assert base % slots == 0 and units % self.per == 0


class Shared:
    pass


def f32(ap):
    return ap.bitcast(F32)


@contextmanager
def semaphores(nc):
    made = []

    def sem(name):
        made.append(nc.alloc_semaphore(name))
        return made[-1]

    yield sem
    nc.clear_and_free_semaphores(made)
    nc.all_engine_barrier()


def weight_ring(nc, sem, ctx, tag, slots, stages):
    r = Ring(slots, stages)
    r.stage = ctx.enter_context(nc.sbuf_tensor(f"{tag}_stage", [P, stages, D], F32))
    r.hi = ctx.enter_context(nc.sbuf_tensor(f"{tag}_w_hi", [P, slots, D], F32R))
    r.lo = ctx.enter_context(nc.sbuf_tensor(f"{tag}_w_lo", [P, slots, D], F32R))
    r.loaded = [sem(f"{tag}_w_loaded{i}") for i in range(stages)]
    r.scaled = sem(f"{tag}_w_scaled")
    r.rounded = sem(f"{tag}_w_rounded")
    r.split = sem(f"{tag}_w_split")
    return r


def fetch_unit(sp, r, unit, j, src):
    sp.wait_ge(r.split, unit + 1)
    sp.dma_start(r.stage[:, j % r.stages, :].rearrange("p (k n) -> p k n", n=src.shape[-1]) if len(src.shape) == 3
                 else r.stage[:, j % r.stages, :], src).then_inc(r.loaded[j % r.stages], 16)


def scale_unit(pool, r, unit, j, times, gain):
    pool.wait_ge(r.loaded[j % r.stages], 16 * (times + 1))
    st = r.stage[:, j % r.stages, :].rearrange("p (k n) -> p k n", n=P)
    pool.tensor_tensor(st, st, gain.unsqueeze(2).to_broadcast([P, DK, P]), ALU.mult).then_inc(r.scaled, 1)


def round_unit(act, r, unit, j, times, gain=None):
    if gain is None:
        act.wait_ge(r.loaded[j % r.stages], 16 * (times + 1))
    else:
        act.wait_ge(r.scaled, unit + 1)
    act.copy(r.hi[:, j % r.slots, :], r.stage[:, j % r.stages, :]).then_inc(r.rounded, 1)


def split_unit(pool, r, unit, j):
    pool.wait_ge(r.rounded, unit + 1)
    pool.tensor_tensor(r.lo[:, j % r.slots, :], r.stage[:, j % r.stages, :], f32(r.hi[:, j % r.slots, :]),
                       ALU.subtract).then_inc(r.split, 1)


def product(pe, out, w_hi, w_lo, x_hi, x_lo, first, last):
    pe.matmul(out, w_hi, x_hi, start=first, stop=False)
    pe.matmul(out, w_lo, x_hi, start=False, stop=False)
    return pe.matmul(out, w_hi, x_lo, start=False, stop=last)


def constants(nc, S, a):
    with semaphores(nc) as sem:
        gains_in, made, strip_in, strip_made, strip_out = (sem(n) for n in (
            "gains_in", "consts_made", "strip_in", "strip_made", "strip_out"))
        with ExitStack() as ctx:
            table = ctx.enter_context(nc.sbuf_tensor("bias_table", [HEADS, 2 * CLIP + 1], F32))
            strip = ctx.enter_context(nc.sbuf_tensor("bias_strip", [HEADS, STRIP], F32))
            block = ctx.enter_context(nc.Block())

            @block.sync
            def _(sp):
                rows = [a["norm_mix"][0], a["norm_mix"][1], a["norm_ffn"][0], a["norm_ffn"][1],
                        a["norm_final"], a["kv_norm"]]
                sp.dma_start(table[:], a["attn_rel_bias"][0]).then_inc(strip_in, 16)
                for i, row in enumerate(rows):
                    sp.dma_start(S.gains[:, i, :], row.rearrange("(k p) -> p k", p=P),
                                 allow_slow_non_contiguous=True).then_inc(gains_in, 16)
                sp.wait_ge(strip_made, 2)
                sp.dma_start(S.strips.rearrange("h r c -> h r c"),
                             strip[:].unsqueeze(1).to_broadcast([HEADS, P, STRIP])).then_inc(strip_out, 16)
                sp.wait_ge(gains_in, 16 * len(rows))
                sp.wait_ge(strip_out, 16)

            @block.vector
            def _(dve):
                dve.wait_ge(strip_in, 16)
                dve.tensor_scalar(strip[:, STRIP_C:], table[:, ::-1], -1.0, None, ALU.mult).then_inc(strip_made, 1)
                dve.tensor_scalar(strip[:, :STRIP_C], table[:, 2 * CLIP:].to_broadcast([HEADS, STRIP_C]), -1.0, None,
                                  ALU.mult).then_inc(strip_made, 1)

            @block.gpsimd
            def _(pool):
                n = [0]

                def step(ins):
                    n[0] += 1
                    ins.then_inc(made, 1)
                    pool.wait_ge(made, n[0])

                step(pool.memset(S.ident[:], 0.0))
                step(pool.affine_select(S.ident[:], S.ident[:], [[-1, P]], ALU.not_equal, 1.0, base=0,
                                        channel_multiplier=1))
                step(pool.memset(S.ones[:], 1.0))
                step(pool.memset(S.eps[:], EPS))
                step(pool.memset(S.causal[:], 1.0))
                step(pool.affine_select(S.causal[:, 0, :], S.causal[:, 0, :], [[1, P]], ALU.is_ge, 0.0, base=0,
                                        channel_multiplier=-1))
                step(pool.memset(S.causal[0:GLA_BLOCK, 0, GLA_BLOCK:], 0.0))
                step(pool.affine_select(S.causal[:, 1, :], S.causal[:, 1, :], [[1, P]], ALU.is_ge, 0.0, base=0,
                                        channel_multiplier=-1))
                view = S.causal[:, 1, :].rearrange("p (b s) -> p b s", s=DEC_S)
                step(pool.affine_select(view, view, [[-DEC_S, DEC_B], [0, DEC_S]], ALU.is_ge, 0.0, base=0,
                                        channel_multiplier=1))
                step(pool.memset(S.own_mask[:], 0.0))
                half = DEC_B // 2
                for head in range(2):
                    for g in range(2):
                        view = S.own_mask[head * DH:(head + 1) * DH, g, :].rearrange("p (b s) -> p b s", s=DEC_S)
                        for sign, base in ((1, half * DEC_S * g), (-1, DEC_S - 1 - half * DEC_S * g)):
                            step(pool.affine_select(view, view, [[-DEC_S * sign, DEC_B], [0, DEC_S]], ALU.is_ge, MASKED,
                                                    base=base, channel_multiplier=sign))
                step(pool.memset(S.stream[:], 1.0))
                step(pool.affine_select(S.stream[:], S.stream[:], [[-DEC_S, DEC_B]], ALU.is_ge, 0.0, base=0,
                                        channel_multiplier=1))
                step(pool.affine_select(S.stream[:], S.stream[:], [[DEC_S, DEC_B]], ALU.is_ge, 0.0,
                                        base=DEC_S - 1, channel_multiplier=-1))


def load_tokens(nc, S, a):
    with semaphores(nc) as sem:
        x_in = [sem(f"x_in{i}") for i in range(2)]
        turned, taken = sem("x_turned"), sem("x_taken")
        with ExitStack() as ctx:
            xt = ctx.enter_context(nc.sbuf_tensor("x_rows", [P, 2, D], F32))
            ps = ctx.enter_context(nc.psum_tensor("x_ps", [P, 2, D], F32))
            block = ctx.enter_context(nc.Block())
            rows = [a["x_prompt"][0, i * P:(i + 1) * P, :] for i in range(NT - 1)]
            rows.append(a["x_sample"].rearrange("b s d -> (b s) d"))

            @block.sync
            def _(sp):
                for i in range(NT):
                    if i >= 2:
                        sp.wait_ge(turned, i - 1)
                    sp.dma_start(xt[:, i % 2, :], rows[i]).then_inc(x_in[i % 2], 16)

            @block.tensor
            def _(pe):
                for i in range(NT):
                    pe.wait_ge(x_in[i % 2], 16 * (i // 2 + 1))
                    if i >= 2:
                        pe.wait_ge(taken, i - 1)
                    for k in range(DK):
                        t = pe.transpose(ps[:, i % 2, k * P:(k + 1) * P], xt[:, i % 2, k * P:(k + 1) * P], S.ident[:])
                    t.then_inc(turned, 1)

            @block.vector
            def _(dve):
                for i in range(NT):
                    dve.wait_ge(turned, i + 1)
                    dve.tensor_copy(S.res[:, :, i * P:(i + 1) * P],
                                    ps[:, i % 2, :].rearrange("p (k t) -> p k t", t=P)).then_inc(taken, 1)


def norm(nc, S, tag, gain, final=False):
    with semaphores(nc) as sem:
        squared, summed, rooted, inverse, normed, rounded, low = (sem(f"{tag}_{n}") for n in (
            "squared", "summed", "rooted", "inverse", "normed", "rounded", "low"))
        with ExitStack() as ctx:
            sq = ctx.enter_context(nc.sbuf_tensor(f"{tag}_sq", [P, DK, GRP], F32))
            y = sq if not final else None
            rms = ctx.enter_context(nc.sbuf_tensor(f"{tag}_rms", [P, NG, GRP], F32))
            ps = ctx.enter_context(nc.psum_tensor(f"{tag}_ps", [P, NG, 512], F32))
            yb = None if final else ctx.enter_context(nc.sbuf_tensor(f"{tag}_y", [P, DK, GRP], F32))
            block = ctx.enter_context(nc.Block())
            cols = [slice(t * GRP, (t + 1) * GRP) for t in range(NG)]
            per = DK if gain is not None else 1

            @block.scalar
            def _(act):
                for t in range(NG):
                    if t:
                        act.wait_ge(summed, t)
                    act.activation(sq[:], S.res[:, :, cols[t]], ACT.Square).then_inc(squared, 1)
                for t in range(NG):
                    act.wait_ge(summed, t + 1)
                    act.activation(rms[:, t, :], ps[:, t, :GRP], ACT.Sqrt, bias=S.eps[:],
                                   scale=1.0 / D).then_inc(rooted, 1)
                for t in range(NG):
                    if final:
                        break
                    act.wait_ge(normed, per * (t + 1))
                    act.copy(S.x_hi[:, :, cols[t]], yb[:]).then_inc(rounded, 1)

            @block.tensor
            def _(pe):
                for t in range(NG):
                    pe.wait_ge(squared, t + 1)
                    for k in range(DK):
                        m = pe.matmul(ps[:, t, :GRP], S.ones[:], sq[:, k, :], start=k == 0, stop=k == DK - 1)
                    m.then_inc(summed, 1)

            @block.vector
            def _(dve):
                for t in range(NG):
                    dve.wait_ge(rooted, t + 1)
                    dve.reciprocal(rms[:, t, :], rms[:, t, :]).then_inc(inverse, 1)
                    dve.wait_ge(inverse, t + 1)
                    if t and not final:
                        dve.wait_ge(low, t)
                    out = S.res[:, :, cols[t]] if final else yb[:]
                    if gain is None:
                        dve.tensor_tensor(out, S.res[:, :, cols[t]],
                                          rms[:, t, :].unsqueeze(1).to_broadcast([P, DK, GRP]),
                                          ALU.mult).then_inc(normed, 1)
                    else:
                        for k in range(DK):
                            dve.scalar_tensor_tensor(out[:, k, :], S.res[:, k, cols[t]], S.gains[:, gain, k:k + 1],
                                                     rms[:, t, :], ALU.mult, ALU.mult).then_inc(normed, 1)
                    if not final:
                        dve.wait_ge(rounded, t + 1)
                        dve.tensor_tensor(S.x_lo[:, :, cols[t]], yb[:], f32(S.x_hi[:, :, cols[t]]),
                                          ALU.subtract).then_inc(low, 1)


def project(nc, S, tag, segments):
    SL, BANKS = 4, 6
    with semaphores(nc) as sem:
        filled = sem(f"{tag}_filled")
        drained = sem(f"{tag}_drained")
        stored = [sem(f"{tag}_stored{i}") for i in range(SL)]
        with ExitStack() as ctx:
            ring = weight_ring(nc, sem, ctx, tag, SL, SL)
            rows = ctx.enter_context(nc.sbuf_tensor(f"{tag}_sums", [P, SL, TOK], F32))
            ps = ctx.enter_context(nc.psum_tensor(f"{tag}_ps", [P, BANKS, 512], F32))
            block = ctx.enter_context(nc.Block())
            plan, base = [], 0
            for w, col, units, gain, out, row, skip in segments:
                plan.append(Segment(w, col, units, gain, out, row, skip, base, SL))
                base += units
            assert all(s.per == SL for s in plan[:-1])

            @block.sync
            def _(sp):
                def fetch(s, it, j):
                    fetch_unit(sp, ring, it * s.per + (s.base + j), j, s.w[:, :, bass.ds(it * (s.per * P) + (s.col + j * P), P)])

                def store(s, it, j):
                    sp.wait_ge(drained, it * (s.per * NG) + (BANKS + (s.base + j + 1) * NG))
                    sp.dma_start(s.out[bass.ds(it * (s.per * P) + (s.row + j * P), P - s.skip), :],
                                 rows[s.skip:, j, :]).then_inc(stored[j], 16)

                last = None
                for s in plan:
                    for j in range(s.per):
                        if last:
                            store(last, last.trips - 1, j)
                        fetch(s, 0, j)
                    if last:
                        for j in range(s.per, last.per):
                            store(last, last.trips - 1, j)
                    if s.trips > 1:
                        with sp.Fori(1, s.trips) as it:
                            for j in range(s.per):
                                store(s, it - 1, j)
                                fetch(s, it, j)
                    last = s
                for j in range(last.per):
                    store(last, last.trips - 1, j)
                for j in range(SL):
                    sp.wait_ge(stored[j], 16 * sum(s.trips for s in plan if j < s.per))

            @block.scalar
            def _(act):
                for s in plan:
                    with act.Fori(0, s.trips) as it:
                        for j in range(s.per):
                            unit = it * s.per + (s.base + j)
                            act.wait_ge(filled, (unit + 1) * NG)
                            round_unit(act, ring, unit, j, it + s.turn, s.gain)

            @block.gpsimd
            def _(pool):
                pool.sem_inc(ring.split, SL)
                for s in plan:
                    with pool.Fori(0, s.trips) as it:
                        for j in range(s.per):
                            unit = it * s.per + (s.base + j)
                            if s.gain is not None:
                                scale_unit(pool, ring, unit, j, it + s.turn, S.gains[:, s.gain, :])
                            split_unit(pool, ring, unit, j)

            @block.tensor
            def _(pe):
                pe.sem_inc(filled, SL * NG)
                for s in plan:
                    with pe.Fori(0, s.trips) as it:
                        for j in range(s.per):
                            pe.wait_ge(ring.split, it * s.per + (s.base + j + 1 + SL))
                            for t in range(NG):
                                g = j * NG + t
                                pe.wait_ge(drained, it * (s.per * NG) + (s.base * NG + g + 1))
                                for k in range(DK):
                                    w, x = slice(k * P, (k + 1) * P), slice(t * GRP, (t + 1) * GRP)
                                    m = product(pe, ps[:, g % BANKS, :GRP], ring.hi[:, j, w], ring.lo[:, j, w],
                                                S.x_hi[:, k, x], S.x_lo[:, k, x], k == 0, k == DK - 1)
                                m.then_inc(filled, 1)

            @block.vector
            def _(dve):
                dve.sem_inc(drained, BANKS)
                for s in plan:
                    with dve.Fori(0, s.trips) as it:
                        for j in range(s.per):
                            dve.wait_ge(stored[j], (it + s.turn) * 16)
                            for t in range(NG):
                                g = j * NG + t
                                dve.wait_ge(filled, it * (s.per * NG) + (SL * NG + s.base * NG + g + 1))
                                dve.tensor_copy(rows[:, j, t * GRP:(t + 1) * GRP],
                                                ps[:, g % BANKS, :GRP]).then_inc(drained, 1)


def add_product(nc, S, tag, w):
    SL, BANKS = 4, 6
    with semaphores(nc) as sem:
        filled = sem(f"{tag}_filled")
        drained = sem(f"{tag}_drained")
        with ExitStack() as ctx:
            ring = weight_ring(nc, sem, ctx, tag, SL, SL)
            ps = ctx.enter_context(nc.psum_tensor(f"{tag}_ps", [P, BANKS, 512], F32))
            block = ctx.enter_context(nc.Block())
            wv = w.rearrange("(k p) n -> p k n", p=P)
            trips = DK // SL

            @block.sync
            def _(sp):
                with sp.Fori(0, trips) as it:
                    for j in range(SL):
                        fetch_unit(sp, ring, it * SL + j, j, wv[:, :, bass.ds(it * (SL * P) + j * P, P)])

            @block.scalar
            def _(act):
                with act.Fori(0, trips) as it:
                    for j in range(SL):
                        act.wait_ge(filled, it * (SL * NG) + (j + 1) * NG)
                        round_unit(act, ring, it * SL + j, j, it)

            @block.gpsimd
            def _(pool):
                pool.sem_inc(ring.split, SL)
                with pool.Fori(0, trips) as it:
                    for j in range(SL):
                        split_unit(pool, ring, it * SL + j, j)

            @block.tensor
            def _(pe):
                pe.sem_inc(filled, SL * NG)
                with pe.Fori(0, trips) as it:
                    for j in range(SL):
                        pe.wait_ge(ring.split, it * SL + (j + 1 + SL))
                        for t in range(NG):
                            g = j * NG + t
                            pe.wait_ge(drained, it * (SL * NG) + (g + 1))
                            for k in range(DK):
                                c, x = slice(k * P, (k + 1) * P), slice(t * GRP, (t + 1) * GRP)
                                m = product(pe, ps[:, g % BANKS, :GRP], ring.hi[:, j, c], ring.lo[:, j, c],
                                            S.x_hi[:, k, x], S.x_lo[:, k, x], k == 0, k == DK - 1)
                            m.then_inc(filled, 1)

            @block.vector
            def _(dve):
                dve.sem_inc(drained, BANKS)
                res = S.res[:].rearrange("p k t -> p (k t)")
                with dve.Fori(0, trips) as it:
                    for j in range(SL):
                        for t in range(NG):
                            g = j * NG + t
                            dve.wait_ge(filled, it * (SL * NG) + (SL * NG + g + 1))
                            h = res[:, bass.ds(it * (SL * TOK) + (j * TOK + t * GRP), GRP)]
                            dve.tensor_tensor(h, h, ps[:, g % BANKS, :GRP], ALU.add).then_inc(drained, 1)


def ffn(nc, S, tag, w_gate, w_up, w_down):
    HT, SL, ST, BANKS = 2, 6, 3, 4
    trips = D_FF // P // HT
    PAIRS_B = HT * NG
    DOWN_B = NG * DK
    with semaphores(nc) as sem:
        pair_filled = sem(f"{tag}_pair_filled")
        gated = sem(f"{tag}_gated")
        pair_drained = sem(f"{tag}_pair_drained")
        hid_rounded = sem(f"{tag}_hid_rounded")
        hid_split = sem(f"{tag}_hid_split")
        down_filled = sem(f"{tag}_down_filled")
        down_drained = sem(f"{tag}_down_drained")
        with ExitStack() as ctx:
            ring = weight_ring(nc, sem, ctx, tag, SL, ST)
            hid_hi = ctx.enter_context(nc.sbuf_tensor(f"{tag}_hid_hi", [P, HT, TOK], F32R))
            hid_lo = ctx.enter_context(nc.sbuf_tensor(f"{tag}_hid_lo", [P, HT, TOK], F32R))
            gate = ctx.enter_context(nc.sbuf_tensor(f"{tag}_gate", [P, 2, GRP], F32))
            hid = ctx.enter_context(nc.sbuf_tensor(f"{tag}_hid", [P, 2, GRP], F32))
            ps = ctx.enter_context(nc.psum_tensor(f"{tag}_pair_ps", [P, 2, 2, 512], F32))
            dps = ctx.enter_context(nc.psum_tensor(f"{tag}_down_ps", [P, BANKS, 512], F32))
            block = ctx.enter_context(nc.Block())
            columns = [w.rearrange("(k p) n -> p k n", p=P) for w in (w_gate, w_up)]

            @block.sync
            def _(sp):
                with sp.Fori(0, trips) as it:
                    for j in range(SL):
                        f = j // 2 if j < 2 * HT else j - 2 * HT
                        if j < 2 * HT:
                            src = columns[j % 2][:, :, bass.ds(it * (HT * P) + f * P, P)]
                        else:
                            src = w_down[bass.ds(it * (HT * P) + f * P, P), :]
                        fetch_unit(sp, ring, it * SL + j, j, src)

            @block.scalar
            def _(act):
                with act.Fori(0, trips) as it:
                    for f in range(HT):
                        for j in (2 * f, 2 * f + 1):
                            act.wait_ge(pair_filled, it * PAIRS_B + (f + 1) * NG)
                            round_unit(act, ring, it * SL + j, j, it * (SL // ST) + j // ST)
                    for g in range(PAIRS_B):
                        f, t = divmod(g, NG)
                        act.wait_ge(pair_filled, it * PAIRS_B + (PAIRS_B + g + 1))
                        act.wait_ge(pair_drained, it * PAIRS_B + (g + 1))
                        act.activation(gate[:, g % 2, :], ps[:, g % 2, 0, :GRP], ACT.Silu).then_inc(gated, 1)
                        act.wait_ge(pair_drained, it * PAIRS_B + (g + 3))
                        act.wait_ge(down_filled, it * DOWN_B + (t + 1) * DK)
                        act.copy(hid_hi[:, f, t * GRP:(t + 1) * GRP], hid[:, g % 2, :]).then_inc(hid_rounded, 1)
                        if g == 0:
                            for j in range(2 * HT, SL):
                                act.wait_ge(down_filled, it * DOWN_B + DOWN_B)
                                round_unit(act, ring, it * SL + j, j, it * (SL // ST) + j // ST)

            @block.gpsimd
            def _(pool):
                pool.sem_inc(ring.split, ST)
                with pool.Fori(0, trips) as it:
                    for j in range(2 * HT):
                        split_unit(pool, ring, it * SL + j, j)
                    for g in range(PAIRS_B):
                        f, t = divmod(g, NG)
                        pool.wait_ge(hid_rounded, it * PAIRS_B + (g + 1))
                        cols = slice(t * GRP, (t + 1) * GRP)
                        pool.tensor_tensor(hid_lo[:, f, cols], hid[:, g % 2, :], f32(hid_hi[:, f, cols]),
                                           ALU.subtract).then_inc(hid_split, 1)
                        if g == 0:
                            for j in range(2 * HT, SL):
                                split_unit(pool, ring, it * SL + j, j)

            @block.tensor
            def _(pe):
                pe.sem_inc(pair_filled, PAIRS_B)
                pe.sem_inc(down_filled, DOWN_B)
                with pe.Fori(0, trips) as it:
                    for g in range(PAIRS_B):
                        f, t = divmod(g, NG)
                        if t == 0:
                            pe.wait_ge(ring.split, it * SL + (ST + 2 * f + 2))
                        pe.wait_ge(pair_drained, it * PAIRS_B + (g + 1))
                        x = slice(t * GRP, (t + 1) * GRP)
                        for u in range(2):
                            for k in range(DK):
                                c = slice(k * P, (k + 1) * P)
                                m = product(pe, ps[:, g % 2, u, :GRP], ring.hi[:, 2 * f + u, c], ring.lo[:, 2 * f + u, c],
                                            S.x_hi[:, k, x], S.x_lo[:, k, x], k == 0, k == DK - 1)
                        m.then_inc(pair_filled, 1)
                    pe.wait_ge(ring.split, it * SL + (ST + SL))
                    for t in range(NG):
                        pe.wait_ge(hid_split, it * PAIRS_B + ((HT - 1) * NG + t + 1))
                        x = slice(t * GRP, (t + 1) * GRP)
                        for m in range(DK):
                            g = t * DK + m
                            pe.wait_ge(down_drained, it * DOWN_B + (g + 1))
                            c = slice(m * P, (m + 1) * P)
                            for f in range(HT):
                                ins = product(pe, dps[:, g % BANKS, :GRP], ring.hi[:, 2 * HT + f, c],
                                              ring.lo[:, 2 * HT + f, c], hid_hi[:, f, x], hid_lo[:, f, x],
                                              f == 0, f == HT - 1)
                            ins.then_inc(down_filled, 1)

            @block.vector
            def _(dve):
                dve.sem_inc(pair_drained, 2)
                dve.sem_inc(down_drained, BANKS)
                with dve.Fori(0, trips) as it:
                    for g in range(PAIRS_B):
                        dve.wait_ge(gated, it * PAIRS_B + (g + 1))
                        if g >= 2:
                            dve.wait_ge(hid_split, it * PAIRS_B + (g - 1))
                        dve.tensor_tensor(hid[:, g % 2, :], gate[:, g % 2, :], ps[:, g % 2, 1, :GRP],
                                          ALU.mult).then_inc(pair_drained, 1)
                    for t in range(NG):
                        for m in range(DK):
                            g = t * DK + m
                            dve.wait_ge(down_filled, it * DOWN_B + (DOWN_B + g + 1))
                            h = S.res[:, m, t * GRP:(t + 1) * GRP]
                            dve.tensor_tensor(h, h, dps[:, g % BANKS, :GRP], ALU.add).then_inc(down_drained, 1)


def store_tokens(nc, S, a):
    with semaphores(nc) as sem:
        turned, taken = sem("y_turned"), sem("y_taken")
        y_out = [sem(f"y_out{i}") for i in range(2)]
        with ExitStack() as ctx:
            yt = ctx.enter_context(nc.sbuf_tensor("y_rows", [P, 2, D], F32))
            ps = ctx.enter_context(nc.psum_tensor("y_ps", [P, 2, D], F32))
            block = ctx.enter_context(nc.Block())
            rows = [a["y_prompt"][0, i * P:(i + 1) * P, :] for i in range(NT - 1)]
            rows.append(a["y_sample"].rearrange("b s d -> (b s) d"))

            @block.tensor
            def _(pe):
                for i in range(NT):
                    if i >= 2:
                        pe.wait_ge(taken, i - 1)
                    for k in range(DK):
                        t = pe.transpose(ps[:, i % 2, k * P:(k + 1) * P], S.res[:, k, i * P:(i + 1) * P], S.ident[:])
                    t.then_inc(turned, 1)

            @block.vector
            def _(dve):
                for i in range(NT):
                    dve.wait_ge(turned, i + 1)
                    if i >= 2:
                        dve.wait_ge(y_out[i % 2], 16 * (i // 2))
                    dve.tensor_copy(yt[:, i % 2, :], ps[:, i % 2, :]).then_inc(taken, 1)

            @block.sync
            def _(sp):
                for i in range(NT):
                    sp.wait_ge(taken, i + 1)
                    sp.dma_start(rows[i], yt[:, i % 2, :]).then_inc(y_out[i % 2], 16)
                for j in range(2):
                    sp.wait_ge(y_out[j], 16 * len(range(j, NT, 2)))
                sp.wait_ge(S.caches_kept, 2 * 16)


def gla_core(nc, S, a):
    with semaphores(nc) as sem:
        NB = SEQ // GLA_BLOCK
        NTP = NT - 1
        VT = GLA_DV // P
        small_in, qk_in, v_in, g_in, st_in = (sem(f"gla_{n}_in") for n in ("small", "qk", "v", "g", "state"))
        turn_filled = sem("gla_turn_filled")
        turn_drained = sem("gla_turn_drained")
        logit_in = sem("gla_logit_in")
        softplus = sem("gla_softplus")
        decay = sem("gla_decay")
        grown = sem("gla_grown")
        scaled = sem("gla_scaled")
        zeroed = sem("gla_zeroed")
        mask_turn = sem("gla_mask_turn")
        s_filled, s_masked = sem("gla_scores_filled"), sem("gla_scores_masked")
        u_filled, stepped = sem("gla_update_filled"), sem("gla_state_stepped")
        o_filled, o_drained = sem("gla_out_filled"), sem("gla_out_drained")
        spread = sem("gla_k2_spread")
        squared, rooted, gated, inverse, normed = (sem(f"gla_{n}") for n in (
            "squared", "rooted", "gated", "inverse", "normed"))
        rounded, split = sem("gla_rounded"), sem("gla_split")
        st_out = sem("gla_state_out")
        TURNS = 14
        STEPS = NB + DEC_B
        with ExitStack() as ctx:
            def sb(name, shape, dt=F32):
                return ctx.enter_context(nc.sbuf_tensor(f"mix_{name}", shape, dt))

            def pb(name, shape):
                return ctx.enter_context(nc.psum_tensor(f"mix_{name}", shape, F32))

            w2 = sb("w_gate2", [RANK, P])
            bg = sb("b_gate", [P, 1])
            ng = sb("norm_gain", [P, VT])
            reset = sb("reset", [P, TOK])
            q, k = sb("q", [P, TOK]), sb("k", [P, TOK])
            vt = sb("vt", [P, VT, TOK])
            g = sb("g", [P, VT, TOK])
            v = sb("v", [P, NT, GLA_DV])
            soft = sb("soft", [P, TOK])
            least = sb("least", [P, TOK])
            b = sb("b", [P, TOK])
            eb = sb("eb", [P, TOK])
            k2t = sb("k2t", [P, NT, P])
            o = sb("o", [P, VT, TOK])
            st_s = sb("state_sample", [P, DEC_B, GLA_DV])
            st = sb("state", [P, 4, GLA_DV])
            st_fin = sb("state_last", [P, GLA_DV])
            sc = sb("scores", [P, 3, P])
            turn = pb("turn", [P, 2, 512])
            sps, ups, ops = pb("score_ps", [P, 2, 512]), pb("update_ps", [P, 2, 512]), pb("out_ps", [P, 2, 512])
            block = ctx.enter_context(nc.Block())
            zt = S.gla_rows
            spread_k2 = vt[:].rearrange("p j t -> p (j t)")[:, :DEC_B * P].rearrange("p (b k) -> p b k", k=P)

            @block.sync
            def _(sp):
                with sp.Fori(0, GLA_H) as h:
                    sp.wait_ge(scaled, h * 4)
                    sp.dma_start(w2[:], a["gla_w_gate2"][0, :, bass.ds(h * P, P)]).then_inc(small_in, 16)
                    sp.dma_start(bg[:], a["gla_b_gate"].rearrange("l (n o) -> (l n) o", o=1)[bass.ds(h * P, P), :]).then_inc(small_in, 16)
                    sp.dma_start(least[0:RANK, :], zt[2 * NQK + 2 * NV:, :]).then_inc(small_in, 16)
                    sp.wait_ge(o_filled, h * NT)
                    sp.dma_start(q[:], zt[bass.ds(h * P, P), :]).then_inc(qk_in, 16)
                    sp.dma_start(k[:], zt[bass.ds(h * P + NQK, P), :]).then_inc(qk_in, 16)
                    sp.wait_ge(turn_filled, h * TURNS)
                    sp.dma_start(vt[:], zt[bass.ds(h * GLA_DV + 2 * NQK, GLA_DV), :].rearrange("(j p) t -> p j t", p=P)).then_inc(v_in, 16)
                    sp.wait_ge(st_out, h * 32)
                    sp.dma_start(st_s[:], a["state_gla"][0, :, bass.ds(h, 1), :, :].rearrange("b o k v -> (o k) b v")).then_inc(st_in, 16)
                    sp.wait_ge(split, h)
                    sp.dma_start(g[:], zt[bass.ds(h * GLA_DV + 2 * NQK + NV, GLA_DV), :].rearrange("(j p) t -> p j t", p=P)).then_inc(g_in, 16)
                    sp.dma_start(ng[:], a["gla_norm"].rearrange("l (h j p) -> p (l h) j", j=VT, p=P)[:, bass.ds(h, 1), :],
                                 allow_slow_non_contiguous=True).then_inc(g_in, 16)

            @block.tensor
            def _(pe):
                def bank(h, n):
                    pe.wait_ge(turn_drained, h * TURNS + (n + 1))
                    return turn[:, n % 2, :]

                with pe.Fori(0, GLA_H) as h:
                    pe.wait_ge(small_in, (h + 1) * 48)
                    for t in range(NG):
                        ps = bank(h, t)
                        pe.matmul(ps[:, :GRP], w2[:], least[0:RANK, t * GRP:(t + 1) * GRP]).then_inc(turn_filled, 1)
                    pe.wait_ge(v_in, (h + 1) * 16)
                    for n in range(5):
                        ps = bank(h, NG + n)
                        for i in range(2 * n, min(2 * n + 2, NT)):
                            for j in range(VT):
                                c = (i % 2) * GLA_DV + j * P
                                m = pe.transpose(ps[:, c:c + P], vt[:, j, i * P:(i + 1) * P], S.ident[:])
                        m.then_inc(turn_filled, 1)
                    pe.wait_ge(scaled, (h + 1) * 4)
                    for n in range(3):
                        ps = bank(h, NG + 5 + n)
                        for i in range(4 * n, min(4 * n + 4, NT)):
                            m = pe.transpose(ps[:, (i % 4) * P:(i % 4 + 1) * P], soft[:, i * P:(i + 1) * P], S.ident[:])
                        m.then_inc(turn_filled, 1)
                    pe.wait_ge(turn_drained, h * TURNS + (2 + NG + 8))

                    def out(i):
                        pe.wait_ge(s_masked, h * NT + (2 + i + 1))
                        if i < NTP:
                            pe.wait_ge(stepped, h * STEPS + (4 + 2 * i + 1))
                        else:
                            pe.wait_ge(st_in, (h + 1) * 16)
                        pe.wait_ge(o_drained, h * NT + (2 if i == 0 else i + 1))
                        slot = i % 2 if i < NTP else 2
                        for j in range(VT):
                            dst, vc = ops[:, i % 2, j * P:(j + 1) * P], slice(j * P, (j + 1) * P)
                            pe.matmul(dst, v[:, i, vc], sc[:, slot, :], start=True, stop=False)
                            if i < NTP:
                                for c in range(2):
                                    cols = slice(c * GLA_BLOCK, (c + 1) * GLA_BLOCK)
                                    m = pe.matmul(dst[:, cols], st[:, (2 * i + c) % 4, vc],
                                                  q[:, i * P + c * GLA_BLOCK:i * P + (c + 1) * GLA_BLOCK],
                                                  start=False, stop=c == 1)
                            else:
                                for s in range(DEC_B):
                                    cols = slice(s * DEC_S, (s + 1) * DEC_S)
                                    m = pe.matmul(dst[:, cols], st_s[:, s, vc],
                                                  q[:, SEQ + s * DEC_S:SEQ + (s + 1) * DEC_S],
                                                  start=False, stop=s == DEC_B - 1)
                        m.then_inc(o_filled, 1)

                    for i in range(NT):
                        pe.wait_ge(s_masked, h * NT + (2 if i == 0 else i + 1))
                        cols = slice(i * P, (i + 1) * P)
                        pe.matmul(sps[:, i % 2, :P], k[:, cols], q[:, cols]).then_inc(s_filled, 1)
                        if i:
                            out(i - 1)
                        if i < NTP:
                            pe.wait_ge(stepped, h * STEPS + (4 + 2 * i))
                            for c in range(2):
                                r = slice(c * GLA_BLOCK, (c + 1) * GLA_BLOCK)
                                m = pe.matmul(ups[:, c, :GLA_DV], k2t[r, i, :], v[r, i, :])
                            m.then_inc(u_filled, 1)
                    out(NTP)
                    pe.wait_ge(spread, h + 1)
                    for n in range(DEC_B // 2):
                        pe.wait_ge(stepped, h * STEPS + (4 + NB + 2 * n))
                        for c in range(2):
                            m = pe.matmul(ups[:, c, :GLA_DV], spread_k2[:, 2 * n + c, :], v[:, NTP, :])
                        m.then_inc(u_filled, 1)
                    pe.wait_ge(squared, h + 1)
                    for t in range(NG):
                        ps = bank(h, NG + 8 + t)
                        for j in range(VT):
                            m = pe.matmul(ps[:, :GRP], S.ones[:], vt[:, j, t * GRP:(t + 1) * GRP],
                                          start=j == 0, stop=j == VT - 1)
                        m.then_inc(turn_filled, 1)

            @block.scalar
            def _(act):
                with act.Fori(0, GLA_H) as h:
                    for t in range(NG):
                        act.wait_ge(turn_filled, h * TURNS + (t + 1))
                        if t == 0:
                            act.wait_ge(turn_filled, h * TURNS)
                        act.activation(soft[:, t * GRP:(t + 1) * GRP], turn[:, t % 2, :GRP], ACT.Identity,
                                       bias=bg[:]).then_inc(turn_drained, 1)
                    act.wait_ge(decay, h * 3 + 1)
                    act.activation(soft[:], soft[:], ACT.Abs).then_inc(softplus, 1)
                    act.wait_ge(softplus, h * 3 + 1)
                    act.activation(soft[:], soft[:], ACT.Exp, scale=-1.0).then_inc(softplus, 1)
                    act.wait_ge(softplus, h * 3 + 2)
                    act.activation(soft[:], soft[:], ACT.Ln, bias=1.0).then_inc(softplus, 1)
                    for n in range(5):
                        act.wait_ge(turn_filled, h * TURNS + (NG + n + 1))
                        w = min(2, NT - 2 * n)
                        act.copy(v[:, 2 * n:2 * n + w, :], turn[:, (NG + n) % 2, :w * GLA_DV].rearrange("p (i d) -> p i d", d=GLA_DV)
                                 ).then_inc(turn_drained, 1)
                    act.wait_ge(decay, h * 3 + 3)
                    act.activation(eb[:], b[:], ACT.Exp, scale=1.0 / GLA_TAU).then_inc(grown, 1)
                    act.activation(least[:], b[:], ACT.Exp, scale=-1.0 / GLA_TAU).then_inc(grown, 1)
                    for n in range(3):
                        act.wait_ge(turn_filled, h * TURNS + (NG + 5 + n + 1))
                        w = min(4, NT - 4 * n)
                        act.copy(k2t[:, 4 * n:4 * n + w, :], turn[:, (NG + 5 + n) % 2, :w * P].rearrange("p (i d) -> p i d", d=P)
                                 ).then_inc(turn_drained, 1)
                    for i in range(NT):
                        act.wait_ge(o_filled, h * NT + (i + 1))
                        act.copy(o[:, :, i * P:(i + 1) * P], ops[:, i % 2, :VT * P].rearrange("p (j t) -> p j t", t=P)
                                 ).then_inc(o_drained, 1)
                    act.wait_ge(o_drained, h * NT + (2 + NT))
                    act.wait_ge(u_filled, (h + 1) * (STEPS // 2))
                    act.activation(vt[:], o[:], ACT.Square).then_inc(squared, 1)
                    for t in range(NG):
                        act.wait_ge(turn_filled, h * TURNS + (NG + 8 + t + 1))
                        act.activation(b[:, t * GRP:(t + 1) * GRP], turn[:, (NG + 8 + t) % 2, :GRP], ACT.Sqrt,
                                       bias=S.eps[:], scale=1.0 / GLA_DV).then_inc(turn_drained, 1)
                    act.wait_ge(g_in, (h + 1) * 32)
                    act.activation(g[:], g[:], ACT.Silu).then_inc(gated, 1)
                    act.wait_ge(normed, (h + 1) * (VT + 1))
                    act.copy(S.x_hi[:].rearrange("p k t -> p (k t)")[:, bass.ds(h * (VT * TOK), VT * TOK)],
                             o[:].rearrange("p j t -> p (j t)")).then_inc(rounded, 1)
                    act.wait_ge(stepped, (h + 1) * STEPS + 4)
                    act.dma_start(a["state_gla_prompt"][0, 0, bass.ds(h, 1), :, :].rearrange("o k v -> (o k) v"), st_fin[:]).then_inc(st_out, 16)
                    act.dma_start(a["state_gla_sample"][0, :, bass.ds(h, 1), :, :].rearrange("b o k v -> (o k) b v"), st_s[:]).then_inc(st_out, 16)
                act.wait_ge(st_out, GLA_H * 32)

            @block.vector
            def _(dve):
                dve.sem_inc(turn_drained, 2)
                dve.sem_inc(s_masked, 2)
                dve.sem_inc(stepped, 4)
                dve.sem_inc(o_drained, 2)
                dve.memset(sc[:], 0.0).then_inc(zeroed, 1)
                dve.memset(reset[:], 1.0).then_inc(zeroed, 1)
                dve.wait_ge(zeroed, 2)
                dve.memset(reset[:, 0:SEQ:GLA_BLOCK], 0.0).then_inc(zeroed, 1)
                dve.memset(reset[:, SEQ::DEC_S], 0.0).then_inc(zeroed, 1)
                dve.wait_ge(zeroed, 4)
                with dve.Fori(0, GLA_H) as h:
                    dve.wait_ge(turn_drained, h * TURNS + (2 + NG))
                    dve.tensor_scalar(least[:], soft[:], 0.0, None, ALU.min).then_inc(decay, 1)
                    dve.wait_ge(softplus, (h + 1) * 3)
                    dve.wait_ge(decay, h * 3 + 1)
                    dve.tensor_tensor(least[:], least[:], soft[:], ALU.subtract).then_inc(decay, 1)
                    dve.wait_ge(decay, h * 3 + 2)
                    dve.tensor_tensor_scan(b[:], reset[:], least[:], 0.0, ALU.mult, ALU.add).then_inc(decay, 1)
                    dve.wait_ge(qk_in, (h + 1) * 32)
                    dve.wait_ge(grown, (h + 1) * 2)
                    dve.scalar_tensor_tensor(q[:], q[:], GLA_DK ** -0.5, eb[:], ALU.mult, ALU.mult).then_inc(scaled, 1)
                    dve.tensor_tensor(k[:], k[:], least[:], ALU.mult).then_inc(scaled, 1)
                    dve.wait_ge(scaled, h * 4 + 2)
                    for lo, hi, blk in ((0, SEQ, GLA_BLOCK), (SEQ, TOK, DEC_S)):
                        n = (hi - lo) // blk
                        dve.tensor_tensor(soft[:, lo:hi].rearrange("p (n t) -> p n t", t=blk),
                                          k[:, lo:hi].rearrange("p (n t) -> p n t", t=blk),
                                          eb[:, lo + blk - 1:hi:blk].unsqueeze(2).to_broadcast([P, n, blk]),
                                          ALU.mult).then_inc(scaled, 1)
                    dve.wait_ge(o_filled, h * NT)
                    dve.memset(st[:, 0, :], 0.0).then_inc(zeroed, 1)
                    dve.wait_ge(zeroed, h + 5)
                    for i in range(NT):
                        dve.wait_ge(s_filled, h * NT + (i + 1))
                        if i >= 2:
                            dve.wait_ge(o_filled, h * NT + (i - 1))
                        dve.sem_inc(mask_turn, 1)
                        dve.copy_predicated(sc[:, i % 2 if i < NTP else 2, :],
                                            S.causal[:, 0 if i < NTP else 1, :].bitcast(I32),
                                            sps[:, i % 2, :P]).then_inc(s_masked, 1)
                        if i == NTP:
                            break
                        dve.wait_ge(u_filled, h * (STEPS // 2) + (i + 1))
                        for c in range(2):
                            n = 2 * i + c
                            dve.wait_ge(stepped, h * STEPS + (4 + n))
                            if n >= 3:
                                dve.wait_ge(o_filled, h * NT + ((n - 3) // 2 + 1))
                            if n == NB - 1:
                                dve.wait_ge(st_out, h * 32)
                            last = n * GLA_BLOCK + GLA_BLOCK - 1
                            dst = st_fin[:] if n == NB - 1 else st[:, (n + 1) % 4, :]
                            dve.scalar_tensor_tensor(dst, st[:, n % 4, :], eb[:, last:last + 1],
                                                     ups[:, c, :GLA_DV],
                                                     ALU.mult, ALU.add).then_inc(stepped, 1)
                    dve.wait_ge(turn_drained, h * TURNS + (2 + NG + 8))
                    dve.tensor_tensor(spread_k2, k2t[:, NTP:NT, :].to_broadcast([P, DEC_B, P]),
                                      S.stream[:].unsqueeze(2).to_broadcast([P, DEC_B, P]), ALU.mult).then_inc(spread, 1)
                    dve.wait_ge(o_filled, (h + 1) * NT)
                    for n in range(DEC_B):
                        dve.wait_ge(u_filled, h * (STEPS // 2) + (NB // 2 + n // 2 + 1))
                        last = SEQ + n * DEC_S + DEC_S - 1
                        dve.scalar_tensor_tensor(st_s[:, n, :], st_s[:, n, :], eb[:, last:last + 1],
                                                 ups[:, n % 2, :GLA_DV],
                                                 ALU.mult, ALU.add).then_inc(stepped, 1)
                    dve.wait_ge(turn_drained, (h + 1) * TURNS + 2)
                    dve.reciprocal(b[:], b[:]).then_inc(inverse, 1)
                    dve.wait_ge(inverse, h + 1)
                    dve.wait_ge(gated, h + 1)
                    for j in range(VT):
                        dve.scalar_tensor_tensor(o[:, j, :], o[:, j, :], ng[:, j:j + 1], b[:],
                                                 ALU.mult, ALU.mult).then_inc(normed, 1)
                    dve.wait_ge(normed, h * (VT + 1) + VT)
                    dve.tensor_tensor(o[:], o[:], g[:], ALU.mult).then_inc(normed, 1)
                    dve.wait_ge(rounded, h + 1)
                    at = bass.ds(h * (VT * TOK), VT * TOK)
                    dve.tensor_tensor(S.x_lo[:].rearrange("p k t -> p (k t)")[:, at], o[:].rearrange("p j t -> p (j t)"),
                                      f32(S.x_hi[:].rearrange("p k t -> p (k t)")[:, at]), ALU.subtract).then_inc(split, 1)


def attention_core(nc, S, a):
    with semaphores(nc) as sem:
        NTP = NT - 1
        UNITS = 2 * NTP
        GB = DEC_B // 2
        GROUPS = DEC_B // GB
        ALLU = UNITS + GROUPS
        TILES_KEPT = 5
        KT_S = PAST // P
        FILLS = 2 + UNITS + 2 * GROUPS
        WIDE = BAND_T * P
        SW = PAST + P
        qkv_in = sem("att_qkv_in")
        kc_in, vc_in = sem("att_kcache_in"), sem("att_vcache_in")
        bias_in, bias_set = sem("att_bias_in"), sem("att_bias_set")
        paced = sem("att_paced")
        q_hi_done, q_lo_done = sem("att_q_hi"), sem("att_q_lo")
        k_hi_done, k_lo_done = sem("att_k_hi"), sem("att_k_lo")
        rows_done, v_hi_done, v_lo_done = sem("att_rows"), sem("att_v_hi"), sem("att_v_lo")
        qz_zero, qz_done = sem("att_qz_zero"), sem("att_qz")
        turn_filled, turn_drained = sem("att_turn_filled"), sem("att_turn_drained")
        s_filled, biased = sem("att_scores_filled"), sem("att_biased")
        exped, inverse, scaled = sem("att_exp"), sem("att_inverse"), sem("att_probs")
        p_hi_done, p_lo_done = sem("att_probs_hi"), sem("att_probs_lo")
        ks_done, ps_done = sem("att_k_sample"), sem("att_p_sample")
        o_filled, o_hi_done, o_lo_done = sem("att_out_filled"), sem("att_out_hi"), sem("att_out_lo")
        cached = sem("att_cache_out")
        with ExitStack() as ctx:
            def sb(name, shape, dt=F32):
                return ctx.enter_context(nc.sbuf_tensor(f"att_{name}", shape, dt))

            def pb(name, shape):
                return ctx.enter_context(nc.psum_tensor(f"att_{name}", shape, F32))

            qf, kf, vf = sb("q", [P, TOK]), sb("k", [P, TOK]), sb("v", [P, TOK])
            q_hi, q_lo = sb("q_hi", [P, SEQ], F32R), sb("q_lo", [P, SEQ], F32R)
            k_hi, k_lo = sb("k_hi", [P, SEQ], F32R), sb("k_lo", [P, SEQ], F32R)
            vr, kr = sb("v_rows", [P, NT, P]), sb("k_rows", [P, TILES_KEPT, P])
            v_hi, v_lo = sb("v_hi", [P, NTP, P], F32R), sb("v_lo", [P, NTP, P], F32R)
            probs = sb("probs", [P, 3, WIDE])
            p_hi, p_lo = sb("p_hi", [P, 2, WIDE], F32R), sb("p_lo", [P, 2, WIDE], F32R)
            top, total = sb("top", [P, 3]), sb("total", [P, 3])
            rec = sb("rec", [P, 3])
            bias = sb("bias", [P, 2, WIDE])
            far = sb("far", [P, 2])
            bias_s = sb("bias_s", [P, GROUPS, SW])
            own = sb("own", [P, DEC_S])
            kc, vc = sb("k_cache", [P, GROUPS, GB, KT_S, P]), sb("v_cache", [P, GROUPS, GB, KT_S, P])
            kt = sb("k_turned", [P, GB, PAST])
            qz = sb("q_sample", [P, GB, P])
            pt = sb("p_turned", [P, KT_S + 1, P])
            sps = pb("score_ps", [P, 2, 1024])
            tps = pb("turn_ps", [P, 1024])
            ops = pb("out_ps", [P, 2, 512])
            block = ctx.enter_context(nc.Block())
            strips = S.strips

            def width(j):
                return P * min(j + 1, BAND_T)

            def skewed(h, head, rows, first, cols, copies=None):
                ap = [[STRIP - 1, rows], [1, cols]]
                if copies:
                    ap = [[0, copies]] + ap
                base = strips[bass.ds(h * 2 + head, 1), 0, first:first + 1]
                return bass.AP(tensor=base.tensor, offset=base.offset, ap=ap)

            @block.sync
            def _(sp):
                with sp.Fori(0, PAIRS) as h:
                    feats = bass.ds(h * P, P)
                    sp.wait_ge(s_filled, h * ALLU)
                    sp.sem_inc(paced, 1)
                    for n, dst in enumerate((qf, kf, vf)):
                        sp.dma_start(dst[:], S.qkv_rows[bass.ds(h * P + n * D, P), :]).then_inc(qkv_in, 16)
                    sp.wait_ge(biased, h * ALLU + 2)
                    sp.sem_inc(paced, 1)
                    for head in range(2):
                        sp.dma_start(bias[:, head, WIDE - 2 * P:], skewed(h, head, P, STRIP_C, 2 * P)).then_inc(bias_in, 16)
                        sp.dma_start(far[:, head:head + 1],
                                     a["attn_rel_bias"][0, bass.ds(h * 2 + head, 1), 2 * CLIP:].to_broadcast([P, 1]),
                                     allow_slow_non_contiguous=True).then_inc(bias_in, 16)
                        half = slice(head * CHUNK, (head + 1) * CHUNK)
                        for g in range(GROUPS):
                            sp.dma_start(bias_s[half, g, :PAST], skewed(h, head, DEC_S, DEC_S - 1, PAST, GB)).then_inc(bias_in, 16)
                        sp.dma_start(own[half, :], skewed(h, head, DEC_S, DEC_S - 1 + PAST, DEC_S, GB)).then_inc(bias_in, 16)
                    sp.wait_ge(turn_filled, h * FILLS)
                    sp.sem_inc(paced, 1)
                    for g in range(GROUPS):
                        for b in range(GB):
                            sp.dma_start(kc[:, g, b], a["cache_k"][g * GB + b].rearrange("(t p) h d -> p t (h d)", p=P)[:, :, feats]).then_inc(kc_in, 16)
                    sp.wait_ge(o_filled, h * ALLU)
                    sp.sem_inc(paced, 1)
                    for g in range(GROUPS):
                        for b in range(GB):
                            sp.dma_start(vc[:, g, b], a["cache_v"][g * GB + b].rearrange("(t p) h d -> p t (h d)", p=P)[:, :, feats]).then_inc(vc_in, 16)

            @block.gpsimd
            def _(pool):
                pool.sem_inc(turn_drained, 1)
                pool.memset(qz[:], 0.0).then_inc(qz_zero, 1)
                with pool.Fori(0, PAIRS) as h:
                    pool.wait_ge(qkv_in, (h + 1) * 48)
                    pool.wait_ge(k_hi_done, h + 1)
                    pool.tensor_tensor(k_lo[:], kf[:, :SEQ], f32(k_hi[:]), ALU.subtract).then_inc(k_lo_done, 1)
                    pool.wait_ge(v_hi_done, h + 1)
                    pool.tensor_tensor(v_lo[:], vr[:, :NTP, :], f32(v_hi[:]), ALU.subtract).then_inc(v_lo_done, 1)
                    for u in range(ALLU):
                        w = width(u // 2) if u < UNITS else SW
                        pool.wait_ge(inverse, h * ALLU + (u + 1))
                        pool.sem_inc(paced, 1)
                        pool.tensor_scalar(probs[:, u % 3, :w], probs[:, u % 3, :w], rec[:, u % 3:u % 3 + 1], None,
                                           ALU.mult).then_inc(scaled, 1)

            @block.tensor
            def _(pe):
                def turn(h, n):
                    pe.wait_ge(turn_drained, h * FILLS + (n + 1))

                def scores(h, u):
                    pe.wait_ge(biased, h * ALLU + (u + 1))
                    if u < UNITS:
                        j, head = divmod(u, 2)
                        f = slice(head * DH, (head + 1) * DH)
                        first, w = j * P + P - width(j), width(j)
                        for c in range(0, w, 512):
                            n = min(512, w - c)
                            m = product(pe, sps[:, u % 2, c:c + n], q_hi[f, j * P:(j + 1) * P], q_lo[f, j * P:(j + 1) * P],
                                        k_hi[f, first + c:first + c + n], k_lo[f, first + c:first + c + n], True, True)
                    else:
                        g = u - UNITS
                        pe.wait_ge(qz_done, (h * GROUPS + (g + 1)) * 2)
                        pe.wait_ge(ks_done, h * GROUPS + (g + 1))
                        for c0, w, src in ((0, PAST, kt), (PAST, P, None)):
                            for b in range(GB):
                                rhs = kt[:, b, :] if src is not None else kf[:, SEQ:]
                                m = pe.matmul(sps[:, u % 2, c0:c0 + w], qz[:, b, :], rhs, start=b == 0, stop=b == GB - 1)
                    m.then_inc(s_filled, 1)

                def turn_probs(h, u):
                    pe.wait_ge(scaled, h * ALLU + (u + 1))
                    turn(h, 2 + u + max(0, min(GROUPS, u - (UNITS - 3))))
                    w = width(u // 2) if u < UNITS else SW
                    for c in range(0, w, P):
                        m = pe.transpose(tps[:, c:c + P], probs[:, u % 3, c:c + P], S.ident[:])
                    m.then_inc(turn_filled, 1)

                def turn_keys(h, g):
                    pe.wait_ge(kc_in, (h * GROUPS + GROUPS) * (GB * 16))
                    turn(h, UNITS + 2 * g)
                    for b in range(GB):
                        for t in range(KT_S):
                            m = pe.transpose(tps[:, b * PAST + t * P:b * PAST + (t + 1) * P], kc[:, g, b, t, :], S.ident[:])
                    m.then_inc(turn_filled, 1)

                def out(h, u):
                    pe.wait_ge(o_lo_done, h * ALLU + (u + 1))
                    dst = ops[:, u % 2, :P]
                    if u < UNITS:
                        pe.wait_ge(p_lo_done, h * UNITS + (u + 1))
                        tiles = width(u // 2) // P
                        for n in range(tiles):
                            i, c = u // 2 + 1 - tiles + n, slice(n * P, (n + 1) * P)
                            m = product(pe, dst, v_hi[:, i, :], v_lo[:, i, :], p_hi[:, u % 2, c], p_lo[:, u % 2, c],
                                        n == 0, n == tiles - 1)
                    else:
                        g = u - UNITS
                        pe.wait_ge(ps_done, h * GROUPS + (g + 1))
                        pe.wait_ge(vc_in, (h * GROUPS + GROUPS) * (GB * 16))
                        pe.matmul(dst, vr[:, NTP, :], pt[:, KT_S, :], start=True, stop=False)
                        for b in range(GB):
                            pick = lambda ap: ap.rearrange("p (h b q) -> p h b q", b=GB, q=DEC_S)[:, :, b, :]
                            for t in range(KT_S):
                                m = pe.matmul(pick(dst), vc[:, g, b, t, :], pick(pt[:, t, :]), start=False,
                                              stop=b == GB - 1 and t == KT_S - 1)
                    m.then_inc(o_filled, 1)

                with pe.Fori(0, PAIRS) as h:
                    pe.wait_ge(qkv_in, (h + 1) * 48)
                    turn(h, 0)
                    for i in range(NTP):
                        m = pe.transpose(tps[:, i * P:(i + 1) * P], vf[:, i * P:(i + 1) * P], S.ident[:])
                    m.then_inc(turn_filled, 1)
                    turn(h, 1)
                    pe.transpose(tps[:, :P], vf[:, SEQ:], S.ident[:])
                    for i in range(TILES_KEPT):
                        c = NT - TILES_KEPT + i
                        m = pe.transpose(tps[:, (i + 1) * P:(i + 2) * P], kf[:, c * P:(c + 1) * P], S.ident[:])
                    m.then_inc(turn_filled, 1)
                    pe.wait_ge(q_lo_done, h + 1)
                    pe.wait_ge(k_lo_done, h + 1)
                    pe.wait_ge(v_lo_done, h + 1)
                    for u in range(ALLU + 3):
                        if UNITS <= u < ALLU:
                            turn_keys(h, u - UNITS)
                        if u < ALLU:
                            scores(h, u)
                        if 2 <= u < ALLU + 2:
                            turn_probs(h, u - 2)
                        if u >= 3:
                            out(h, u - 3)

            @block.scalar
            def _(act):
                with act.Fori(0, PAIRS) as h:
                    act.wait_ge(qkv_in, (h + 1) * 48)
                    act.activation(q_hi[:], qf[:, :SEQ], ACT.Copy, scale=-DH ** -0.5).then_inc(q_hi_done, 1)
                    act.copy(k_hi[:], kf[:, :SEQ]).then_inc(k_hi_done, 1)
                    act.wait_ge(turn_filled, h * FILLS + 1)
                    act.wait_ge(cached, h * 64)
                    act.wait_ge(o_filled, h * ALLU)
                    act.copy(vr[:, :NTP, :], tps[:].rearrange("p (i d) -> p i d", d=P)).then_inc(turn_drained, 1)
                    act.wait_ge(turn_filled, h * FILLS + 2)
                    act.copy(vr[:, NTP, :], tps[:, :P]).then_inc(rows_done, 1)
                    act.copy(kr[:], tps[:, P:(TILES_KEPT + 1) * P].rearrange("p (i d) -> p i d", d=P)).then_inc(turn_drained, 1)
                    act.wait_ge(turn_drained, h * FILLS + 2)
                    act.copy(v_hi[:], vr[:, :NTP, :]).then_inc(v_hi_done, 1)
                    act.wait_ge(turn_drained, h * FILLS + 3)
                    act.wait_ge(rows_done, h + 1)
                    feats = bass.ds(h * P, P)
                    for src, nm in ((kr[:], "k"), (vr[:, NT - TILES_KEPT:, :], "v")):
                        act.dma_start(a[f"cache_{nm}_prompt"][0].rearrange("(i t) h d -> t i (h d)", t=P)[:, :, feats],
                                      src[:, :TILES_KEPT - 1, :]).then_inc(cached, 16)
                        act.dma_start(a[f"cache_{nm}_sample"].rearrange("b s h d -> b s (h d)")[:, PAST - DEC_S:, feats],
                                      src[:, TILES_KEPT - 1, :]).then_inc(cached, 16)
                    for u in range(ALLU + 3):
                        if UNITS <= u < ALLU:
                            g = u - UNITS
                            act.wait_ge(turn_filled, h * FILLS + (UNITS + 2 * g + 1))
                            act.wait_ge(s_filled, h * ALLU + u)
                            act.copy(kt[:], tps[:].rearrange("p (b t) -> p b t", b=GB)).then_inc(ks_done, 1)
                            act.wait_ge(ks_done, h * GROUPS + (g + 1))
                            act.sem_inc(turn_drained, 1)
                        if u < ALLU:
                            w = width(u // 2) if u < UNITS else SW
                            act.wait_ge(biased, h * ALLU + (2 + u + 1))
                            act.activation(probs[:, u % 3, :w], probs[:, u % 3, :w], ACT.Exp, scale=-1.0,
                                           bias=top[:, u % 3:u % 3 + 1],
                                           accum_out=total[:, u % 3:u % 3 + 1]).then_inc(exped, 1)
                        v = u - 2
                        if 0 <= v < ALLU:
                            fill = 2 + v + max(0, min(GROUPS, v - (UNITS - 3)))
                            act.wait_ge(turn_filled, h * FILLS + (fill + 1))
                            if v < UNITS:
                                w = width(v // 2)
                                if v >= 2:
                                    act.wait_ge(o_filled, h * ALLU + (v - 1))
                                act.copy(p_hi[:, v % 2, :w], tps[:, :w]).then_inc(p_hi_done, 1)
                            else:
                                act.wait_ge(o_filled, h * ALLU + v)
                                act.copy(pt[:].rearrange("p t c -> p (t c)"), tps[:, :SW]).then_inc(ps_done, 1)
                                act.wait_ge(ps_done, h * GROUPS + (v - UNITS + 1))
                                act.sem_inc(turn_drained, 1)
                        v = u - 3
                        if v >= 0:
                            act.wait_ge(o_filled, h * ALLU + (v + 1))
                            if v < UNITS:
                                j, head = divmod(v, 2)
                                f = slice(head * DH, (head + 1) * DH)
                                flat = S.x_hi[:].rearrange("p k t -> p (k t)")
                                act.copy(flat[f, bass.ds(h * TOK + j * P, P)], ops[f, v % 2, :P]).then_inc(o_hi_done, 1)
                            else:
                                g = v - UNITS
                                flat = S.x_hi[:].rearrange("p k t -> p (k t)")
                                for head in range(2):
                                    f = slice(head * DH, (head + 1) * DH)
                                    act.copy(flat[f, bass.ds(h * TOK + (SEQ + g * GB * DEC_S), GB * DEC_S)],
                                             ops[f, v % 2, head * DH:(head + 1) * DH]).then_inc(o_hi_done, 1)
                act.wait_ge(cached, PAIRS * 64)

            @block.vector
            def _(dve):
                dve.sem_inc(biased, 2)
                dve.sem_inc(o_lo_done, 2)
                with dve.Fori(0, PAIRS) as h:
                    dve.wait_ge(q_hi_done, h + 1)
                    dve.scalar_tensor_tensor(q_lo[:], qf[:, :SEQ], -DH ** -0.5, f32(q_hi[:]), ALU.mult,
                                             ALU.subtract).then_inc(q_lo_done, 1)
                    dve.wait_ge(bias_in, (h + 1) * 160)
                    for head in range(2):
                        dve.memset(bias[:, head, :WIDE - 2 * P], 0.0).then_inc(bias_set, 1)
                    dve.memset(bias[:CHUNK, :, WIDE - CHUNK:], MASKED).then_inc(bias_set, 1)
                    dve.wait_ge(bias_set, h * (6 + GROUPS) + 3)
                    for head in range(2):
                        dve.tensor_scalar(bias[:, head, :WIDE - 2 * P], bias[:, head, :WIDE - 2 * P], far[:, head:head + 1],
                                          -1.0, ALU.add, ALU.mult).then_inc(bias_set, 1)
                    dve.wait_ge(bias_set, h * (6 + GROUPS) + 5)
                    dve.memset(bias[CHUNK:, :, :CHUNK], MASKED).then_inc(bias_set, 1)
                    mask = S.own_mask[:].rearrange("p g (b s) -> p g b s", s=DEC_S)
                    for g in range(GROUPS):
                        dve.tensor_tensor(bias_s[:, g, PAST:].rearrange("p (b s) -> p b s", s=DEC_S),
                                          own[:].unsqueeze(1).to_broadcast([P, DEC_B, DEC_S]), mask[:, g],
                                          ALU.add).then_inc(bias_set, 1)
                    dve.wait_ge(bias_set, (h + 1) * (6 + GROUPS))
                    dve.wait_ge(qz_zero, 1)
                    for u in range(ALLU + 3):
                        if u < ALLU:
                            if u >= UNITS:
                                g = u - UNITS
                                dve.wait_ge(s_filled, h * ALLU + u)
                                for head in range(2):
                                    f = slice(head * DH, (head + 1) * DH)
                                    dst = qz[f].rearrange("p b c -> p (b c)")
                                    dst = bass.AP(tensor=dst.tensor, offset=dst.offset + head * DH,
                                                  ap=[dst.ap[0], [P + DEC_S, GB], [1, DEC_S]])
                                    src = qf[f, SEQ + g * GB * DEC_S:SEQ + (g + 1) * GB * DEC_S]
                                    dve.tensor_scalar(dst, src.rearrange("p (b s) -> p b s", s=DEC_S), -DH ** -0.5, None,
                                                      ALU.mult).then_inc(qz_done, 1)
                            w = width(u // 2) if u < UNITS else SW
                            in1 = bias[:, u % 2, WIDE - w:] if u < UNITS else bias_s[:, u - UNITS, :]
                            dve.wait_ge(s_filled, h * ALLU + (u + 1))
                            v = u - 3
                            if v >= 0:
                                dve.wait_ge(turn_filled, h * FILLS + (2 + v + max(0, min(GROUPS, v - (UNITS - 3))) + 1))
                            else:
                                dve.wait_ge(turn_filled, h * FILLS)
                            dve.sem_inc(paced, 1)
                            dve.tensor_tensor_reduce(probs[:, u % 3, :w], sps[:, u % 2, :w], in1, 1.0, 3e38, ALU.add,
                                                     ALU.min, top[:, u % 3:u % 3 + 1]).then_inc(biased, 1)
                        v = u - 1
                        if 0 <= v < ALLU:
                            dve.wait_ge(exped, h * ALLU + (v + 1))
                            dve.reciprocal(rec[:, v % 3:v % 3 + 1], total[:, v % 3:v % 3 + 1]).then_inc(inverse, 1)
                        v = u - 2
                        if 0 <= v < UNITS:
                            w = width(v // 2)
                            dve.wait_ge(p_hi_done, h * UNITS + (v + 1))
                            dve.tensor_tensor(p_lo[:, v % 2, :w], tps[:, :w], f32(p_hi[:, v % 2, :w]),
                                              ALU.subtract).then_inc(p_lo_done, 1)
                            dve.wait_ge(p_lo_done, h * UNITS + (v + 1))
                            dve.sem_inc(turn_drained, 1)
                        v = u - 3
                        if v >= 0:
                            flat_hi, flat_lo = (t[:].rearrange("p k t -> p (k t)") for t in (S.x_hi, S.x_lo))
                            if v < UNITS:
                                j, head = divmod(v, 2)
                                f = slice(head * DH, (head + 1) * DH)
                                at = bass.ds(h * TOK + j * P, P)
                                dve.wait_ge(o_hi_done, h * (UNITS + 2 * GROUPS) + (v + 1))
                                dve.tensor_tensor(flat_lo[f, at], ops[f, v % 2, :P], f32(flat_hi[f, at]),
                                                  ALU.subtract).then_inc(o_lo_done, 1)
                            else:
                                g = v - UNITS
                                at = bass.ds(h * TOK + (SEQ + g * GB * DEC_S), GB * DEC_S)
                                dve.wait_ge(o_hi_done, h * (UNITS + 2 * GROUPS) + (UNITS + 2 * g + 2))
                                for head in range(2):
                                    f = slice(head * DH, (head + 1) * DH)
                                    m = dve.tensor_tensor(flat_lo[f, at], ops[f, v % 2, head * DH:(head + 1) * DH],
                                                          f32(flat_hi[f, at]), ALU.subtract)
                                m.then_inc(o_lo_done, 1)


def keep_caches(nc, S, a):
    with nc.Block() as block:
        @block.scalar
        def _(act):
            for nm in "kv":
                rows = [a[n].rearrange("b s h d -> b (s h d)") for n in (f"cache_{nm}", f"cache_{nm}_sample")]
                act.dma_start(rows[1][:, :(PAST - DEC_S) * D], rows[0][:, DEC_S * D:]).then_inc(S.caches_kept, 16)


def build(nc, a):
    with ExitStack() as ctx:
        def sb(name, shape, dt=F32):
            return ctx.enter_context(nc.sbuf_tensor(name, shape, dt))

        def dram(name, shape):
            return nc.dram_tensor(name, shape, F32, kind="Internal").ap()

        S = Shared()
        S.res = sb("res", [P, DK, TOK])
        S.x_hi = sb("x_hi", [P, DK, TOK], F32R)
        S.x_lo = sb("x_lo", [P, DK, TOK], F32R)
        S.ident, S.ones, S.eps = sb("ident", [P, P]), sb("ones", [P, P]), sb("eps", [P, 1])
        S.causal, S.stream, S.own_mask = sb("causal", [P, 2, P]), sb("stream", [P, DEC_B]), sb("own_mask", [P, 2, P])
        S.gains = sb("gains", [P, 6, DK])
        S.gla_rows, S.qkv_rows = dram("gla_rows", [GLA_IN, TOK]), dram("qkv_rows", [3 * D, TOK])
        S.strips = dram("strips", [HEADS, P, STRIP])
        S.caches_kept = nc.alloc_semaphore("caches_kept")
        w_in = a["gla_w_in"][0]
        body = 2 * NQK + 2 * NV
        constants(nc, S, a)
        load_tokens(nc, S, a)
        norm(nc, S, "n0", G_MIX0)
        project(nc, S, "in", [(w_in, 0, body // P, None, S.gla_rows, 0, 0),
                              (w_in, GLA_IN - P, 1, None, S.gla_rows, body, P - RANK)])
        gla_core(nc, S, a)
        add_product(nc, S, "go", a["gla_w_out"][0])
        norm(nc, S, "n1", G_FFN0)
        keep_caches(nc, S, a)
        ffn(nc, S, "f0", a["ffn_w_gate"][0], a["ffn_w_up"][0], a["ffn_w_down"][0])
        norm(nc, S, "n2", None)
        project(nc, S, "qkv", [(a["attn_w_q"][0], 0, DK, G_MIX1, S.qkv_rows, 0, 0),
                               (a["w_kv"], 0, 2 * DK, G_KV, S.qkv_rows, D, 0)])
        attention_core(nc, S, a)
        add_product(nc, S, "ao", a["attn_w_out"][0])
        norm(nc, S, "n3", G_FFN1)
        ffn(nc, S, "f1", a["ffn_w_gate"][1], a["ffn_w_up"][1], a["ffn_w_down"][1])
        norm(nc, S, "n4", G_FINAL, final=True)
        store_tokens(nc, S, a)


_INS = ["x_prompt", "x_sample", "state_gla", "cache_k", "cache_v", "norm_mix", "norm_ffn", "norm_final",
        "gla_w_in", "gla_w_gate2", "gla_b_gate", "gla_norm", "gla_w_out", "kv_norm", "w_kv", "attn_w_q",
        "attn_rel_bias", "attn_w_out", "ffn_w_gate", "ffn_w_up", "ffn_w_down"]
_OUTS = [("y_prompt", (1, SEQ, D)), ("y_sample", (DEC_B, DEC_S, D)),
         ("state_gla_prompt", (1, 1, GLA_H, GLA_DK, GLA_DV)),
         ("cache_k_prompt", (1, 512, HEADS, DH)), ("cache_v_prompt", (1, 512, HEADS, DH)),
         ("state_gla_sample", (1, DEC_B, GLA_H, GLA_DK, GLA_DV)),
         ("cache_k_sample", (DEC_B, PAST, HEADS, DH)), ("cache_v_sample", (DEC_B, PAST, HEADS, DH))]


def kernel(**inputs):
    import numpy as _np
    import concourse.bacc as _bacc
    from concourse.bass_utils import run_bass_kernel_spmd as _run

    nc = _bacc.Bacc("TRN2", target_bir_lowering=False, num_devices=1)
    arrays, args = {}, {}
    for name in _INS:
        arrays[f"in_{name}"] = _np.ascontiguousarray(inputs[name])
        args[name] = nc.dram_tensor(f"in_{name}", arrays[f"in_{name}"].shape, F32, kind="ExternalInput").ap()
    for name, shape in _OUTS:
        args[name] = nc.dram_tensor(f"out_{name}", shape, F32, kind="ExternalOutput").ap()
    build(nc, args)
    r = _run(nc, [arrays], core_ids=[0])
    return tuple(r.results[0][f"out_{name}"] for name, _ in _OUTS)
```

```python
from contextlib import ExitStack, contextmanager

import concourse.bass as bass
from concourse import mybir

F32 = mybir.dt.float32
F32R = mybir.dt.float32r
I32 = mybir.dt.int32
ALU = mybir.AluOpType
ACT = mybir.ActivationFunctionType

P = 128
D = 1024
DK = D // P
SEQ = 1024
DEC_B, DEC_S = 8, 16
DEC = DEC_B * DEC_S
TOK = SEQ + DEC
NT = TOK // P
GRP = 384
NG = TOK // GRP
EPS = 1e-6
GLA_H, GLA_DK, GLA_DV, GLA_BLOCK, GLA_TAU, RANK = 4, 128, 256, 64, 16.0, 16
NQK, NV = GLA_H * GLA_DK, GLA_H * GLA_DV
GLA_IN = 2 * NQK + 2 * NV + RANK
HEADS, DH = 16, 64
PAIRS = HEADS // 2
PAST = 256
CHUNK = 64
BAND_T = 5
CLIP = 128
D_FF = 2816
MASKED = 1e30
STRIP_C = (BAND_T - 1) * P - 1
STRIP = STRIP_C + 2 * CLIP + 1

G_MIX0, G_MIX1, G_FFN0, G_FFN1, G_FINAL, G_KV = range(6)


class Ring:

    def __init__(self, slots, stages):
        self.slots, self.stages = slots, stages


class Segment:

    def __init__(self, w, col, units, gain, out, row, skip, base, slots):
        self.w, self.col, self.gain, self.out, self.row, self.skip = (
            w.rearrange("(k p) n -> p k n", p=P), col, gain, out, row, skip)
        self.per = min(slots, units)
        self.trips = units // self.per
        self.base, self.turn = base, base // slots
        assert base % slots == 0 and units % self.per == 0


class Shared:
    pass


def operands(nc, S, ctx, tag):
    S.x_hi = ctx.enter_context(nc.sbuf_tensor(f"{tag}_x_hi", [P, DK, TOK], F32R))
    S.x_lo = ctx.enter_context(nc.sbuf_tensor(f"{tag}_x_lo", [P, DK, TOK], F32R))


def f32(ap):
    return ap.bitcast(F32)


@contextmanager
def semaphores(nc):
    made = []

    def sem(name):
        made.append(nc.alloc_semaphore(name))
        return made[-1]

    yield sem
    nc.clear_and_free_semaphores(made)
    nc.all_engine_barrier()


def weight_ring(nc, sem, ctx, tag, slots, stages):
    r = Ring(slots, stages)
    r.stage = ctx.enter_context(nc.sbuf_tensor(f"{tag}_stage", [P, stages, D], F32))
    r.hi = ctx.enter_context(nc.sbuf_tensor(f"{tag}_w_hi", [P, slots, D], F32R))
    r.lo = ctx.enter_context(nc.sbuf_tensor(f"{tag}_w_lo", [P, slots, D], F32R))
    r.loaded = [sem(f"{tag}_w_loaded{i}") for i in range(stages)]
    r.scaled = sem(f"{tag}_w_scaled")
    r.rounded = sem(f"{tag}_w_rounded")
    r.split = sem(f"{tag}_w_split")
    return r


def fetch_unit(sp, r, unit, j, src):
    sp.wait_ge(r.split, unit + 1)
    sp.dma_start(r.stage[:, j % r.stages, :].rearrange("p (k n) -> p k n", n=src.shape[-1]) if len(src.shape) == 3
                 else r.stage[:, j % r.stages, :], src).then_inc(r.loaded[j % r.stages], 16)


def scale_unit(pool, r, unit, j, times, gain):
    pool.wait_ge(r.loaded[j % r.stages], 16 * (times + 1))
    st = r.stage[:, j % r.stages, :].rearrange("p (k n) -> p k n", n=P)
    pool.tensor_tensor(st, st, gain.unsqueeze(2).to_broadcast([P, DK, P]), ALU.mult).then_inc(r.scaled, 1)


def round_unit(act, r, unit, j, times, gain=None):
    if gain is None:
        act.wait_ge(r.loaded[j % r.stages], 16 * (times + 1))
    else:
        act.wait_ge(r.scaled, unit + 1)
    act.copy(r.hi[:, j % r.slots, :], r.stage[:, j % r.stages, :]).then_inc(r.rounded, 1)


def split_unit(pool, r, unit, j):
    pool.wait_ge(r.rounded, unit + 1)
    pool.tensor_tensor(r.lo[:, j % r.slots, :], r.stage[:, j % r.stages, :], f32(r.hi[:, j % r.slots, :]),
                       ALU.subtract).then_inc(r.split, 1)


def product(pe, out, w_hi, w_lo, x_hi, x_lo, first, last):
    pe.matmul(out, w_hi, x_hi, start=first, stop=False)
    pe.matmul(out, w_lo, x_hi, start=False, stop=False)
    return pe.matmul(out, w_hi, x_lo, start=False, stop=last)


def constants(nc, S, a):
    with semaphores(nc) as sem:
        gains_in, made, strip_in, strip_made, strip_out = (sem(n) for n in (
            "gains_in", "consts_made", "strip_in", "strip_made", "strip_out"))
        with ExitStack() as ctx:
            table = ctx.enter_context(nc.sbuf_tensor("bias_table", [HEADS, 2 * CLIP + 1], F32))
            strip = ctx.enter_context(nc.sbuf_tensor("bias_strip", [HEADS, STRIP], F32))
            block = ctx.enter_context(nc.Block())

            @block.sync
            def _(sp):
                rows = [a["norm_mix"][0], a["norm_mix"][1], a["norm_ffn"][0], a["norm_ffn"][1],
                        a["norm_final"], a["kv_norm"]]
                sp.dma_start(table[:], a["attn_rel_bias"][0]).then_inc(strip_in, 16)
                for i, row in enumerate(rows):
                    sp.dma_start(S.gains[:, i, :], row.rearrange("(k p) -> p k", p=P),
                                 allow_slow_non_contiguous=True).then_inc(gains_in, 16)
                sp.wait_ge(strip_made, 2)
                sp.dma_start(S.strips.rearrange("h r c -> h r c"),
                             strip[:].unsqueeze(1).to_broadcast([HEADS, P, STRIP])).then_inc(strip_out, 16)
                sp.wait_ge(gains_in, 16 * len(rows))
                sp.wait_ge(strip_out, 16)

            @block.vector
            def _(dve):
                dve.wait_ge(strip_in, 16)
                dve.tensor_scalar(strip[:, STRIP_C:], table[:, ::-1], -1.0, None, ALU.mult).then_inc(strip_made, 1)
                dve.tensor_scalar(strip[:, :STRIP_C], table[:, 2 * CLIP:].to_broadcast([HEADS, STRIP_C]), -1.0, None,
                                  ALU.mult).then_inc(strip_made, 1)

            @block.gpsimd
            def _(pool):
                n = [0]

                def step(ins):
                    n[0] += 1
                    ins.then_inc(made, 1)
                    pool.wait_ge(made, n[0])

                step(pool.memset(S.ident[:], 0.0))
                step(pool.affine_select(S.ident[:], S.ident[:], [[-1, P]], ALU.not_equal, 1.0, base=0,
                                        channel_multiplier=1))
                step(pool.memset(S.ones[:], 1.0))
                step(pool.memset(S.eps[:], EPS))
                step(pool.memset(S.causal[:], 1.0))
                step(pool.affine_select(S.causal[:, 0, :], S.causal[:, 0, :], [[1, P]], ALU.is_ge, 0.0, base=0,
                                        channel_multiplier=-1))
                step(pool.memset(S.causal[0:GLA_BLOCK, 0, GLA_BLOCK:], 0.0))
                step(pool.affine_select(S.causal[:, 1, :], S.causal[:, 1, :], [[1, P]], ALU.is_ge, 0.0, base=0,
                                        channel_multiplier=-1))
                view = S.causal[:, 1, :].rearrange("p (b s) -> p b s", s=DEC_S)
                step(pool.affine_select(view, view, [[-DEC_S, DEC_B], [0, DEC_S]], ALU.is_ge, 0.0, base=0,
                                        channel_multiplier=1))
                step(pool.memset(S.own_mask[:], 0.0))
                half = DEC_B // 2
                for head in range(2):
                    for g in range(2):
                        view = S.own_mask[head * DH:(head + 1) * DH, g, :].rearrange("p (b s) -> p b s", s=DEC_S)
                        for sign, base in ((1, half * DEC_S * g), (-1, DEC_S - 1 - half * DEC_S * g)):
                            step(pool.affine_select(view, view, [[-DEC_S * sign, DEC_B], [0, DEC_S]], ALU.is_ge, MASKED,
                                                    base=base, channel_multiplier=sign))
                step(pool.memset(S.stream[:], 1.0))
                step(pool.affine_select(S.stream[:], S.stream[:], [[-DEC_S, DEC_B]], ALU.is_ge, 0.0, base=0,
                                        channel_multiplier=1))
                step(pool.affine_select(S.stream[:], S.stream[:], [[DEC_S, DEC_B]], ALU.is_ge, 0.0,
                                        base=DEC_S - 1, channel_multiplier=-1))


def load_tokens(nc, S, a):
    with semaphores(nc) as sem:
        x_in = [sem(f"x_in{i}") for i in range(2)]
        turned, taken = sem("x_turned"), sem("x_taken")
        with ExitStack() as ctx:
            xt = ctx.enter_context(nc.sbuf_tensor("x_rows", [P, 2, D], F32))
            ps = ctx.enter_context(nc.psum_tensor("x_ps", [P, 2, D], F32))
            block = ctx.enter_context(nc.Block())
            rows = [a["x_prompt"][0, i * P:(i + 1) * P, :] for i in range(NT - 1)]
            rows.append(a["x_sample"].rearrange("b s d -> (b s) d"))

            @block.sync
            def _(sp):
                for i in range(NT):
                    if i >= 2:
                        sp.wait_ge(turned, i - 1)
                    sp.dma_start(xt[:, i % 2, :], rows[i]).then_inc(x_in[i % 2], 16)

            @block.tensor
            def _(pe):
                for i in range(NT):
                    pe.wait_ge(x_in[i % 2], 16 * (i // 2 + 1))
                    if i >= 2:
                        pe.wait_ge(taken, i - 1)
                    for k in range(DK):
                        t = pe.transpose(ps[:, i % 2, k * P:(k + 1) * P], xt[:, i % 2, k * P:(k + 1) * P], S.ident[:])
                    t.then_inc(turned, 1)

            @block.vector
            def _(dve):
                for i in range(NT):
                    dve.wait_ge(turned, i + 1)
                    dve.tensor_copy(S.res[:, :, i * P:(i + 1) * P],
                                    ps[:, i % 2, :].rearrange("p (k t) -> p k t", t=P)).then_inc(taken, 1)


class Norm:
    BUFS = 4

    def __init__(self, nc, S, sem, ctx, tag, gain, sums, spread, final=False):
        self.S, self.gain, self.sums, self.spread, self.final = S, gain, sums, spread, final
        self.squared, self.paired, self.added = sem(f"{tag}_squared"), sem(f"{tag}_paired"), sem(f"{tag}_added")
        self.summed, self.rooted, self.inverse = sem(f"{tag}_summed"), sem(f"{tag}_rooted"), sem(f"{tag}_inverse")
        self.diagonal, self.spread_out = sem(f"{tag}_diagonal"), sem(f"{tag}_spread")
        self.normed, self.rounded = sem(f"{tag}_normed"), sem(f"{tag}_rounded")
        self.low = [sem(f"{tag}_low{i}") for i in range(2)]
        self.work = ctx.enter_context(nc.sbuf_tensor(f"{tag}_work", [P, self.BUFS, GRP], F32))
        self.acc = ctx.enter_context(nc.sbuf_tensor(f"{tag}_acc", [P, NG, GRP], F32))
        self.rms = ctx.enter_context(nc.sbuf_tensor(f"{tag}_rms", [P, NT], F32))

    def chunk(self, tensor, c):
        t, k = divmod(c, DK)
        return tensor[:, k, t * GRP:(t + 1) * GRP]

    def splitter(self, c):
        by = [0 if i % DK % 3 == 0 else 1 for i in range(c + 1)]
        return by[c], by[:c].count(by[c])

    def scalar(self, act):
        for q in range(NG * DK // 2):
            t, i = divmod(q, DK // 2)
            if q >= 2:
                act.wait_ge(self.added, q - 1)
            act.activation(self.work[:, q % 2 * 2:q % 2 * 2 + 2, :], self.S.res[:, 2 * i:2 * i + 2, t * GRP:(t + 1) * GRP],
                           ACT.Square).then_inc(self.squared, 1)
        act.wait_ge(self.summed, NG)
        act.activation(self.rms[:], self.sums[:, :NT], ACT.Sqrt, bias=self.S.eps[:], scale=1.0 / D).then_inc(self.rooted, 1)

    def round(self, act):
        for c in range(NG * DK):
            act.wait_ge(self.normed, c + 1)
            act.copy(self.chunk(self.S.x_hi, c), self.work[:, c % self.BUFS, :]).then_inc(self.rounded, 1)

    def tensor(self, pe):
        for t in range(NG):
            pe.wait_ge(self.added, (t + 1) * DK // 2)
            for i in range(NG):
                tile = t * NG + i
                m = pe.matmul(self.sums[:, tile:tile + 1], self.acc[:, t, i * P:(i + 1) * P], self.S.ones[:, :1])
            m.then_inc(self.summed, 1)
        for t in range(NG):
            pe.wait_ge(self.diagonal, t + 1)
            pe.matmul(self.spread[t], self.S.ones[:], self.acc[:, t, :]).then_inc(self.spread_out, 1)

    def vector(self, dve):
        for q in range(NG * DK // 2):
            t, i = divmod(q, DK // 2)
            a, b = self.work[:, q % 2 * 2, :], self.work[:, q % 2 * 2 + 1, :]
            dve.wait_ge(self.squared, q + 1)
            if i == 0:
                dve.tensor_tensor(self.acc[:, t, :], a, b, ALU.add).then_inc(self.added, 1)
                continue
            dve.tensor_tensor(a, a, b, ALU.add).then_inc(self.paired, 1)
            dve.wait_ge(self.paired, t * (DK // 2 - 1) + i)
            dve.wait_ge(self.added, q)
            dve.tensor_tensor(self.acc[:, t, :], self.acc[:, t, :], a, ALU.add).then_inc(self.added, 1)
        dve.wait_ge(self.rooted, 1)
        dve.reciprocal(self.rms[:], self.rms[:]).then_inc(self.inverse, 1)
        dve.wait_ge(self.inverse, 1)
        for t in range(NG):
            dve.tensor_tensor(self.acc[:, t, :].rearrange("p (i c) -> p i c", c=P),
                              self.S.ident[:].unsqueeze(1).to_broadcast([P, NG, P]),
                              self.rms[:, t * NG:(t + 1) * NG].unsqueeze(2).to_broadcast([P, NG, P]),
                              ALU.mult).then_inc(self.diagonal, 1)
        for c in range(NG * DK + 2):
            if c < NG * DK:
                t, k = divmod(c, DK)
                if k == 0:
                    dve.wait_ge(self.spread_out, t + 1)
                if not self.final and c >= self.BUFS:
                    by, done = self.splitter(c - self.BUFS)
                    dve.wait_ge(self.low[by], done + 1)
                x = self.chunk(self.S.res, c)
                out = x if self.final else self.work[:, c % self.BUFS, :]
                if self.gain is None:
                    dve.tensor_tensor(out, x, self.spread[t], ALU.mult).then_inc(self.normed, 1)
                else:
                    dve.scalar_tensor_tensor(out, x, self.S.gains[:, self.gain, k:k + 1], self.spread[t], ALU.mult,
                                             ALU.mult).then_inc(self.normed, 1)
            if c >= 2 and not self.final and self.splitter(c - 2)[0] == 0:
                self.split(dve, c - 2)

    def split(self, engine, c):
        engine.wait_ge(self.rounded, c + 1)
        engine.tensor_tensor(self.chunk(self.S.x_lo, c), self.work[:, c % self.BUFS, :], f32(self.chunk(self.S.x_hi, c)),
                             ALU.subtract).then_inc(self.low[self.splitter(c)[0]], 1)

    def gpsimd(self, pool):
        for c in range(NG * DK):
            if self.splitter(c)[0] == 1:
                self.split(pool, c)

    def ready(self, pe, t):
        if self.final:
            pe.wait_ge(self.normed, (t + 1) * DK)
            return
        for by in range(2):
            pe.wait_ge(self.low[by], sum(self.splitter(c)[0] == by for c in range((t + 1) * DK)))


def project(nc, S, tag, gain, segments):
    SL, BANKS = 4, 6
    with semaphores(nc) as sem:
        filled = sem(f"{tag}_filled")
        drained = sem(f"{tag}_drained")
        stored = [sem(f"{tag}_stored{i}") for i in range(SL)]
        with ExitStack() as ctx:
            ring = weight_ring(nc, sem, ctx, tag, SL, SL)
            rows = ctx.enter_context(nc.sbuf_tensor(f"{tag}_sums", [P, SL, TOK], F32))
            ps = ctx.enter_context(nc.psum_tensor(f"{tag}_ps", [P, BANKS, 512], F32))
            norm = Norm(nc, S, sem, ctx, f"{tag}_norm", gain, ps[:, 2, :], [ps[:, 3 + t, :GRP] for t in range(NG)])
            block = ctx.enter_context(nc.Block())
            plan, base = [], 0
            for w, col, units, gain, out, row, skip in segments:
                plan.append(Segment(w, col, units, gain, out, row, skip, base, SL))
                base += units
            assert all(s.per == SL for s in plan[:-1])

            @block.sync
            def _(sp):
                def fetch(s, it, j):
                    fetch_unit(sp, ring, it * s.per + (s.base + j), j, s.w[:, :, bass.ds(it * (s.per * P) + (s.col + j * P), P)])

                def store(s, it, j):
                    sp.wait_ge(drained, it * (s.per * NG) + (BANKS + (s.base + j + 1) * NG))
                    sp.dma_start(s.out[bass.ds(it * (s.per * P) + (s.row + j * P), P - s.skip), :],
                                 rows[s.skip:, j, :]).then_inc(stored[j], 16)

                last = None
                for s in plan:
                    for j in range(s.per):
                        if last:
                            store(last, last.trips - 1, j)
                        fetch(s, 0, j)
                    if last:
                        for j in range(s.per, last.per):
                            store(last, last.trips - 1, j)
                    if s.trips > 1:
                        with sp.Fori(1, s.trips) as it:
                            for j in range(s.per):
                                store(s, it - 1, j)
                                fetch(s, it, j)
                    last = s
                for j in range(last.per):
                    store(last, last.trips - 1, j)
                for j in range(SL):
                    sp.wait_ge(stored[j], 16 * sum(s.trips for s in plan if j < s.per))

            BEFORE = 2

            @block.scalar
            def _(act):
                def units(s, it, first, last):
                    for j in range(first, last):
                        unit = it * s.per + (s.base + j)
                        act.wait_ge(filled, (unit + 1) * NG)
                        round_unit(act, ring, unit, j, it + s.turn, s.gain)

                norm.scalar(act)
                units(plan[0], 0, 0, BEFORE)
                norm.round(act)
                units(plan[0], 0, BEFORE, SL)
                for s in plan:
                    with act.Fori(1 if s is plan[0] else 0, s.trips) as it:
                        units(s, it, 0, s.per)

            @block.gpsimd
            def _(pool):
                def units(s, it, first, last):
                    for j in range(first, last):
                        unit = it * s.per + (s.base + j)
                        if s.gain is not None:
                            scale_unit(pool, ring, unit, j, it + s.turn, S.gains[:, s.gain, :])
                        split_unit(pool, ring, unit, j)

                pool.sem_inc(ring.split, SL)
                units(plan[0], 0, 0, BEFORE)
                norm.gpsimd(pool)
                units(plan[0], 0, BEFORE, SL)
                for s in plan:
                    with pool.Fori(1 if s is plan[0] else 0, s.trips) as it:
                        units(s, it, 0, s.per)

            @block.tensor
            def _(pe):
                pe.sem_inc(filled, SL * NG)
                norm.tensor(pe)
                for s in plan:
                    with pe.Fori(0, s.trips) as it:
                        for j in range(s.per):
                            pe.wait_ge(ring.split, it * s.per + (s.base + j + 1 + SL))
                            for t in range(NG):
                                g = j * NG + t
                                if s is plan[0] and j == 0:
                                    norm.ready(pe, t)
                                pe.wait_ge(drained, it * (s.per * NG) + (s.base * NG + g + 1))
                                for k in range(DK):
                                    w, x = slice(k * P, (k + 1) * P), slice(t * GRP, (t + 1) * GRP)
                                    m = product(pe, ps[:, g % BANKS, :GRP], ring.hi[:, j, w], ring.lo[:, j, w],
                                                S.x_hi[:, k, x], S.x_lo[:, k, x], k == 0, k == DK - 1)
                                m.then_inc(filled, 1)

            @block.vector
            def _(dve):
                norm.vector(dve)
                dve.sem_inc(drained, BANKS)
                for s in plan:
                    with dve.Fori(0, s.trips) as it:
                        for j in range(s.per):
                            dve.wait_ge(stored[j], (it + s.turn) * 16)
                            for t in range(NG):
                                g = j * NG + t
                                dve.wait_ge(filled, it * (s.per * NG) + (SL * NG + s.base * NG + g + 1))
                                dve.tensor_copy(rows[:, j, t * GRP:(t + 1) * GRP],
                                                ps[:, g % BANKS, :GRP]).then_inc(drained, 1)


def add_product(nc, S, tag, w):
    SL, BANKS = 4, 6
    with semaphores(nc) as sem:
        filled = sem(f"{tag}_filled")
        drained = sem(f"{tag}_drained")
        rounded, low = sem(f"{tag}_rounded"), sem(f"{tag}_low")
        with ExitStack() as ctx:
            operands(nc, S, ctx, tag)
            ring = weight_ring(nc, sem, ctx, tag, SL, SL)
            ps = ctx.enter_context(nc.psum_tensor(f"{tag}_ps", [P, BANKS, 512], F32))
            block = ctx.enter_context(nc.Block())
            wv = w.rearrange("(k p) n -> p k n", p=P)
            trips = DK // SL

            @block.sync
            def _(sp):
                with sp.Fori(0, trips) as it:
                    for j in range(SL):
                        fetch_unit(sp, ring, it * SL + j, j, wv[:, :, bass.ds(it * (SL * P) + j * P, P)])

            @block.scalar
            def _(act):
                for t in range(NG):
                    cols = slice(t * GRP, (t + 1) * GRP)
                    act.copy(S.x_hi[:, :, cols], S.mixed[:, :, cols]).then_inc(rounded, 1)
                with act.Fori(0, trips) as it:
                    for j in range(SL):
                        act.wait_ge(filled, it * (SL * NG) + (j + 1) * NG)
                        round_unit(act, ring, it * SL + j, j, it)

            @block.gpsimd
            def _(pool):
                pool.sem_inc(ring.split, SL)
                with pool.Fori(0, trips) as it:
                    for j in range(SL):
                        split_unit(pool, ring, it * SL + j, j)

            @block.tensor
            def _(pe):
                pe.sem_inc(filled, SL * NG)
                pe.wait_ge(low, NG)
                with pe.Fori(0, trips) as it:
                    for j in range(SL):
                        pe.wait_ge(ring.split, it * SL + (j + 1 + SL))
                        for t in range(NG):
                            g = j * NG + t
                            pe.wait_ge(drained, it * (SL * NG) + (g + 1))
                            for k in range(DK):
                                c, x = slice(k * P, (k + 1) * P), slice(t * GRP, (t + 1) * GRP)
                                m = product(pe, ps[:, g % BANKS, :GRP], ring.hi[:, j, c], ring.lo[:, j, c],
                                            S.x_hi[:, k, x], S.x_lo[:, k, x], k == 0, k == DK - 1)
                            m.then_inc(filled, 1)

            @block.vector
            def _(dve):
                dve.sem_inc(drained, BANKS)
                for t in range(NG):
                    cols = slice(t * GRP, (t + 1) * GRP)
                    dve.wait_ge(rounded, t + 1)
                    dve.tensor_tensor(S.x_lo[:, :, cols], S.mixed[:, :, cols], f32(S.x_hi[:, :, cols]),
                                      ALU.subtract).then_inc(low, 1)
                res = S.res[:].rearrange("p k t -> p (k t)")
                with dve.Fori(0, trips) as it:
                    for j in range(SL):
                        for t in range(NG):
                            g = j * NG + t
                            dve.wait_ge(filled, it * (SL * NG) + (SL * NG + g + 1))
                            h = res[:, bass.ds(it * (SL * TOK) + (j * TOK + t * GRP), GRP)]
                            dve.tensor_tensor(h, h, ps[:, g % BANKS, :GRP], ALU.add).then_inc(drained, 1)


def ffn(nc, S, tag, gain, w_gate, w_up, w_down):
    HT, SL, ST, BANKS = 2, 6, 3, 4
    trips = D_FF // P // HT
    PAIRS_B = HT * NG
    DOWN_B = NG * DK
    with semaphores(nc) as sem:
        pair_filled = sem(f"{tag}_pair_filled")
        gated = sem(f"{tag}_gated")
        pair_drained = sem(f"{tag}_pair_drained")
        hid_rounded = sem(f"{tag}_hid_rounded")
        hid_split = sem(f"{tag}_hid_split")
        down_filled = sem(f"{tag}_down_filled")
        down_drained = sem(f"{tag}_down_drained")
        with ExitStack() as ctx:
            ring = weight_ring(nc, sem, ctx, tag, SL, ST)
            hid_hi = ctx.enter_context(nc.sbuf_tensor(f"{tag}_hid_hi", [P, HT, TOK], F32R))
            hid_lo = ctx.enter_context(nc.sbuf_tensor(f"{tag}_hid_lo", [P, HT, TOK], F32R))
            gate = ctx.enter_context(nc.sbuf_tensor(f"{tag}_gate", [P, 2, GRP], F32))
            hid = ctx.enter_context(nc.sbuf_tensor(f"{tag}_hid", [P, 2, GRP], F32))
            ps = ctx.enter_context(nc.psum_tensor(f"{tag}_pair_ps", [P, 2, 2, 512], F32))
            dps = ctx.enter_context(nc.psum_tensor(f"{tag}_down_ps", [P, BANKS, 512], F32))
            norm = Norm(nc, S, sem, ctx, f"{tag}_norm", gain, dps[:, 0, :], [dps[:, 1 + t, :GRP] for t in range(NG)])
            block = ctx.enter_context(nc.Block())
            columns = [w.rearrange("(k p) n -> p k n", p=P) for w in (w_gate, w_up)]

            @block.sync
            def _(sp):
                with sp.Fori(0, trips) as it:
                    for j in range(SL):
                        f = j // 2 if j < 2 * HT else j - 2 * HT
                        if j < 2 * HT:
                            src = columns[j % 2][:, :, bass.ds(it * (HT * P) + f * P, P)]
                        else:
                            src = w_down[bass.ds(it * (HT * P) + f * P, P), :]
                        fetch_unit(sp, ring, it * SL + j, j, src)

            @block.scalar
            def _(act):
                def gate_up(it, f):
                    for j in (2 * f, 2 * f + 1):
                        act.wait_ge(pair_filled, it * PAIRS_B + (f + 1) * NG)
                        round_unit(act, ring, it * SL + j, j, it * (SL // ST) + j // ST)

                def hidden(it):
                    for g in range(PAIRS_B):
                        f, t = divmod(g, NG)
                        act.wait_ge(pair_filled, it * PAIRS_B + (PAIRS_B + g + 1))
                        act.wait_ge(pair_drained, it * PAIRS_B + (g + 1))
                        act.activation(gate[:, g % 2, :], ps[:, g % 2, 0, :GRP], ACT.Silu).then_inc(gated, 1)
                        act.wait_ge(pair_drained, it * PAIRS_B + (g + 3))
                        act.wait_ge(down_filled, it * DOWN_B + (t + 1) * DK)
                        act.copy(hid_hi[:, f, t * GRP:(t + 1) * GRP], hid[:, g % 2, :]).then_inc(hid_rounded, 1)
                        if g == 0:
                            for j in range(2 * HT, SL):
                                act.wait_ge(down_filled, it * DOWN_B + DOWN_B)
                                round_unit(act, ring, it * SL + j, j, it * (SL // ST) + j // ST)

                norm.scalar(act)
                gate_up(0, 0)
                norm.round(act)
                for f in range(1, HT):
                    gate_up(0, f)
                hidden(0)
                with act.Fori(1, trips) as it:
                    for f in range(HT):
                        gate_up(it, f)
                    hidden(it)

            @block.gpsimd
            def _(pool):
                def hidden(it):
                    for g in range(PAIRS_B):
                        f, t = divmod(g, NG)
                        pool.wait_ge(hid_rounded, it * PAIRS_B + (g + 1))
                        cols = slice(t * GRP, (t + 1) * GRP)
                        pool.tensor_tensor(hid_lo[:, f, cols], hid[:, g % 2, :], f32(hid_hi[:, f, cols]),
                                           ALU.subtract).then_inc(hid_split, 1)
                        if g == 0:
                            for j in range(2 * HT, SL):
                                split_unit(pool, ring, it * SL + j, j)

                pool.sem_inc(ring.split, ST)
                for j in range(2):
                    split_unit(pool, ring, j, j)
                norm.gpsimd(pool)
                for j in range(2, 2 * HT):
                    split_unit(pool, ring, j, j)
                hidden(0)
                with pool.Fori(1, trips) as it:
                    for j in range(2 * HT):
                        split_unit(pool, ring, it * SL + j, j)
                    hidden(it)

            @block.tensor
            def _(pe):
                pe.sem_inc(pair_filled, PAIRS_B)
                pe.sem_inc(down_filled, DOWN_B)
                norm.tensor(pe)
                with pe.Fori(0, trips) as it:
                    for g in range(PAIRS_B):
                        f, t = divmod(g, NG)
                        if t == 0:
                            pe.wait_ge(ring.split, it * SL + (ST + 2 * f + 2))
                        pe.wait_ge(pair_drained, it * PAIRS_B + (g + 1))
                        if f == 0:
                            norm.ready(pe, t)
                        x = slice(t * GRP, (t + 1) * GRP)
                        for u in range(2):
                            for k in range(DK):
                                c = slice(k * P, (k + 1) * P)
                                m = product(pe, ps[:, g % 2, u, :GRP], ring.hi[:, 2 * f + u, c], ring.lo[:, 2 * f + u, c],
                                            S.x_hi[:, k, x], S.x_lo[:, k, x], k == 0, k == DK - 1)
                        m.then_inc(pair_filled, 1)
                    pe.wait_ge(ring.split, it * SL + (ST + SL))
                    for t in range(NG):
                        pe.wait_ge(hid_split, it * PAIRS_B + ((HT - 1) * NG + t + 1))
                        x = slice(t * GRP, (t + 1) * GRP)
                        for m in range(DK):
                            g = t * DK + m
                            pe.wait_ge(down_drained, it * DOWN_B + (g + 1))
                            c = slice(m * P, (m + 1) * P)
                            for f in range(HT):
                                ins = product(pe, dps[:, g % BANKS, :GRP], ring.hi[:, 2 * HT + f, c],
                                              ring.lo[:, 2 * HT + f, c], hid_hi[:, f, x], hid_lo[:, f, x],
                                              f == 0, f == HT - 1)
                            ins.then_inc(down_filled, 1)

            @block.vector
            def _(dve):
                norm.vector(dve)
                dve.sem_inc(pair_drained, 2)
                dve.sem_inc(down_drained, BANKS)
                with dve.Fori(0, trips) as it:
                    for g in range(PAIRS_B):
                        dve.wait_ge(gated, it * PAIRS_B + (g + 1))
                        if g >= 2:
                            dve.wait_ge(hid_split, it * PAIRS_B + (g - 1))
                        dve.tensor_tensor(hid[:, g % 2, :], gate[:, g % 2, :], ps[:, g % 2, 1, :GRP],
                                          ALU.mult).then_inc(pair_drained, 1)
                    for t in range(NG):
                        for m in range(DK):
                            g = t * DK + m
                            dve.wait_ge(down_filled, it * DOWN_B + (DOWN_B + g + 1))
                            h = S.res[:, m, t * GRP:(t + 1) * GRP]
                            dve.tensor_tensor(h, h, dps[:, g % BANKS, :GRP], ALU.add).then_inc(down_drained, 1)


def store_tokens(nc, S, a):
    with semaphores(nc) as sem:
        turned, taken = sem("y_turned"), sem("y_taken")
        y_out = [sem(f"y_out{i}") for i in range(2)]
        with ExitStack() as ctx:
            yt = ctx.enter_context(nc.sbuf_tensor("y_rows", [P, 2, D], F32))
            ps = ctx.enter_context(nc.psum_tensor("y_ps", [P, 2, D], F32))
            nps = ctx.enter_context(nc.psum_tensor("y_norm_ps", [P, 1 + NG, 512], F32))
            norm = Norm(nc, S, sem, ctx, "y_norm", G_FINAL, nps[:, 0, :], [nps[:, 1 + t, :GRP] for t in range(NG)],
                        final=True)
            block = ctx.enter_context(nc.Block())
            rows = [a["y_prompt"][0, i * P:(i + 1) * P, :] for i in range(NT - 1)]
            rows.append(a["y_sample"].rearrange("b s d -> (b s) d"))

            @block.scalar
            def _(act):
                norm.scalar(act)
                for i in range(NT):
                    act.wait_ge(turned, i + 1)
                    if i >= 2:
                        act.wait_ge(y_out[i % 2], 16 * (i // 2))
                    act.copy(yt[:, i % 2, :], ps[:, i % 2, :]).then_inc(taken, 1)

            @block.tensor
            def _(pe):
                norm.tensor(pe)
                for i in range(NT):
                    norm.ready(pe, i * P // GRP)
                    if i >= 2:
                        pe.wait_ge(taken, i - 1)
                    for k in range(DK):
                        t = pe.transpose(ps[:, i % 2, k * P:(k + 1) * P], S.res[:, k, i * P:(i + 1) * P], S.ident[:])
                    t.then_inc(turned, 1)

            @block.vector
            def _(dve):
                norm.vector(dve)

            @block.sync
            def _(sp):
                for i in range(NT):
                    sp.wait_ge(taken, i + 1)
                    sp.dma_start(rows[i], yt[:, i % 2, :]).then_inc(y_out[i % 2], 16)
                for j in range(2):
                    sp.wait_ge(y_out[j], 16 * len(range(j, NT, 2)))
                sp.wait_ge(S.caches_kept, 2 * DEC_B * 16)


def gla_core(nc, S, a):
    with semaphores(nc) as sem:
        NB = SEQ // GLA_BLOCK
        NTP = NT - 1
        VT = GLA_DV // P
        small_in, qk_in, v_in, g_in, st_in = (sem(f"gla_{n}_in") for n in ("small", "qk", "v", "g", "state"))
        turn_filled = sem("gla_turn_filled")
        turn_drained = sem("gla_turn_drained")
        logit_in = sem("gla_logit_in")
        softplus = sem("gla_softplus")
        decay = sem("gla_decay")
        grown = sem("gla_grown")
        scaled = sem("gla_scaled")
        zeroed = sem("gla_zeroed")
        mask_turn = sem("gla_mask_turn")
        s_filled, s_masked = sem("gla_scores_filled"), sem("gla_scores_masked")
        u_filled, stepped = sem("gla_update_filled"), sem("gla_state_stepped")
        o_filled, o_drained = sem("gla_out_filled"), sem("gla_out_drained")
        spread = sem("gla_k2_spread")
        squared, rooted, gated, inverse, normed = (sem(f"gla_{n}") for n in (
            "squared", "rooted", "gated", "inverse", "normed"))
        mixed = sem("gla_mixed")
        st_out = sem("gla_state_out")
        TURNS = 14
        STEPS = NB + DEC_B
        with ExitStack() as ctx:
            def sb(name, shape, dt=F32):
                return ctx.enter_context(nc.sbuf_tensor(f"mix_{name}", shape, dt))

            def pb(name, shape):
                return ctx.enter_context(nc.psum_tensor(f"mix_{name}", shape, F32))

            w2 = sb("w_gate2", [RANK, P])
            bg = sb("b_gate", [P, 1])
            ng = sb("norm_gain", [P, VT])
            reset = sb("reset", [P, TOK])
            q, k = sb("q", [P, TOK]), sb("k", [P, TOK])
            vt = sb("vt", [P, VT, TOK])
            g = sb("g", [P, VT, TOK])
            v = sb("v", [P, NT, GLA_DV])
            soft = sb("soft", [P, TOK])
            least = sb("least", [P, TOK])
            b = sb("b", [P, TOK])
            eb = sb("eb", [P, TOK])
            k2t = sb("k2t", [P, NT, P])
            o = sb("o", [P, VT, TOK])
            st_s = sb("state_sample", [P, DEC_B, GLA_DV])
            st = sb("state", [P, 4, GLA_DV])
            st_fin = sb("state_last", [P, GLA_DV])
            sc = sb("scores", [P, 3, P])
            turn = pb("turn", [P, 2, 512])
            sps, ups, ops = pb("score_ps", [P, 2, 512]), pb("update_ps", [P, 2, 512]), pb("out_ps", [P, 2, 512])
            block = ctx.enter_context(nc.Block())
            zt = S.gla_rows
            spread_k2 = vt[:].rearrange("p j t -> p (j t)")[:, :DEC_B * P].rearrange("p (b k) -> p b k", k=P)

            @block.sync
            def _(sp):
                with sp.Fori(0, GLA_H) as h:
                    sp.wait_ge(scaled, h * 4)
                    sp.dma_start(w2[:], a["gla_w_gate2"][0, :, bass.ds(h * P, P)]).then_inc(small_in, 16)
                    sp.dma_start(bg[:], a["gla_b_gate"].rearrange("l (n o) -> (l n) o", o=1)[bass.ds(h * P, P), :]).then_inc(small_in, 16)
                    sp.dma_start(least[0:RANK, :], zt[2 * NQK + 2 * NV:, :]).then_inc(small_in, 16)
                    sp.wait_ge(o_filled, h * NT)
                    sp.dma_start(q[:], zt[bass.ds(h * P, P), :]).then_inc(qk_in, 16)
                    sp.dma_start(k[:], zt[bass.ds(h * P + NQK, P), :]).then_inc(qk_in, 16)
                    sp.wait_ge(turn_filled, h * TURNS)
                    sp.dma_start(vt[:], zt[bass.ds(h * GLA_DV + 2 * NQK, GLA_DV), :].rearrange("(j p) t -> p j t", p=P)).then_inc(v_in, 16)
                    sp.wait_ge(st_out, h * 32)
                    sp.dma_start(st_s[:], a["state_gla"][0, :, bass.ds(h, 1), :, :].rearrange("b o k v -> (o k) b v")).then_inc(st_in, 16)
                    sp.wait_ge(mixed, h)
                    sp.dma_start(g[:], zt[bass.ds(h * GLA_DV + 2 * NQK + NV, GLA_DV), :].rearrange("(j p) t -> p j t", p=P)).then_inc(g_in, 16)
                    sp.dma_start(ng[:], a["gla_norm"].rearrange("l (h j p) -> p (l h) j", j=VT, p=P)[:, bass.ds(h, 1), :],
                                 allow_slow_non_contiguous=True).then_inc(g_in, 16)

            @block.tensor
            def _(pe):
                def bank(h, n):
                    pe.wait_ge(turn_drained, h * TURNS + (n + 1))
                    return turn[:, n % 2, :]

                with pe.Fori(0, GLA_H) as h:
                    pe.wait_ge(small_in, (h + 1) * 48)
                    for t in range(NG):
                        ps = bank(h, t)
                        pe.matmul(ps[:, :GRP], w2[:], least[0:RANK, t * GRP:(t + 1) * GRP]).then_inc(turn_filled, 1)
                    pe.wait_ge(v_in, (h + 1) * 16)
                    for n in range(5):
                        ps = bank(h, NG + n)
                        for i in range(2 * n, min(2 * n + 2, NT)):
                            for j in range(VT):
                                c = (i % 2) * GLA_DV + j * P
                                m = pe.transpose(ps[:, c:c + P], vt[:, j, i * P:(i + 1) * P], S.ident[:])
                        m.then_inc(turn_filled, 1)
                    pe.wait_ge(scaled, (h + 1) * 4)
                    for n in range(3):
                        ps = bank(h, NG + 5 + n)
                        for i in range(4 * n, min(4 * n + 4, NT)):
                            m = pe.transpose(ps[:, (i % 4) * P:(i % 4 + 1) * P], soft[:, i * P:(i + 1) * P], S.ident[:])
                        m.then_inc(turn_filled, 1)
                    pe.wait_ge(turn_drained, h * TURNS + (2 + NG + 8))

                    def out(i):
                        pe.wait_ge(s_masked, h * NT + (2 + i + 1))
                        if i < NTP:
                            pe.wait_ge(stepped, h * STEPS + (4 + 2 * i + 1))
                        else:
                            pe.wait_ge(st_in, (h + 1) * 16)
                        pe.wait_ge(o_drained, h * NT + (2 if i == 0 else i + 1))
                        slot = i % 2 if i < NTP else 2
                        for j in range(VT):
                            dst, vc = ops[:, i % 2, j * P:(j + 1) * P], slice(j * P, (j + 1) * P)
                            pe.matmul(dst, v[:, i, vc], sc[:, slot, :], start=True, stop=False)
                            if i < NTP:
                                for c in range(2):
                                    cols = slice(c * GLA_BLOCK, (c + 1) * GLA_BLOCK)
                                    m = pe.matmul(dst[:, cols], st[:, (2 * i + c) % 4, vc],
                                                  q[:, i * P + c * GLA_BLOCK:i * P + (c + 1) * GLA_BLOCK],
                                                  start=False, stop=c == 1)
                            else:
                                for s in range(DEC_B):
                                    cols = slice(s * DEC_S, (s + 1) * DEC_S)
                                    m = pe.matmul(dst[:, cols], st_s[:, s, vc],
                                                  q[:, SEQ + s * DEC_S:SEQ + (s + 1) * DEC_S],
                                                  start=False, stop=s == DEC_B - 1)
                        m.then_inc(o_filled, 1)

                    for i in range(NT):
                        pe.wait_ge(s_masked, h * NT + (2 if i == 0 else i + 1))
                        cols = slice(i * P, (i + 1) * P)
                        pe.matmul(sps[:, i % 2, :P], k[:, cols], q[:, cols]).then_inc(s_filled, 1)
                        if i:
                            out(i - 1)
                        if i < NTP:
                            pe.wait_ge(stepped, h * STEPS + (4 + 2 * i))
                            for c in range(2):
                                r = slice(c * GLA_BLOCK, (c + 1) * GLA_BLOCK)
                                m = pe.matmul(ups[:, c, :GLA_DV], k2t[r, i, :], v[r, i, :])
                            m.then_inc(u_filled, 1)
                    out(NTP)
                    pe.wait_ge(spread, h + 1)
                    for n in range(DEC_B // 2):
                        pe.wait_ge(stepped, h * STEPS + (4 + NB + 2 * n))
                        for c in range(2):
                            m = pe.matmul(ups[:, c, :GLA_DV], spread_k2[:, 2 * n + c, :], v[:, NTP, :])
                        m.then_inc(u_filled, 1)
                    pe.wait_ge(squared, h + 1)
                    for t in range(NG):
                        ps = bank(h, NG + 8 + t)
                        for j in range(VT):
                            m = pe.matmul(ps[:, :GRP], S.ones[:], vt[:, j, t * GRP:(t + 1) * GRP],
                                          start=j == 0, stop=j == VT - 1)
                        m.then_inc(turn_filled, 1)

            @block.scalar
            def _(act):
                with act.Fori(0, GLA_H) as h:
                    for t in range(NG):
                        act.wait_ge(turn_filled, h * TURNS + (t + 1))
                        if t == 0:
                            act.wait_ge(turn_filled, h * TURNS)
                        act.activation(soft[:, t * GRP:(t + 1) * GRP], turn[:, t % 2, :GRP], ACT.Identity,
                                       bias=bg[:]).then_inc(turn_drained, 1)
                    act.wait_ge(decay, h * 3 + 1)
                    act.activation(soft[:], soft[:], ACT.Abs).then_inc(softplus, 1)
                    act.wait_ge(softplus, h * 3 + 1)
                    act.activation(soft[:], soft[:], ACT.Exp, scale=-1.0).then_inc(softplus, 1)
                    act.wait_ge(softplus, h * 3 + 2)
                    act.activation(soft[:], soft[:], ACT.Ln, bias=1.0).then_inc(softplus, 1)
                    for n in range(5):
                        act.wait_ge(turn_filled, h * TURNS + (NG + n + 1))
                        w = min(2, NT - 2 * n)
                        act.copy(v[:, 2 * n:2 * n + w, :], turn[:, (NG + n) % 2, :w * GLA_DV].rearrange("p (i d) -> p i d", d=GLA_DV)
                                 ).then_inc(turn_drained, 1)
                    act.wait_ge(decay, h * 3 + 3)
                    act.activation(eb[:], b[:], ACT.Exp, scale=1.0 / GLA_TAU).then_inc(grown, 1)
                    act.activation(least[:], b[:], ACT.Exp, scale=-1.0 / GLA_TAU).then_inc(grown, 1)
                    for n in range(3):
                        act.wait_ge(turn_filled, h * TURNS + (NG + 5 + n + 1))
                        w = min(4, NT - 4 * n)
                        act.copy(k2t[:, 4 * n:4 * n + w, :], turn[:, (NG + 5 + n) % 2, :w * P].rearrange("p (i d) -> p i d", d=P)
                                 ).then_inc(turn_drained, 1)
                    for i in range(NT):
                        act.wait_ge(o_filled, h * NT + (i + 1))
                        act.copy(o[:, :, i * P:(i + 1) * P], ops[:, i % 2, :VT * P].rearrange("p (j t) -> p j t", t=P)
                                 ).then_inc(o_drained, 1)
                    act.wait_ge(o_drained, h * NT + (2 + NT))
                    act.wait_ge(u_filled, (h + 1) * (STEPS // 2))
                    act.activation(vt[:], o[:], ACT.Square).then_inc(squared, 1)
                    for t in range(NG):
                        act.wait_ge(turn_filled, h * TURNS + (NG + 8 + t + 1))
                        act.activation(b[:, t * GRP:(t + 1) * GRP], turn[:, (NG + 8 + t) % 2, :GRP], ACT.Sqrt,
                                       bias=S.eps[:], scale=1.0 / GLA_DV).then_inc(turn_drained, 1)
                    act.wait_ge(g_in, (h + 1) * 32)
                    act.activation(g[:], g[:], ACT.Silu).then_inc(gated, 1)
                    act.wait_ge(stepped, (h + 1) * STEPS + 4)
                    act.dma_start(a["state_gla_prompt"][0, 0, bass.ds(h, 1), :, :].rearrange("o k v -> (o k) v"), st_fin[:]).then_inc(st_out, 16)
                    act.dma_start(a["state_gla_sample"][0, :, bass.ds(h, 1), :, :].rearrange("b o k v -> (o k) b v"), st_s[:]).then_inc(st_out, 16)
                act.wait_ge(st_out, GLA_H * 32)

            @block.vector
            def _(dve):
                dve.sem_inc(turn_drained, 2)
                dve.sem_inc(s_masked, 2)
                dve.sem_inc(stepped, 4)
                dve.sem_inc(o_drained, 2)
                dve.memset(sc[:], 0.0).then_inc(zeroed, 1)
                dve.memset(reset[:], 1.0).then_inc(zeroed, 1)
                dve.wait_ge(zeroed, 2)
                dve.memset(reset[:, 0:SEQ:GLA_BLOCK], 0.0).then_inc(zeroed, 1)
                dve.memset(reset[:, SEQ::DEC_S], 0.0).then_inc(zeroed, 1)
                dve.wait_ge(zeroed, 4)
                with dve.Fori(0, GLA_H) as h:
                    dve.wait_ge(turn_drained, h * TURNS + (2 + NG))
                    dve.tensor_scalar(least[:], soft[:], 0.0, None, ALU.min).then_inc(decay, 1)
                    dve.wait_ge(softplus, (h + 1) * 3)
                    dve.wait_ge(decay, h * 3 + 1)
                    dve.tensor_tensor(least[:], least[:], soft[:], ALU.subtract).then_inc(decay, 1)
                    dve.wait_ge(decay, h * 3 + 2)
                    dve.tensor_tensor_scan(b[:], reset[:], least[:], 0.0, ALU.mult, ALU.add).then_inc(decay, 1)
                    dve.wait_ge(qk_in, (h + 1) * 32)
                    dve.wait_ge(grown, (h + 1) * 2)
                    dve.scalar_tensor_tensor(q[:], q[:], GLA_DK ** -0.5, eb[:], ALU.mult, ALU.mult).then_inc(scaled, 1)
                    dve.tensor_tensor(k[:], k[:], least[:], ALU.mult).then_inc(scaled, 1)
                    dve.wait_ge(scaled, h * 4 + 2)
                    for lo, hi, blk in ((0, SEQ, GLA_BLOCK), (SEQ, TOK, DEC_S)):
                        n = (hi - lo) // blk
                        dve.tensor_tensor(soft[:, lo:hi].rearrange("p (n t) -> p n t", t=blk),
                                          k[:, lo:hi].rearrange("p (n t) -> p n t", t=blk),
                                          eb[:, lo + blk - 1:hi:blk].unsqueeze(2).to_broadcast([P, n, blk]),
                                          ALU.mult).then_inc(scaled, 1)
                    dve.wait_ge(o_filled, h * NT)
                    dve.memset(st[:, 0, :], 0.0).then_inc(zeroed, 1)
                    dve.wait_ge(zeroed, h + 5)
                    for i in range(NT):
                        dve.wait_ge(s_filled, h * NT + (i + 1))
                        if i >= 2:
                            dve.wait_ge(o_filled, h * NT + (i - 1))
                        dve.sem_inc(mask_turn, 1)
                        dve.copy_predicated(sc[:, i % 2 if i < NTP else 2, :],
                                            S.causal[:, 0 if i < NTP else 1, :].bitcast(I32),
                                            sps[:, i % 2, :P]).then_inc(s_masked, 1)
                        if i == NTP:
                            break
                        dve.wait_ge(u_filled, h * (STEPS // 2) + (i + 1))
                        for c in range(2):
                            n = 2 * i + c
                            dve.wait_ge(stepped, h * STEPS + (4 + n))
                            if n >= 3:
                                dve.wait_ge(o_filled, h * NT + ((n - 3) // 2 + 1))
                            if n == NB - 1:
                                dve.wait_ge(st_out, h * 32)
                            last = n * GLA_BLOCK + GLA_BLOCK - 1
                            dst = st_fin[:] if n == NB - 1 else st[:, (n + 1) % 4, :]
                            dve.scalar_tensor_tensor(dst, st[:, n % 4, :], eb[:, last:last + 1],
                                                     ups[:, c, :GLA_DV],
                                                     ALU.mult, ALU.add).then_inc(stepped, 1)
                    dve.wait_ge(turn_drained, h * TURNS + (2 + NG + 8))
                    dve.tensor_tensor(spread_k2, k2t[:, NTP:NT, :].to_broadcast([P, DEC_B, P]),
                                      S.stream[:].unsqueeze(2).to_broadcast([P, DEC_B, P]), ALU.mult).then_inc(spread, 1)
                    dve.wait_ge(o_filled, (h + 1) * NT)
                    for n in range(DEC_B):
                        dve.wait_ge(u_filled, h * (STEPS // 2) + (NB // 2 + n // 2 + 1))
                        last = SEQ + n * DEC_S + DEC_S - 1
                        dve.scalar_tensor_tensor(st_s[:, n, :], st_s[:, n, :], eb[:, last:last + 1],
                                                 ups[:, n % 2, :GLA_DV],
                                                 ALU.mult, ALU.add).then_inc(stepped, 1)
                    dve.wait_ge(turn_drained, (h + 1) * TURNS + 2)
                    dve.reciprocal(b[:], b[:]).then_inc(inverse, 1)
                    dve.wait_ge(inverse, h + 1)
                    dve.wait_ge(gated, h + 1)
                    for j in range(VT):
                        dve.scalar_tensor_tensor(o[:, j, :], o[:, j, :], ng[:, j:j + 1], b[:],
                                                 ALU.mult, ALU.mult).then_inc(normed, 1)
                    dve.wait_ge(normed, (h + 1) * VT)
                    dve.tensor_tensor(S.mixed[:].rearrange("p k t -> p (k t)")[:, bass.ds(h * (VT * TOK), VT * TOK)],
                                      o[:].rearrange("p j t -> p (j t)"), g[:].rearrange("p j t -> p (j t)"),
                                      ALU.mult).then_inc(mixed, 1)


def attention_core(nc, S, a):
    with semaphores(nc) as sem:
        NTP = NT - 1
        UNITS = 2 * NTP
        GB = DEC_B // 2
        GROUPS = DEC_B // GB
        ALLU = UNITS + GROUPS
        KEPT = 5
        KT_S = PAST // P
        WIDE = BAND_T * P
        SW = PAST + P
        BANK = 512
        PREPS = 4
        AT_Q, AT_FILL = 9, 10
        AT_KEYS = (2, 7)

        def width(u):
            return P * min(u // 2 + 1, BAND_T) if u < UNITS else SW

        def parts(u):
            w = width(u)
            return [(0, w)] if w <= 3 * P else [(0, 3 * P), (3 * P, w)]

        def order(last):
            number, n = {}, PREPS
            for u in range(ALLU + 2 if last else ALLU):
                if not last and AT_FILL <= u < AT_FILL + PREPS:
                    number["prep", u - AT_FILL] = n
                    n += 1
                if u in AT_KEYS:
                    for m in range(2):
                        number["keys", AT_KEYS.index(u), m] = n
                        n += 1
                if u >= 2:
                    for m in range(len(parts(u - 2))):
                        number["probs", u - 2, m] = n
                        n += 1
            return number, n

        STEADY, end = order(False)
        FILLS = end - PREPS + GROUPS
        for g in range(GROUPS):
            STEADY["probs", UNITS + g, 0] = FILLS + PREPS - GROUPS + g
        LAST, _ = order(True)
        assert FILLS % 2 == 0

        LAST_PAIR = PAIRS - 1

        def fill(h, *key):
            n = (LAST if isinstance(h, int) and h == LAST_PAIR else STEADY)[key]
            return n % 2, h * (FILLS // 2) + n // 2, h * FILLS + n

        def prep_fill(h, n):
            return (n % 2, n // 2, n) if h is None else fill(h, "prep", n)

        def back(h, u, steps):
            v = u - steps
            if v < 0:
                return (None, None) if isinstance(h, int) and h == 0 else (h - 1, v + ALLU)
            return (h, v) if v < ALLU else (None, None)

        def pairs(engine, body):
            body(0, 0, False)
            with engine.Fori(0, (PAIRS - 2) // 2) as it:
                body(it * 2 + 1, 1, False)
                body(it * 2 + 2, 0, False)
            body(LAST_PAIR, 1, True)

        qkv_in, bias_in = sem("att_qkv_in"), sem("att_bias_in")
        kc_in, vc_in = sem("att_kcache_in"), sem("att_vcache_in")
        masked = sem("att_bias_masked")
        paced = sem("att_paced")
        q_scaled, rows_done, qz_done = sem("att_q_scaled"), sem("att_rows"), sem("att_qz")
        turn_filled = sem("att_turn_filled")
        taken = [sem(f"att_turn_taken{i}") for i in range(2)]
        s_filled, biased = sem("att_scores_filled"), sem("att_biased")
        exped, inverse, scaled = sem("att_exp"), sem("att_inverse"), sem("att_probs")
        o_filled, o_taken = sem("att_out_filled"), sem("att_out_taken")
        cached = sem("att_cache_out")
        with ExitStack() as ctx:
            def sb(name, shape, dt=F32):
                return ctx.enter_context(nc.sbuf_tensor(f"att_{name}", shape, dt))

            def pb(name, shape):
                return ctx.enter_context(nc.psum_tensor(f"att_{name}", shape, F32))

            qf, kf, vf = sb("q", [P, TOK]), sb("k", [P, 2, TOK]), sb("v", [P, TOK])
            qs = sb("q_scaled", [P, 2, TOK])
            vr, kr = sb("v_rows", [P, 2, NT, P]), sb("k_rows", [P, KEPT, P])
            probs = sb("probs", [P, 3, WIDE])
            pt = sb("p_turned", [P, 2, WIDE])
            top, total = sb("top", [P, 3]), sb("total", [P, 3])
            rec = sb("rec", [P, 3])
            bias = sb("bias", [P, 2, 2, WIDE])
            bias_s = sb("bias_s", [P, 2, GROUPS, SW])
            own = sb("own", [P, 2, DEC_S])
            kc = sb("k_cache", [P, GB, KT_S, P])
            vc = sb("v_cache", [P, GROUPS, GB, KT_S, P])
            kt = sb("k_turned", [P, GROUPS, GB, PAST])
            qz = sb("q_sample", [P, GROUPS, GB, P])
            sps = pb("score_ps", [P, 2, 2 * BANK])
            tps = pb("turn_ps", [P, 2, BANK])
            ops = pb("out_ps", [P, 2, BANK])
            block = ctx.enter_context(nc.Block())

            def skewed(h, head, rows, first, cols, copies=None):
                ap = [[STRIP - 1, rows], [1, cols]]
                if copies:
                    ap = [[0, copies]] + ap
                base = S.strips[bass.ds(h * 2 + head, 1), 0, first:first + 1]
                return bass.AP(tensor=base.tensor, offset=base.offset, ap=ap)

            @block.sync
            def _(sp):
                def load_qkv(h, b):
                    for n, dst in enumerate((qf[:], kf[:, b, :], vf[:])):
                        sp.dma_start(dst, S.qkv_rows[bass.ds(h * P + n * D, P), :]).then_inc(qkv_in, 16)

                def load_bias(h, b):
                    zero = STRIP_C + CLIP
                    for head in range(2):
                        sp.dma_start(bias[:, b, head, :], skewed(h, head, P, zero - (WIDE - P), WIDE)).then_inc(bias_in, 16)
                        half = slice(head * CHUNK, (head + 1) * CHUNK)
                        for g in range(GROUPS):
                            sp.dma_start(bias_s[half, b, g, :PAST],
                                         skewed(h, head, DEC_S, zero - PAST, PAST, GB)).then_inc(bias_in, 16)
                        sp.dma_start(own[half, b, :], skewed(h, head, DEC_S, zero, DEC_S, GB)).then_inc(bias_in, 16)

                def load_cache(h, g, name, dst, signal):
                    for b in range(GB):
                        src = a[name][g * GB + b].rearrange("(t p) h d -> p t (h d)", p=P)
                        sp.dma_start(dst[:, b], src[:, :, bass.ds(h * P, P)]).then_inc(signal, 16)

                load_qkv(0, 0)
                load_bias(0, 0)
                load_cache(0, 0, "cache_k", kc, kc_in)
                for g in range(GROUPS):
                    load_cache(0, g, "cache_v", vc[:, g], vc_in)

                def keep_rows(stream):
                    for nm in "kv":
                        old, new = (a[n].rearrange("b s h d -> b (s h d)")[bass.ds(stream, 1)]
                                    for n in (f"cache_{nm}", f"cache_{nm}_sample"))
                        sp.dma_start(new[:, :(PAST - DEC_S) * D], old[:, DEC_S * D:]).then_inc(S.caches_kept, 16)

                assert PAIRS == DEC_B

                def pair(h, b, last):
                    if not last:
                        sp.wait_ge(q_scaled, h + 1)
                        sp.sem_inc(paced, 1)
                        sp.wait_ge(rows_done, h + 1)
                        sp.sem_inc(paced, 1)
                        sp.wait_ge(biased, h * ALLU + 2)
                        sp.sem_inc(paced, 1)
                        load_qkv(h + 1, 1 - b)
                    sp.wait_ge(turn_filled, fill(h, "keys", 0, 1)[2] + 1)
                    sp.sem_inc(paced, 1)
                    load_cache(h, 1, "cache_k", kc, kc_in)
                    if not (isinstance(h, int) and h == 0):
                        sp.wait_ge(o_filled, h * ALLU + 1)
                        sp.sem_inc(paced, 1)
                        for g in range(GROUPS):
                            load_cache(h, g, "cache_v", vc[:, g], vc_in)
                    if not last:
                        sp.wait_ge(masked, h * (2 + GROUPS) + (2 + GROUPS))
                        sp.sem_inc(paced, 1)
                        load_bias(h + 1, 1 - b)
                        sp.wait_ge(turn_filled, fill(h, "keys", 1, 1)[2] + 1)
                        sp.sem_inc(paced, 1)
                        load_cache(h + 1, 0, "cache_k", kc, kc_in)
                    keep_rows(h)

                pairs(sp, pair)

            @block.gpsimd
            def _(pool):
                MASKS = 2 + GROUPS
                for i in range(2):
                    pool.sem_inc(taken[i], 1)
                pool.memset(qz[:], 0.0).then_inc(qz_done, 1)

                def mask_bias(h, b):
                    pool.wait_ge(bias_in, h * 128 + 128)
                    pool.sem_inc(paced, 1)
                    pool.memset(bias[:CHUNK, b, :, WIDE - CHUNK:], MASKED).then_inc(masked, 1)
                    pool.wait_ge(masked, h * MASKS + 1)
                    pool.sem_inc(paced, 1)
                    pool.memset(bias[CHUNK:, b, :, :CHUNK], MASKED).then_inc(masked, 1)
                    pool.wait_ge(masked, h * MASKS + 2)
                    mask = S.own_mask[:].rearrange("p g (b s) -> p g b s", s=DEC_S)
                    for g in range(GROUPS):
                        pool.tensor_tensor(bias_s[:, b, g, PAST:].rearrange("p (b s) -> p b s", s=DEC_S),
                                           own[:, b, :].unsqueeze(1).to_broadcast([P, DEC_B, DEC_S]), mask[:, g],
                                           ALU.add).then_inc(masked, 1)

                mask_bias(0, 0)

                def pair(h, b, last):
                    pool.wait_ge(s_filled, h * ALLU + 1)
                    pool.sem_inc(paced, 1)
                    pool.wait_ge(q_scaled, h + 1)
                    pool.sem_inc(paced, 1)
                    n = 0
                    for g in range(GROUPS):
                        for head in range(2):
                            f = slice(head * DH, (head + 1) * DH)
                            dst = qz[f, g].rearrange("p b c -> p (b c)")
                            dst = bass.AP(tensor=dst.tensor, offset=dst.offset + head * DH,
                                          ap=[dst.ap[0], [P + DEC_S, GB], [1, DEC_S]])
                            src = qs[f, b, SEQ + g * GB * DEC_S:SEQ + (g + 1) * GB * DEC_S]
                            pool.wait_ge(qz_done, h * (2 * GROUPS) + (n + 1))
                            pool.sem_inc(paced, 1)
                            pool.tensor_copy(dst, src.rearrange("p (b s) -> p b s", s=DEC_S)).then_inc(qz_done, 1)
                            n += 1
                    if not last:
                        mask_bias(h + 1, 1 - b)

                pairs(pool, pair)

            @block.tensor
            def _(pe):
                def bank(at):
                    pe.wait_ge(taken[at[0]], at[1] + 1)
                    return tps[:, at[0], :]

                def is_taken(at):
                    pe.wait_ge(taken[at[0]], at[1] + 2)

                def prepare(h, b, n):
                    if n == 0:
                        pe.wait_ge(qkv_in, 48 if h is None else h * 48 + 96)
                    k = kf[:, b, :]
                    src = [(vf, i) for i in range(NTP)] + [(k, NT - KEPT + i) for i in range(KEPT)] + [(vf, NTP)]
                    dst = bank(prep_fill(h, n))
                    for i, (t, c) in enumerate(src[4 * n:4 * n + 4]):
                        m = pe.transpose(dst[:, i * P:(i + 1) * P], t[:, c * P:(c + 1) * P], S.ident[:])
                    m.then_inc(turn_filled, 1)

                def scores(h, b, u):
                    pe.wait_ge(biased, h * ALLU + (u + 1))
                    if u < UNITS:
                        j, head = divmod(u, 2)
                        f = slice(head * DH, (head + 1) * DH)
                        w = width(u)
                        first = j * P + P - w
                        for c in range(0, w, BANK):
                            n = min(BANK, w - c)
                            m = pe.matmul(sps[:, u % 2, c:c + n], qs[f, b, j * P:(j + 1) * P],
                                          kf[f, b, first + c:first + c + n])
                    else:
                        g = u - UNITS
                        pe.wait_ge(qz_done, h * (2 * GROUPS) + (2 * g + 3))
                        for m in range(2):
                            is_taken(fill(h, "keys", g, m))
                        for c, w, src in ((0, PAST, kt), (PAST, P, None)):
                            for s in range(GB):
                                rhs = kf[:, b, SEQ:] if src is None else kt[:, g, s, :]
                                m = pe.matmul(sps[:, u % 2, c:c + w], qz[:, g, s, :], rhs, start=s == 0, stop=s == GB - 1)
                    m.then_inc(s_filled, 1)

                def turn_keys(h, g):
                    pe.wait_ge(kc_in, h * (GROUPS * GB * 16) + (g + 1) * GB * 16)
                    for n in range(2):
                        dst = bank(fill(h, "keys", g, n))
                        for i in range(4):
                            m = pe.transpose(dst[:, i * P:(i + 1) * P], kc[:, 2 * n + i // 2, i % 2, :], S.ident[:])
                        m.then_inc(turn_filled, 1)

                def turn_probs(h, v):
                    pe.wait_ge(scaled, h * ALLU + (v + 1))
                    for n, (lo, hi) in enumerate(parts(v)):
                        dst = bank(fill(h, "probs", v, n))
                        for c in range(lo, hi, P):
                            m = pe.transpose(dst[:, c - lo:c - lo + P], probs[:, v % 3, c:c + P], S.ident[:])
                        m.then_inc(turn_filled, 1)

                def out(h, b, v):
                    pe.wait_ge(o_taken, h * ALLU + (v + 1))
                    dst = ops[:, v % 2, :P]
                    for n in range(len(parts(v))):
                        is_taken(fill(h, "probs", v, n))
                    if v < UNITS:
                        tiles = width(v) // P
                        for n in range(tiles):
                            i, c = v // 2 + 1 - tiles + n, slice(n * P, (n + 1) * P)
                            m = pe.matmul(dst, vr[:, b, i, :], pt[:, v % 2, c], start=n == 0, stop=n == tiles - 1)
                    else:
                        g = v - UNITS
                        pe.wait_ge(vc_in, h * (GROUPS * GB * 16) + GROUPS * GB * 16)
                        turned = lambda t: pt[:, v % 2, t * P:(t + 1) * P]
                        pe.matmul(dst, vr[:, b, NTP, :], turned(KT_S), start=True, stop=False)
                        for s in range(GB):
                            pick = lambda ap: ap.rearrange("p (h b q) -> p h b q", b=GB, q=DEC_S)[:, :, s, :]
                            for t in range(KT_S):
                                m = pe.matmul(pick(dst), vc[:, g, s, t, :], pick(turned(t)), start=False,
                                              stop=s == GB - 1 and t == KT_S - 1)
                    m.then_inc(o_filled, 1)

                for n in range(PREPS):
                    prepare(None, 0, n)

                def pair(h, b, last):
                    pe.wait_ge(q_scaled, h + 1)
                    pe.wait_ge(rows_done, h + 1)
                    for u in range(ALLU + 3 if last else ALLU):
                        if u < ALLU:
                            scores(h, b, u)
                        if not last and AT_FILL <= u < AT_FILL + PREPS:
                            prepare(h, 1 - b, u - AT_FILL)
                        if u in AT_KEYS:
                            turn_keys(h, AT_KEYS.index(u))
                        at, v = back(h, u, 2)
                        if v is not None:
                            turn_probs(at, v)
                        at, v = back(h, u, 3)
                        if v is not None:
                            out(at, b if v == u - 3 else 1 - b, v)

                pairs(pe, pair)

            @block.scalar
            def _(act):
                def is_filled(at):
                    act.wait_ge(turn_filled, at[2] + 1)
                    return tps[:, at[0], :]

                def scale_q(h, b):
                    act.wait_ge(qkv_in, h * 48 + 48)
                    act.activation(qs[:, b, :], qf[:], ACT.Copy, scale=-DH ** -0.5).then_inc(q_scaled, 1)

                def take(h, b, n, pair):
                    at = prep_fill(h, n)
                    src = is_filled(at)
                    if h is not None and n == 0:
                        act.wait_ge(cached, h * 64 + 64)
                    if n < 2:
                        act.copy(vr[:, b, 4 * n:4 * n + 4, :].rearrange("p i d -> p (i d)"), src).then_inc(taken[at[0]], 1)
                    elif n == 2:
                        act.copy(kr[:, :KEPT - 1, :].rearrange("p i d -> p (i d)"), src).then_inc(taken[at[0]], 1)
                    else:
                        act.copy(kr[:, KEPT - 1, :], src[:, :P])
                        act.copy(vr[:, b, NTP, :], src[:, P:2 * P]).then_inc(taken[at[0]], 1)
                        for m in range(2):
                            act.wait_ge(taken[m], prep_fill(h, 2 + m)[1] + 2)
                        act.sem_inc(rows_done, 1)
                        feats = bass.ds(pair * P, P)
                        for rows, nm in ((kr, "k"), (vr[:, b, NT - KEPT:], "v")):
                            act.dma_start(a[f"cache_{nm}_prompt"][0].rearrange("(i t) h d -> t i (h d)", t=P)[:, :, feats],
                                          rows[:, :KEPT - 1, :]).then_inc(cached, 16)
                            act.dma_start(a[f"cache_{nm}_sample"].rearrange("b s h d -> b s (h d)")[:, PAST - DEC_S:, feats],
                                          rows[:, KEPT - 1, :]).then_inc(cached, 16)

                def exponential(h, u):
                    w = width(u)
                    act.wait_ge(biased, h * ALLU + (u + 3))
                    act.activation(probs[:, u % 3, :w], probs[:, u % 3, :w], ACT.Exp, scale=-1.0,
                                   bias=top[:, u % 3:u % 3 + 1], accum_out=total[:, u % 3:u % 3 + 1]).then_inc(exped, 1)

                def take_probs(h, v):
                    at = fill(h, "probs", v, 0)
                    src = is_filled(at)
                    lo, hi = parts(v)[0]
                    act.copy(pt[:, v % 2, lo:hi], src[:, :hi - lo]).then_inc(taken[at[0]], 1)

                def take_out(h, v):
                    act.wait_ge(o_filled, h * ALLU + (v + 1))
                    flat = S.mixed[:].rearrange("p k t -> p (k t)")
                    if v < UNITS:
                        j, head = divmod(v, 2)
                        f = slice(head * DH, (head + 1) * DH)
                        act.copy(flat[f, bass.ds(h * TOK + j * P, P)], ops[f, v % 2, :P]).then_inc(o_taken, 1)
                    else:
                        g = v - UNITS
                        for head in range(2):
                            f = slice(head * DH, (head + 1) * DH)
                            m = act.copy(flat[f, bass.ds(h * TOK + (SEQ + g * GB * DEC_S), GB * DEC_S)],
                                         ops[f, v % 2, head * DH:(head + 1) * DH])
                        m.then_inc(o_taken, 1)

                scale_q(0, 0)
                for n in range(PREPS):
                    take(None, 0, n, 0)

                def pair(h, b, last):
                    for u in range(ALLU + 3 if last else ALLU):
                        if not last and u == AT_Q:
                            scale_q(h + 1, 1 - b)
                        if not last and AT_FILL <= u < AT_FILL + PREPS:
                            take(h, 1 - b, u - AT_FILL, h + 1)
                        if u in AT_KEYS:
                            g = AT_KEYS.index(u)
                            for n in range(2):
                                at = fill(h, "keys", g, n)
                                act.copy(kt[:, g, 2 * n:2 * n + 2, :].rearrange("p b t -> p (b t)"),
                                         is_filled(at)).then_inc(taken[at[0]], 1)
                        at, v = back(h, u, 2)
                        if v is not None:
                            take_probs(at, v)
                        if u < ALLU:
                            exponential(h, u)
                        at, v = back(h, u, 3)
                        if v is not None:
                            take_out(at, v)

                pairs(act, pair)
                act.wait_ge(cached, PAIRS * 64)

            @block.vector
            def _(dve):
                dve.sem_inc(biased, 2)
                dve.sem_inc(o_taken, 2)

                def add_bias(h, b, u):
                    w = width(u)
                    in1 = bias[:, b, u % 2, WIDE - w:] if u < UNITS else bias_s[:, b, u - UNITS, :]
                    dve.wait_ge(s_filled, h * ALLU + (u + 1))
                    at, v = back(h, u, 3)
                    if v is not None:
                        dve.wait_ge(turn_filled, fill(at, "probs", v, len(parts(v)) - 1)[2] + 1)
                    dve.sem_inc(paced, 1)
                    dve.tensor_tensor_reduce(probs[:, u % 3, :w], sps[:, u % 2, :w], in1, 1.0, 3e38, ALU.add,
                                             ALU.min, top[:, u % 3:u % 3 + 1]).then_inc(biased, 1)

                def normalise(h, v):
                    w, s = width(v), slice(v % 3, v % 3 + 1)
                    dve.wait_ge(exped, h * ALLU + (v + 1))
                    dve.reciprocal(rec[:, s], total[:, s]).then_inc(inverse, 1)
                    dve.wait_ge(inverse, h * ALLU + (v + 1))
                    dve.tensor_scalar(probs[:, v % 3, :w], probs[:, v % 3, :w], rec[:, s], None,
                                      ALU.mult).then_inc(scaled, 1)

                def take_probs(h, v):
                    if len(parts(v)) == 2:
                        at = fill(h, "probs", v, 1)
                        lo, hi = parts(v)[1]
                        dve.wait_ge(turn_filled, at[2] + 1)
                        dve.wait_ge(o_filled, h * ALLU + (v - 1))
                        dve.tensor_copy(pt[:, v % 2, lo:hi], tps[:, at[0], :hi - lo]).then_inc(taken[at[0]], 1)

                def pair(h, b, last):
                    dve.wait_ge(masked, h * (2 + GROUPS) + (2 + GROUPS))
                    for u in range(ALLU + 3 if last else ALLU):
                        if u < ALLU:
                            add_bias(h, b, u)
                        at, v = back(h, u, 1)
                        if v is not None:
                            normalise(at, v)
                        at, v = back(h, u, 2)
                        if v is not None:
                            take_probs(at, v)

                pairs(dve, pair)


def build(nc, a):
    with ExitStack() as ctx:
        def sb(name, shape, dt=F32):
            return ctx.enter_context(nc.sbuf_tensor(name, shape, dt))

        def dram(name, shape):
            return nc.dram_tensor(name, shape, F32, kind="Internal").ap()

        S = Shared()
        S.res = sb("res", [P, DK, TOK])
        S.ident, S.ones, S.eps = sb("ident", [P, P]), sb("ones", [P, P]), sb("eps", [P, 1])
        S.causal, S.stream, S.own_mask = sb("causal", [P, 2, P]), sb("stream", [P, DEC_B]), sb("own_mask", [P, 2, P])
        S.gains = sb("gains", [P, 6, DK])
        S.gla_rows, S.qkv_rows = dram("gla_rows", [GLA_IN, TOK]), dram("qkv_rows", [3 * D, TOK])
        S.strips = dram("strips", [HEADS, P, STRIP])
        S.caches_kept = nc.alloc_semaphore("caches_kept")
        w_in = a["gla_w_in"][0]
        body = 2 * NQK + 2 * NV
        constants(nc, S, a)
        load_tokens(nc, S, a)
        with ExitStack() as phase:
            operands(nc, S, phase, "in")
            project(nc, S, "in", G_MIX0, [(w_in, 0, body // P, None, S.gla_rows, 0, 0),
                                          (w_in, GLA_IN - P, 1, None, S.gla_rows, body, P - RANK)])
        with nc.sbuf_tensor("gla_mixed", [P, DK, TOK], F32) as S.mixed:
            gla_core(nc, S, a)
            add_product(nc, S, "go", a["gla_w_out"][0])
        with ExitStack() as phase:
            operands(nc, S, phase, "f0")
            ffn(nc, S, "f0", G_FFN0, a["ffn_w_gate"][0], a["ffn_w_up"][0], a["ffn_w_down"][0])
            project(nc, S, "qkv", None, [(a["attn_w_q"][0], 0, DK, G_MIX1, S.qkv_rows, 0, 0),
                                         (a["w_kv"], 0, 2 * DK, G_KV, S.qkv_rows, D, 0)])
        with nc.sbuf_tensor("att_mixed", [P, DK, TOK], F32) as S.mixed:
            attention_core(nc, S, a)
            add_product(nc, S, "ao", a["attn_w_out"][0])
        with ExitStack() as phase:
            operands(nc, S, phase, "f1")
            ffn(nc, S, "f1", G_FFN1, a["ffn_w_gate"][1], a["ffn_w_up"][1], a["ffn_w_down"][1])
        store_tokens(nc, S, a)


_INS = ["x_prompt", "x_sample", "state_gla", "cache_k", "cache_v", "norm_mix", "norm_ffn", "norm_final",
        "gla_w_in", "gla_w_gate2", "gla_b_gate", "gla_norm", "gla_w_out", "kv_norm", "w_kv", "attn_w_q",
        "attn_rel_bias", "attn_w_out", "ffn_w_gate", "ffn_w_up", "ffn_w_down"]
_OUTS = [("y_prompt", (1, SEQ, D)), ("y_sample", (DEC_B, DEC_S, D)),
         ("state_gla_prompt", (1, 1, GLA_H, GLA_DK, GLA_DV)),
         ("cache_k_prompt", (1, 512, HEADS, DH)), ("cache_v_prompt", (1, 512, HEADS, DH)),
         ("state_gla_sample", (1, DEC_B, GLA_H, GLA_DK, GLA_DV)),
         ("cache_k_sample", (DEC_B, PAST, HEADS, DH)), ("cache_v_sample", (DEC_B, PAST, HEADS, DH))]


def kernel(**inputs):
    import numpy as _np
    import concourse.bacc as _bacc
    from concourse.bass_utils import run_bass_kernel_spmd as _run

    nc = _bacc.Bacc("TRN2", target_bir_lowering=False, num_devices=1)
    arrays, args = {}, {}
    for name in _INS:
        arrays[f"in_{name}"] = _np.ascontiguousarray(inputs[name])
        args[name] = nc.dram_tensor(f"in_{name}", arrays[f"in_{name}"].shape, F32, kind="ExternalInput").ap()
    for name, shape in _OUTS:
        args[name] = nc.dram_tensor(f"out_{name}", shape, F32, kind="ExternalOutput").ap()
    build(nc, args)
    r = _run(nc, [arrays], core_ids=[0])
    return tuple(r.results[0][f"out_{name}"] for name, _ in _OUTS)
```

```python
from contextlib import ExitStack, contextmanager

import concourse.bass as bass
from concourse import mybir

F32 = mybir.dt.float32
F32R = mybir.dt.float32r
I32 = mybir.dt.int32
ALU = mybir.AluOpType
ACT = mybir.ActivationFunctionType

P = 128
D = 1024
DK = D // P
SEQ = 1024
DEC_B, DEC_S = 8, 16
DEC = DEC_B * DEC_S
TOK = SEQ + DEC
NT = TOK // P
GRP = 384
NG = TOK // GRP
EPS = 1e-6
GLA_H, GLA_DK, GLA_DV, GLA_BLOCK, GLA_TAU, RANK = 4, 128, 256, 64, 16.0, 16
NQK, NV = GLA_H * GLA_DK, GLA_H * GLA_DV
GLA_IN = 2 * NQK + 2 * NV + RANK
HEADS, DH = 16, 64
PAIRS = HEADS // 2
PAST = 256
CHUNK = 64
BAND_T = 5
CLIP = 128
D_FF = 2816
MASKED = 1e30
STRIP_C = (BAND_T - 1) * P - 1
STRIP = STRIP_C + 2 * CLIP + 1

G_MIX0, G_MIX1, G_FFN0, G_FFN1, G_FINAL, G_KV = range(6)


class Ring:

    def __init__(self, slots, stages):
        self.slots, self.stages = slots, stages


class Segment:

    def __init__(self, w, col, units, gain, out, row, skip, base, slots):
        self.w, self.col, self.gain, self.out, self.row, self.skip = (
            w.rearrange("(k p) n -> p k n", p=P), col, gain, out, row, skip)
        self.per = min(slots, units)
        self.trips = units // self.per
        self.base, self.turn = base, base // slots
        assert base % slots == 0 and units % self.per == 0


class Shared:
    pass


def operands(nc, S, ctx, tag):
    S.x_hi = ctx.enter_context(nc.sbuf_tensor(f"{tag}_x_hi", [P, DK, TOK], F32R))
    S.x_lo = ctx.enter_context(nc.sbuf_tensor(f"{tag}_x_lo", [P, DK, TOK], F32R))


def f32(ap):
    return ap.bitcast(F32)


@contextmanager
def semaphores(nc):
    made = []

    def sem(name):
        made.append(nc.alloc_semaphore(name))
        return made[-1]

    yield sem
    nc.clear_and_free_semaphores(made)
    nc.all_engine_barrier()


def weight_ring(nc, sem, ctx, tag, slots, stages):
    r = Ring(slots, stages)
    r.stage = ctx.enter_context(nc.sbuf_tensor(f"{tag}_stage", [P, stages, D], F32))
    r.hi = ctx.enter_context(nc.sbuf_tensor(f"{tag}_w_hi", [P, slots, D], F32R))
    r.lo = ctx.enter_context(nc.sbuf_tensor(f"{tag}_w_lo", [P, slots, D], F32R))
    r.loaded = [sem(f"{tag}_w_loaded{i}") for i in range(stages)]
    r.scaled = sem(f"{tag}_w_scaled")
    r.rounded = sem(f"{tag}_w_rounded")
    r.split = sem(f"{tag}_w_split")
    return r


def fetch_unit(sp, r, unit, j, src):
    sp.wait_ge(r.split, unit + 1)
    sp.dma_start(r.stage[:, j % r.stages, :].rearrange("p (k n) -> p k n", n=src.shape[-1]) if len(src.shape) == 3
                 else r.stage[:, j % r.stages, :], src).then_inc(r.loaded[j % r.stages], 16)


def scale_unit(pool, r, unit, j, times, gain):
    pool.wait_ge(r.loaded[j % r.stages], 16 * (times + 1))
    st = r.stage[:, j % r.stages, :].rearrange("p (k n) -> p k n", n=P)
    pool.tensor_tensor(st, st, gain.unsqueeze(2).to_broadcast([P, DK, P]), ALU.mult).then_inc(r.scaled, 1)


def round_unit(act, r, unit, j, times, gain=None):
    if gain is None:
        act.wait_ge(r.loaded[j % r.stages], 16 * (times + 1))
    else:
        act.wait_ge(r.scaled, unit + 1)
    act.copy(r.hi[:, j % r.slots, :], r.stage[:, j % r.stages, :]).then_inc(r.rounded, 1)


def split_unit(pool, r, unit, j):
    pool.wait_ge(r.rounded, unit + 1)
    pool.tensor_tensor(r.lo[:, j % r.slots, :], r.stage[:, j % r.stages, :], f32(r.hi[:, j % r.slots, :]),
                       ALU.subtract).then_inc(r.split, 1)


def product(pe, out, w_hi, w_lo, x_hi, x_lo, first, last):
    pe.matmul(out, w_hi, x_hi, start=first, stop=False)
    pe.matmul(out, w_lo, x_hi, start=False, stop=False)
    return pe.matmul(out, w_hi, x_lo, start=False, stop=last)


def constants(nc, S, a):
    with semaphores(nc) as sem:
        gains_in, made, strip_in, strip_made = (sem(n) for n in ("gains_in", "consts_made", "strip_in", "strip_made"))
        with ExitStack() as ctx:
            table = ctx.enter_context(nc.sbuf_tensor("bias_table", [HEADS, 2 * CLIP + 1], F32))
            strip = S.strip
            block = ctx.enter_context(nc.Block())

            @block.sync
            def _(sp):
                rows = [a["norm_mix"][0], a["norm_mix"][1], a["norm_ffn"][0], a["norm_ffn"][1],
                        a["norm_final"], a["kv_norm"]]
                sp.dma_start(table[:], a["attn_rel_bias"][0]).then_inc(strip_in, 16)
                for i, row in enumerate(rows):
                    sp.dma_start(S.gains[:, i, :], row.rearrange("(k p) -> p k", p=P),
                                 allow_slow_non_contiguous=True).then_inc(gains_in, 16)
                sp.wait_ge(strip_made, 2)
                sp.wait_ge(gains_in, 16 * len(rows))

            @block.vector
            def _(dve):
                dve.wait_ge(strip_in, 16)
                dve.tensor_scalar(strip[:, STRIP_C:], table[:, ::-1], -1.0, None, ALU.mult).then_inc(strip_made, 1)
                dve.tensor_scalar(strip[:, :STRIP_C], table[:, 2 * CLIP:].to_broadcast([HEADS, STRIP_C]), -1.0, None,
                                  ALU.mult).then_inc(strip_made, 1)

            @block.gpsimd
            def _(pool):
                n = [0]

                def step(ins):
                    n[0] += 1
                    ins.then_inc(made, 1)
                    pool.wait_ge(made, n[0])

                step(pool.memset(S.ident[:], 0.0))
                step(pool.affine_select(S.ident[:], S.ident[:], [[-1, P]], ALU.not_equal, 1.0, base=0,
                                        channel_multiplier=1))
                step(pool.memset(S.ones[:], 1.0))
                step(pool.memset(S.eps[:], EPS))
                step(pool.memset(S.causal[:], 1.0))
                step(pool.affine_select(S.causal[:, 0, :], S.causal[:, 0, :], [[1, P]], ALU.is_ge, 0.0, base=0,
                                        channel_multiplier=-1))
                step(pool.memset(S.causal[0:GLA_BLOCK, 0, GLA_BLOCK:], 0.0))
                step(pool.affine_select(S.causal[:, 1, :], S.causal[:, 1, :], [[1, P]], ALU.is_ge, 0.0, base=0,
                                        channel_multiplier=-1))
                view = S.causal[:, 1, :].rearrange("p (b s) -> p b s", s=DEC_S)
                step(pool.affine_select(view, view, [[-DEC_S, DEC_B], [0, DEC_S]], ALU.is_ge, 0.0, base=0,
                                        channel_multiplier=1))
                step(pool.memset(S.own_mask[:], 0.0))
                half = DEC_B // 2
                for head in range(2):
                    for g in range(2):
                        view = S.own_mask[head * DH:(head + 1) * DH, g, :].rearrange("p (b s) -> p b s", s=DEC_S)
                        for sign, base in ((1, half * DEC_S * g), (-1, DEC_S - 1 - half * DEC_S * g)):
                            step(pool.affine_select(view, view, [[-DEC_S * sign, DEC_B], [0, DEC_S]], ALU.is_ge, MASKED,
                                                    base=base, channel_multiplier=sign))
                step(pool.memset(S.stream[:], 1.0))
                step(pool.affine_select(S.stream[:], S.stream[:], [[-DEC_S, DEC_B]], ALU.is_ge, 0.0, base=0,
                                        channel_multiplier=1))
                step(pool.affine_select(S.stream[:], S.stream[:], [[DEC_S, DEC_B]], ALU.is_ge, 0.0,
                                        base=DEC_S - 1, channel_multiplier=-1))


def load_tokens(nc, S, a):
    with semaphores(nc) as sem:
        x_in = [sem(f"x_in{i}") for i in range(NT)]
        turned, taken = sem("x_turned"), sem("x_taken")
        with ExitStack() as ctx:
            xt = ctx.enter_context(nc.sbuf_tensor("x_rows", [P, NT, D], F32))
            ps = ctx.enter_context(nc.psum_tensor("x_ps", [P, 2, D], F32))
            block = ctx.enter_context(nc.Block())
            rows = [a["x_prompt"][0, i * P:(i + 1) * P, :] for i in range(NT - 1)]
            rows.append(a["x_sample"].rearrange("b s d -> (b s) d"))

            @block.sync
            def _(sp):
                for i in range(NT):
                    sp.dma_start(xt[:, i, :], rows[i]).then_inc(x_in[i], 16)

            @block.tensor
            def _(pe):
                for i in range(NT):
                    pe.wait_ge(x_in[i], 16)
                    if i >= 2:
                        pe.wait_ge(taken, i - 1)
                    for k in range(DK):
                        t = pe.transpose(ps[:, i % 2, k * P:(k + 1) * P], xt[:, i, k * P:(k + 1) * P], S.ident[:])
                    t.then_inc(turned, 1)

            @block.vector
            def _(dve):
                for i in range(NT):
                    dve.wait_ge(turned, i + 1)
                    dve.tensor_copy(S.res[:, :, i * P:(i + 1) * P],
                                    ps[:, i % 2, :].rearrange("p (k t) -> p k t", t=P)).then_inc(taken, 1)


class Norm:
    BUFS = 4

    def __init__(self, nc, S, sem, ctx, tag, gain, sums, spread, final=False):
        self.S, self.gain, self.sums, self.spread, self.final = S, gain, sums, spread, final
        self.squared, self.paired, self.added = sem(f"{tag}_squared"), sem(f"{tag}_paired"), sem(f"{tag}_added")
        self.summed, self.rooted, self.inverse = sem(f"{tag}_summed"), sem(f"{tag}_rooted"), sem(f"{tag}_inverse")
        self.diagonal, self.spread_out = sem(f"{tag}_diagonal"), sem(f"{tag}_spread")
        self.normed, self.rounded = sem(f"{tag}_normed"), sem(f"{tag}_rounded")
        self.low = [sem(f"{tag}_low{i}") for i in range(2)]
        self.work = ctx.enter_context(nc.sbuf_tensor(f"{tag}_work", [P, self.BUFS, GRP], F32))
        self.acc = ctx.enter_context(nc.sbuf_tensor(f"{tag}_acc", [P, NG, GRP], F32))
        self.rms = ctx.enter_context(nc.sbuf_tensor(f"{tag}_rms", [P, NT], F32))

    def chunk(self, tensor, c):
        t, k = divmod(c, DK)
        return tensor[:, k, t * GRP:(t + 1) * GRP]

    def splitter(self, c):
        by = [0 if i % DK % 3 == 0 else 1 for i in range(c + 1)]
        return by[c], by[:c].count(by[c])

    def scalar(self, act):
        self.squares(act)
        self.root(act)

    def squares(self, act):
        for q in range(NG * DK // 2):
            t, i = divmod(q, DK // 2)
            if q >= 2:
                act.wait_ge(self.added, q - 1)
            act.activation(self.work[:, q % 2 * 2:q % 2 * 2 + 2, :], self.S.res[:, 2 * i:2 * i + 2, t * GRP:(t + 1) * GRP],
                           ACT.Square).then_inc(self.squared, 1)

    def root(self, act):
        act.wait_ge(self.summed, NG)
        act.activation(self.rms[:], self.sums[:, :NT], ACT.Sqrt, bias=self.S.eps[:], scale=1.0 / D).then_inc(self.rooted, 1)

    def round(self, act):
        for c in range(NG * DK):
            act.wait_ge(self.normed, c + 1)
            act.copy(self.chunk(self.S.x_hi, c), self.work[:, c % self.BUFS, :]).then_inc(self.rounded, 1)

    def tensor(self, pe):
        self.sum_all(pe)
        self.spread_all(pe)

    def sum_all(self, pe):
        for t in range(NG):
            pe.wait_ge(self.added, (t + 1) * DK // 2)
            for i in range(NG):
                tile = t * NG + i
                m = pe.matmul(self.sums[:, tile:tile + 1], self.acc[:, t, i * P:(i + 1) * P], self.S.ones[:, :1])
            m.then_inc(self.summed, 1)

    def spread_all(self, pe):
        for t in range(NG):
            pe.wait_ge(self.diagonal, t + 1)
            pe.matmul(self.spread[t], self.S.ones[:], self.acc[:, t, :]).then_inc(self.spread_out, 1)

    def vector(self, dve):
        self.statistics(dve)
        self.normalise(dve)

    def statistics(self, dve):
        for q in range(NG * DK // 2):
            t, i = divmod(q, DK // 2)
            a, b = self.work[:, q % 2 * 2, :], self.work[:, q % 2 * 2 + 1, :]
            dve.wait_ge(self.squared, q + 1)
            if i == 0:
                dve.tensor_tensor(self.acc[:, t, :], a, b, ALU.add).then_inc(self.added, 1)
                continue
            dve.tensor_tensor(a, a, b, ALU.add).then_inc(self.paired, 1)
            dve.wait_ge(self.paired, t * (DK // 2 - 1) + i)
            dve.wait_ge(self.added, q)
            dve.tensor_tensor(self.acc[:, t, :], self.acc[:, t, :], a, ALU.add).then_inc(self.added, 1)
        dve.wait_ge(self.rooted, 1)
        dve.reciprocal(self.rms[:], self.rms[:]).then_inc(self.inverse, 1)
        dve.wait_ge(self.inverse, 1)
        for t in range(NG):
            dve.tensor_tensor(self.acc[:, t, :].rearrange("p (i c) -> p i c", c=P),
                              self.S.ident[:].unsqueeze(1).to_broadcast([P, NG, P]),
                              self.rms[:, t * NG:(t + 1) * NG].unsqueeze(2).to_broadcast([P, NG, P]),
                              ALU.mult).then_inc(self.diagonal, 1)

    def normalise(self, dve):
        for c in range(NG * DK + 2):
            if c < NG * DK:
                t, k = divmod(c, DK)
                if k == 0:
                    dve.wait_ge(self.spread_out, t + 1)
                if not self.final and c >= self.BUFS:
                    by, done = self.splitter(c - self.BUFS)
                    dve.wait_ge(self.low[by], done + 1)
                x = self.chunk(self.S.res, c)
                out = x if self.final else self.work[:, c % self.BUFS, :]
                if self.gain is None:
                    dve.tensor_tensor(out, x, self.spread[t], ALU.mult).then_inc(self.normed, 1)
                else:
                    dve.scalar_tensor_tensor(out, x, self.S.gains[:, self.gain, k:k + 1], self.spread[t], ALU.mult,
                                             ALU.mult).then_inc(self.normed, 1)
            if c >= 2 and not self.final and self.splitter(c - 2)[0] == 0:
                self.split(dve, c - 2)

    def split(self, engine, c):
        engine.wait_ge(self.rounded, c + 1)
        engine.tensor_tensor(self.chunk(self.S.x_lo, c), self.work[:, c % self.BUFS, :], f32(self.chunk(self.S.x_hi, c)),
                             ALU.subtract).then_inc(self.low[self.splitter(c)[0]], 1)

    def gpsimd(self, pool):
        for c in range(NG * DK):
            if self.splitter(c)[0] == 1:
                self.split(pool, c)

    def ready(self, pe, t):
        if self.final:
            pe.wait_ge(self.normed, (t + 1) * DK)
            return
        for by in range(2):
            pe.wait_ge(self.low[by], sum(self.splitter(c)[0] == by for c in range((t + 1) * DK)))


class LateNorm(Norm):

    def __init__(self, nc, S, sem, ctx, tag, gain, sums, spread):
        super().__init__(nc, S, sem, ctx, tag, gain, sums, [spread] * NG)
        self.kept = sem(f"{tag}_kept")

    def round(self, act, t):
        for c in range(t * DK, (t + 1) * DK):
            k = c % DK
            if self.gain is None:
                m = act.copy(self.chunk(self.S.x_hi, c), self.chunk(self.S.res, c))
            else:
                m = act.activation(self.chunk(self.S.x_hi, c), self.chunk(self.S.res, c), ACT.Copy,
                                   scale=self.S.gains[:, self.gain, k:k + 1])
            m.then_inc(self.rounded, 1)

    def split_all(self, dve):
        for c in range(NG * DK):
            k = c % DK
            dve.wait_ge(self.rounded, c + 1)
            x, hi, lo = (self.chunk(tensor, c) for tensor in (self.S.res, self.S.x_hi, self.S.x_lo))
            if self.gain is None:
                m = dve.tensor_tensor(lo, x, f32(hi), ALU.subtract)
            else:
                m = dve.scalar_tensor_tensor(lo, x, self.S.gains[:, self.gain, k:k + 1], f32(hi), ALU.mult, ALU.subtract)
            m.then_inc(self.low[0], 1)

    def keep(self, act):
        for t in range(NG):
            act.wait_ge(self.spread_out, t + 1)
            act.copy(self.work[:, t, :], self.spread[t]).then_inc(self.kept, 1)

    def spread_all(self, pe):
        for t in range(NG):
            pe.wait_ge(self.diagonal, t + 1)
            if t:
                pe.wait_ge(self.kept, t)
            pe.matmul(self.spread[t], self.S.ones[:], self.acc[:, t, :]).then_inc(self.spread_out, 1)

    def ready(self, pe, t):
        pe.wait_ge(self.low[0], (t + 1) * DK)


def keep_strips(sp, S):
    sp.dma_start(S.strips, S.strip[:].unsqueeze(1).to_broadcast([HEADS, P, STRIP])).then_inc(S.strips_kept, 16)


def project(nc, S, tag, gain, segments, aside=None):
    SL, BANKS = 4, 6
    with semaphores(nc) as sem:
        filled = sem(f"{tag}_filled")
        drained = sem(f"{tag}_drained")
        stored = [sem(f"{tag}_stored{i}") for i in range(SL)]
        with ExitStack() as ctx:
            ring = weight_ring(nc, sem, ctx, tag, SL, SL)
            rows = ctx.enter_context(nc.sbuf_tensor(f"{tag}_sums", [P, SL, TOK], F32))
            ps = ctx.enter_context(nc.psum_tensor(f"{tag}_ps", [P, BANKS, 512], F32))
            nps = ctx.enter_context(nc.psum_tensor(f"{tag}_norm_ps", [P, 2, 512], F32))
            norm = LateNorm(nc, S, sem, ctx, f"{tag}_norm", gain, nps[:, 0, :], nps[:, 1, :GRP])
            block = ctx.enter_context(nc.Block())
            plan, base = [], 0
            for w, col, units, gain, out, row, skip in segments:
                plan.append(Segment(w, col, units, gain, out, row, skip, base, SL))
                base += units
            assert all(s.per == SL for s in plan[:-1])

            @block.sync
            def _(sp):
                def fetch(s, it, j):
                    fetch_unit(sp, ring, it * s.per + (s.base + j), j, s.w[:, :, bass.ds(it * (s.per * P) + (s.col + j * P), P)])

                def store(s, it, j):
                    sp.wait_ge(drained, it * (s.per * NG) + (BANKS + (s.base + j + 1) * NG))
                    sp.dma_start(s.out[bass.ds(it * (s.per * P) + (s.row + j * P), P - s.skip), :],
                                 rows[s.skip:, j, :]).then_inc(stored[j], 16)

                last = None
                for s in plan:
                    for j in range(s.per):
                        if last:
                            store(last, last.trips - 1, j)
                        fetch(s, 0, j)
                    if aside and s is plan[0]:
                        aside(sp, S)
                    if last:
                        for j in range(s.per, last.per):
                            store(last, last.trips - 1, j)
                    if s.trips > 1:
                        with sp.Fori(1, s.trips) as it:
                            for j in range(s.per):
                                store(s, it - 1, j)
                                fetch(s, it, j)
                    last = s
                for j in range(last.per):
                    store(last, last.trips - 1, j)
                for j in range(SL):
                    sp.wait_ge(stored[j], 16 * (1 + sum(s.trips for s in plan if j < s.per)))

            BEFORE = 2

            @block.scalar
            def _(act):
                def units(s, it, first, last):
                    for j in range(first, last):
                        unit = it * s.per + (s.base + j)
                        act.wait_ge(filled, (unit + 1) * NG)
                        round_unit(act, ring, unit, j, it + s.turn, s.gain)

                norm.round(act, 0)
                units(plan[0], 0, 0, BEFORE)
                for t in range(1, NG):
                    norm.round(act, t)
                norm.squares(act)
                units(plan[0], 0, BEFORE, SL)
                norm.root(act)
                norm.keep(act)
                for s in plan:
                    with act.Fori(1 if s is plan[0] else 0, s.trips) as it:
                        units(s, it, 0, s.per)

            @block.gpsimd
            def _(pool):
                def units(s, it, first, last):
                    for j in range(first, last):
                        unit = it * s.per + (s.base + j)
                        if s.gain is not None:
                            scale_unit(pool, ring, unit, j, it + s.turn, S.gains[:, s.gain, :])
                        split_unit(pool, ring, unit, j)

                pool.sem_inc(ring.split, SL)
                units(plan[0], 0, 0, SL)
                for s in plan:
                    with pool.Fori(1 if s is plan[0] else 0, s.trips) as it:
                        units(s, it, 0, s.per)

            @block.tensor
            def _(pe):
                def unit(s, it, j):
                    pe.wait_ge(ring.split, it * s.per + (s.base + j + 1 + SL))
                    for t in range(NG):
                        g = j * NG + t
                        if isinstance(it, int) and s is plan[0] and j == 0:
                            norm.ready(pe, t)
                        pe.wait_ge(drained, it * (s.per * NG) + (s.base * NG + g + 1))
                        for k in range(DK):
                            w, x = slice(k * P, (k + 1) * P), slice(t * GRP, (t + 1) * GRP)
                            m = product(pe, ps[:, g % BANKS, :GRP], ring.hi[:, j, w], ring.lo[:, j, w],
                                        S.x_hi[:, k, x], S.x_lo[:, k, x], k == 0, k == DK - 1)
                        m.then_inc(filled, 1)
                        if isinstance(it, int) and s is plan[0] and j == 1:
                            if t == 1:
                                norm.sum_all(pe)
                            if t == NG - 1:
                                norm.spread_all(pe)

                pe.sem_inc(filled, SL * NG)
                for j in range(SL):
                    unit(plan[0], 0, j)
                for s in plan:
                    with pe.Fori(1 if s is plan[0] else 0, s.trips) as it:
                        for j in range(s.per):
                            unit(s, it, j)

            @block.vector
            def _(dve):
                dve.sem_inc(drained, BANKS)
                for j in range(SL):
                    dve.sem_inc(stored[j], 16)
                norm.split_all(dve)
                norm.statistics(dve)
                dve.wait_ge(norm.kept, NG)
                for s in plan:
                    with dve.Fori(0, s.trips) as it:
                        for j in range(s.per):
                            dve.wait_ge(stored[j], (it + s.turn + 1) * 16)
                            for t in range(NG):
                                g = j * NG + t
                                dve.wait_ge(filled, it * (s.per * NG) + (SL * NG + s.base * NG + g + 1))
                                dve.tensor_tensor(rows[:, j, t * GRP:(t + 1) * GRP], ps[:, g % BANKS, :GRP],
                                                  norm.work[:, t, :], ALU.mult).then_inc(drained, 1)


def add_product(nc, S, tag, w):
    SL, BANKS = 4, 6
    with semaphores(nc) as sem:
        filled = sem(f"{tag}_filled")
        drained = sem(f"{tag}_drained")
        rounded, low = sem(f"{tag}_rounded"), sem(f"{tag}_low")
        with ExitStack() as ctx:
            operands(nc, S, ctx, tag)
            ring = weight_ring(nc, sem, ctx, tag, SL, SL)
            ps = ctx.enter_context(nc.psum_tensor(f"{tag}_ps", [P, BANKS, 512], F32))
            block = ctx.enter_context(nc.Block())
            wv = w.rearrange("(k p) n -> p k n", p=P)
            trips = DK // SL

            @block.sync
            def _(sp):
                with sp.Fori(0, trips) as it:
                    for j in range(SL):
                        fetch_unit(sp, ring, it * SL + j, j, wv[:, :, bass.ds(it * (SL * P) + j * P, P)])

            @block.scalar
            def _(act):
                for t in range(NG):
                    cols = slice(t * GRP, (t + 1) * GRP)
                    act.copy(S.x_hi[:, :, cols], S.mixed[:, :, cols]).then_inc(rounded, 1)
                with act.Fori(0, trips) as it:
                    for j in range(SL):
                        act.wait_ge(filled, it * (SL * NG) + (j + 1) * NG)
                        round_unit(act, ring, it * SL + j, j, it)

            @block.gpsimd
            def _(pool):
                pool.sem_inc(ring.split, SL)
                with pool.Fori(0, trips) as it:
                    for j in range(SL):
                        split_unit(pool, ring, it * SL + j, j)

            @block.tensor
            def _(pe):
                pe.sem_inc(filled, SL * NG)
                with pe.Fori(0, trips) as it:
                    for j in range(SL):
                        pe.wait_ge(ring.split, it * SL + (j + 1 + SL))
                        for t in range(NG):
                            g = j * NG + t
                            if j == 0:
                                pe.wait_ge(low, t + 1)
                            pe.wait_ge(drained, it * (SL * NG) + (g + 1))
                            for k in range(DK):
                                c, x = slice(k * P, (k + 1) * P), slice(t * GRP, (t + 1) * GRP)
                                m = product(pe, ps[:, g % BANKS, :GRP], ring.hi[:, j, c], ring.lo[:, j, c],
                                            S.x_hi[:, k, x], S.x_lo[:, k, x], k == 0, k == DK - 1)
                            m.then_inc(filled, 1)

            @block.vector
            def _(dve):
                dve.sem_inc(drained, BANKS)
                for t in range(NG):
                    cols = slice(t * GRP, (t + 1) * GRP)
                    dve.wait_ge(rounded, t + 1)
                    dve.tensor_tensor(S.x_lo[:, :, cols], S.mixed[:, :, cols], f32(S.x_hi[:, :, cols]),
                                      ALU.subtract).then_inc(low, 1)
                res = S.res[:].rearrange("p k t -> p (k t)")
                with dve.Fori(0, trips) as it:
                    for j in range(SL):
                        for t in range(NG):
                            g = j * NG + t
                            dve.wait_ge(filled, it * (SL * NG) + (SL * NG + g + 1))
                            h = res[:, bass.ds(it * (SL * TOK) + (j * TOK + t * GRP), GRP)]
                            dve.tensor_tensor(h, h, ps[:, g % BANKS, :GRP], ALU.add).then_inc(drained, 1)


def ffn(nc, S, tag, gain, w_gate, w_up, w_down):
    HT, SL, ST, BANKS = 2, 6, 3, 4
    trips = D_FF // P // HT
    PAIRS_B = HT * NG
    DOWN_B = NG * DK
    with semaphores(nc) as sem:
        pair_filled = sem(f"{tag}_pair_filled")
        gated = sem(f"{tag}_gated")
        pair_drained = sem(f"{tag}_pair_drained")
        hid_rounded = sem(f"{tag}_hid_rounded")
        hid_split = sem(f"{tag}_hid_split")
        down_filled = sem(f"{tag}_down_filled")
        down_drained = sem(f"{tag}_down_drained")
        with ExitStack() as ctx:
            ring = weight_ring(nc, sem, ctx, tag, SL, ST)
            hid_hi = ctx.enter_context(nc.sbuf_tensor(f"{tag}_hid_hi", [P, HT, TOK], F32R))
            hid_lo = ctx.enter_context(nc.sbuf_tensor(f"{tag}_hid_lo", [P, HT, TOK], F32R))
            gate = ctx.enter_context(nc.sbuf_tensor(f"{tag}_gate", [P, 2, GRP], F32))
            hid = ctx.enter_context(nc.sbuf_tensor(f"{tag}_hid", [P, 2, GRP], F32))
            ps = ctx.enter_context(nc.psum_tensor(f"{tag}_pair_ps", [P, 2, 2, 512], F32))
            dps = ctx.enter_context(nc.psum_tensor(f"{tag}_down_ps", [P, BANKS, 512], F32))
            norm = Norm(nc, S, sem, ctx, f"{tag}_norm", gain, dps[:, 0, :], [dps[:, 1 + t, :GRP] for t in range(NG)])
            block = ctx.enter_context(nc.Block())
            columns = [w.rearrange("(k p) n -> p k n", p=P) for w in (w_gate, w_up)]

            @block.sync
            def _(sp):
                with sp.Fori(0, trips) as it:
                    for j in range(SL):
                        f = j // 2 if j < 2 * HT else j - 2 * HT
                        if j < 2 * HT:
                            src = columns[j % 2][:, :, bass.ds(it * (HT * P) + f * P, P)]
                        else:
                            src = w_down[bass.ds(it * (HT * P) + f * P, P), :]
                        fetch_unit(sp, ring, it * SL + j, j, src)

            @block.scalar
            def _(act):
                def gate_up(it, f):
                    for j in (2 * f, 2 * f + 1):
                        act.wait_ge(pair_filled, it * PAIRS_B + (f + 1) * NG)
                        round_unit(act, ring, it * SL + j, j, it * (SL // ST) + j // ST)

                def hidden(it):
                    for g in range(PAIRS_B):
                        f, t = divmod(g, NG)
                        act.wait_ge(pair_filled, it * PAIRS_B + (PAIRS_B + g + 1))
                        act.wait_ge(pair_drained, it * PAIRS_B + (g + 1))
                        act.activation(gate[:, g % 2, :], ps[:, g % 2, 0, :GRP], ACT.Silu).then_inc(gated, 1)
                        act.wait_ge(pair_drained, it * PAIRS_B + (g + 3))
                        act.wait_ge(down_filled, it * DOWN_B + (t + 1) * DK)
                        act.copy(hid_hi[:, f, t * GRP:(t + 1) * GRP], hid[:, g % 2, :]).then_inc(hid_rounded, 1)
                        if g == 0:
                            for j in range(2 * HT, SL):
                                act.wait_ge(down_filled, it * DOWN_B + DOWN_B)
                                round_unit(act, ring, it * SL + j, j, it * (SL // ST) + j // ST)

                norm.scalar(act)
                gate_up(0, 0)
                norm.round(act)
                for f in range(1, HT):
                    gate_up(0, f)
                hidden(0)
                with act.Fori(1, trips) as it:
                    for f in range(HT):
                        gate_up(it, f)
                    hidden(it)

            @block.gpsimd
            def _(pool):
                def hidden(it):
                    for g in range(PAIRS_B):
                        f, t = divmod(g, NG)
                        pool.wait_ge(hid_rounded, it * PAIRS_B + (g + 1))
                        cols = slice(t * GRP, (t + 1) * GRP)
                        pool.tensor_tensor(hid_lo[:, f, cols], hid[:, g % 2, :], f32(hid_hi[:, f, cols]),
                                           ALU.subtract).then_inc(hid_split, 1)
                        if g == 0:
                            for j in range(2 * HT, SL):
                                split_unit(pool, ring, it * SL + j, j)

                pool.sem_inc(ring.split, ST)
                for j in range(2):
                    split_unit(pool, ring, j, j)
                norm.gpsimd(pool)
                for j in range(2, 2 * HT):
                    split_unit(pool, ring, j, j)
                hidden(0)
                with pool.Fori(1, trips) as it:
                    for j in range(2 * HT):
                        split_unit(pool, ring, it * SL + j, j)
                    hidden(it)

            @block.tensor
            def _(pe):
                pe.sem_inc(pair_filled, PAIRS_B)
                pe.sem_inc(down_filled, DOWN_B)
                norm.tensor(pe)
                with pe.Fori(0, trips) as it:
                    for g in range(PAIRS_B):
                        f, t = divmod(g, NG)
                        if t == 0:
                            pe.wait_ge(ring.split, it * SL + (ST + 2 * f + 2))
                        pe.wait_ge(pair_drained, it * PAIRS_B + (g + 1))
                        if f == 0:
                            norm.ready(pe, t)
                        x = slice(t * GRP, (t + 1) * GRP)
                        for u in range(2):
                            for k in range(DK):
                                c = slice(k * P, (k + 1) * P)
                                m = product(pe, ps[:, g % 2, u, :GRP], ring.hi[:, 2 * f + u, c], ring.lo[:, 2 * f + u, c],
                                            S.x_hi[:, k, x], S.x_lo[:, k, x], k == 0, k == DK - 1)
                        m.then_inc(pair_filled, 1)
                    pe.wait_ge(ring.split, it * SL + (ST + SL))
                    for t in range(NG):
                        pe.wait_ge(hid_split, it * PAIRS_B + ((HT - 1) * NG + t + 1))
                        x = slice(t * GRP, (t + 1) * GRP)
                        for m in range(DK):
                            g = t * DK + m
                            pe.wait_ge(down_drained, it * DOWN_B + (g + 1))
                            c = slice(m * P, (m + 1) * P)
                            for f in range(HT):
                                ins = product(pe, dps[:, g % BANKS, :GRP], ring.hi[:, 2 * HT + f, c],
                                              ring.lo[:, 2 * HT + f, c], hid_hi[:, f, x], hid_lo[:, f, x],
                                              f == 0, f == HT - 1)
                            ins.then_inc(down_filled, 1)

            @block.vector
            def _(dve):
                dve.sem_inc(pair_drained, 2)
                norm.vector(dve)
                dve.sem_inc(down_drained, BANKS)
                with dve.Fori(0, trips) as it:
                    for g in range(PAIRS_B):
                        dve.wait_ge(gated, it * PAIRS_B + (g + 1))
                        if g >= 2:
                            dve.wait_ge(hid_split, it * PAIRS_B + (g - 1))
                        dve.tensor_tensor(hid[:, g % 2, :], gate[:, g % 2, :], ps[:, g % 2, 1, :GRP],
                                          ALU.mult).then_inc(pair_drained, 1)
                    for t in range(NG):
                        for m in range(DK):
                            g = t * DK + m
                            dve.wait_ge(down_filled, it * DOWN_B + (DOWN_B + g + 1))
                            h = S.res[:, m, t * GRP:(t + 1) * GRP]
                            dve.tensor_tensor(h, h, dps[:, g % BANKS, :GRP], ALU.add).then_inc(down_drained, 1)


def store_tokens(nc, S, a):
    with semaphores(nc) as sem:
        turned, taken = sem("y_turned"), sem("y_taken")
        y_out = sem("y_out")
        with ExitStack() as ctx:
            yt = ctx.enter_context(nc.sbuf_tensor("y_rows", [P, NT, D], F32))
            ps = ctx.enter_context(nc.psum_tensor("y_ps", [P, 2, D], F32))
            nps = ctx.enter_context(nc.psum_tensor("y_norm_ps", [P, 1 + NG, 512], F32))
            norm = Norm(nc, S, sem, ctx, "y_norm", G_FINAL, nps[:, 0, :], [nps[:, 1 + t, :GRP] for t in range(NG)],
                        final=True)
            block = ctx.enter_context(nc.Block())
            rows = [a["y_prompt"][0, i * P:(i + 1) * P, :] for i in range(NT - 1)]
            rows.append(a["y_sample"].rearrange("b s d -> (b s) d"))

            @block.scalar
            def _(act):
                norm.scalar(act)
                for i in range(NT):
                    act.wait_ge(turned, i + 1)
                    act.copy(yt[:, i, :], ps[:, i % 2, :]).then_inc(taken, 1)

            @block.tensor
            def _(pe):
                norm.tensor(pe)
                for i in range(NT):
                    norm.ready(pe, i * P // GRP)
                    if i >= 2:
                        pe.wait_ge(taken, i - 1)
                    for k in range(DK):
                        t = pe.transpose(ps[:, i % 2, k * P:(k + 1) * P], S.res[:, k, i * P:(i + 1) * P], S.ident[:])
                    t.then_inc(turned, 1)

            @block.vector
            def _(dve):
                norm.vector(dve)

            @block.sync
            def _(sp):
                for i in range(NT):
                    sp.wait_ge(taken, i + 1)
                    sp.dma_start(rows[i], yt[:, i, :]).then_inc(y_out, 16)
                sp.wait_ge(y_out, 16 * NT)
                sp.wait_ge(S.caches_kept, 2 * DEC_B * 16)


def gla_core(nc, S, a):
    with semaphores(nc) as sem:
        NB = SEQ // GLA_BLOCK
        NTP = NT - 1
        VT = GLA_DV // P
        STATES = 6
        STEPS = NB + DEC_B
        LAST = GLA_H - 1
        V_FILLS, K2_FILLS = 5, 4
        K2_TILES = [list(range(NT))[i * NT // K2_FILLS:(i + 1) * NT // K2_FILLS] for i in range(K2_FILLS)]
        KINDS = (("sums", 1), ("spread", NG), ("logit", NG), ("v", V_FILLS), ("k2", K2_FILLS))
        FILLS = sum(n for _, n in KINDS)
        BEFORE = NG + V_FILLS + K2_FILLS
        assert FILLS % 2 == 0

        def number(kind):
            return sum(n for _, n in KINDS[:[k for k, _ in KINDS].index(kind)])

        def first(h):
            return isinstance(h, int) and h == 0

        def place(h, n):
            return n % 2, h * (FILLS // 2) + n // 2, h * FILLS + n

        def prep(h, kind, n):
            if first(h):
                return place(0, number(kind) - number("logit") + n)
            return place(h - 1, BEFORE - number("logit") + number(kind) + n)

        def post(h, kind, n):
            at = BEFORE - number("logit") + number(kind) + n
            if isinstance(h, int) and h == LAST:
                return place(LAST, at + number("logit"))
            return place(h + 1, at)

        def heads(engine, body):
            body(0, 0, False)
            with engine.Fori(0, (GLA_H - 2) // 2) as it:
                body(it * 2 + 1, 1, False)
                body(it * 2 + 2, 0, False)
            body(LAST, 1, True)

        small_in, qk_in, v_in, g_in, st_in = (sem(f"gla_{n}_in") for n in ("small", "qk", "v", "g", "state"))
        paced = sem("gla_paced")
        turn_filled = sem("gla_turn_filled")
        taken = [sem(f"gla_turn_taken{i}") for i in range(2)]
        softplus = sem("gla_softplus")
        decay = sem("gla_decay")
        grown = sem("gla_grown")
        scaled, k2_made = sem("gla_scaled"), sem("gla_k2_made")
        zeroed = sem("gla_zeroed")
        s_filled, s_masked = sem("gla_scores_filled"), sem("gla_scores_masked")
        u_filled, stepped = sem("gla_update_filled"), sem("gla_state_stepped")
        o_filled, o_taken = sem("gla_out_filled"), sem("gla_out_taken")
        spread = sem("gla_k2_spread")
        squared, added = sem("gla_squared"), sem("gla_squares_added")
        gated, inverse, diagonal, normed, mixed = (sem(f"gla_{n}") for n in (
            "gated", "inverse", "diagonal", "normed", "mixed"))
        st_out = sem("gla_state_out")
        with ExitStack() as ctx:
            def sb(name, shape, dt=F32):
                return ctx.enter_context(nc.sbuf_tensor(f"mix_{name}", shape, dt))

            def pb(name, shape):
                return ctx.enter_context(nc.psum_tensor(f"mix_{name}", shape, F32))

            w2 = sb("w_gate2", [RANK, P])
            bg = sb("b_gate", [P, 1])
            ng = sb("norm_gain", [P, VT])
            reset = sb("reset", [P, TOK])
            q, k = sb("q", [P, 2, TOK]), sb("k", [P, 2, TOK])
            vt = sb("vt", [P, VT, TOK])
            g = sb("g", [P, VT, TOK])
            v = sb("v", [P, 2, NT, GLA_DV])
            soft = sb("soft", [P, TOK])
            least = sb("least", [P, TOK])
            b_sum = sb("b", [P, TOK])
            eb = sb("eb", [P, 2, TOK])
            k2t = sb("k2t", [P, 2, NT, P])
            spread_k2 = sb("k2_spread", [P, DEC_B, P])
            st_s = sb("state_sample", [P, DEC_B, GLA_DV])
            st = sb("state", [P, STATES, GLA_DV])
            st_fin = sb("state_last", [P, GLA_DV])
            sc = sb("scores", [P, 3, P])
            sq = sb("squares", [P, 2, VT, P])
            acc = sb("squares_added", [P, NT, P])
            rms = sb("rms", [P, NT])
            diag = sb("diagonals", [P, NG, GRP])
            turn = pb("turn", [P, 2, 512])
            sps, ups, ops = pb("score_ps", [P, 2, 512]), pb("update_ps", [P, 2, 512]), pb("out_ps", [P, 2, 512])
            block = ctx.enter_context(nc.Block())
            zt = S.gla_rows

            def out_columns(h, j, first_token, tokens):
                flat = S.mixed[:].rearrange("p k t -> p (k t)")
                if j is None:
                    return flat[:, bass.ds(h * (VT * TOK), VT * TOK)].rearrange(
                        "p (j t) -> p j t", t=TOK)[:, :, first_token:first_token + tokens]
                return flat[:, bass.ds(h * (VT * TOK) + (j * TOK + first_token), tokens)]

            @block.sync
            def _(sp):
                def load_small(h):
                    sp.dma_start(w2[:], a["gla_w_gate2"][0, :, bass.ds(h * P, P)]).then_inc(small_in, 16)
                    sp.dma_start(bg[:], a["gla_b_gate"].rearrange("l (n o) -> (l n) o", o=1)[bass.ds(h * P, P), :]
                                 ).then_inc(small_in, 16)
                    sp.dma_start(least[0:RANK, :], zt[2 * NQK + 2 * NV:, :]).then_inc(small_in, 16)

                def load_v(h):
                    sp.dma_start(vt[:], zt[bass.ds(h * GLA_DV + 2 * NQK, GLA_DV), :].rearrange("(j p) t -> p j t", p=P)
                                 ).then_inc(v_in, 16)

                def load_qk(h, b):
                    sp.dma_start(q[:, b, :], zt[bass.ds(h * P, P), :]).then_inc(qk_in, 16)
                    sp.dma_start(k[:, b, :], zt[bass.ds(h * P + NQK, P), :]).then_inc(qk_in, 16)

                load_small(0)
                load_qk(0, 0)
                load_v(0)

                def head(h, b, last):
                    if not last:
                        sp.wait_ge(scaled, h * 2 + 2)
                        sp.sem_inc(paced, 1)
                        load_small(h + 1)
                        sp.wait_ge(turn_filled, prep(h, "v", V_FILLS - 1)[2] + 1)
                        sp.sem_inc(paced, 1)
                        load_v(h + 1)
                    if not first(h):
                        sp.wait_ge(st_out, h * 32)
                        sp.sem_inc(paced, 1)
                    sp.dma_start(st_s[:], a["state_gla"][0, :, bass.ds(h, 1), :, :].rearrange("b o k v -> (o k) b v")
                                 ).then_inc(st_in, 16)
                    if not last:
                        sp.wait_ge(o_filled, h * NT + 1)
                        sp.sem_inc(paced, 1)
                        load_qk(h + 1, 1 - b)
                    if not first(h):
                        sp.wait_ge(mixed, h * NG)
                        sp.sem_inc(paced, 1)
                    sp.dma_start(g[:], zt[bass.ds(h * GLA_DV + 2 * NQK + NV, GLA_DV), :].rearrange("(j p) t -> p j t", p=P)
                                 ).then_inc(g_in, 16)
                    sp.dma_start(ng[:], a["gla_norm"].rearrange("l (h j p) -> p (l h) j", j=VT, p=P)[:, bass.ds(h, 1), :],
                                 allow_slow_non_contiguous=True).then_inc(g_in, 16)

                heads(sp, head)
                sp.wait_ge(S.strips_kept, 16)

            @block.tensor
            def _(pe):
                def bank(at):
                    pe.wait_ge(taken[at[0]], at[1] + 1)
                    return turn[:, at[0], :]

                def logits(h):
                    pe.wait_ge(small_in, h * 48 + 48)
                    for t in range(NG):
                        dst = bank(prep(h, "logit", t))
                        pe.matmul(dst[:, :GRP], w2[:], least[0:RANK, t * GRP:(t + 1) * GRP]).then_inc(turn_filled, 1)

                def turn_v(h, n):
                    pe.wait_ge(v_in, h * 16 + 16)
                    dst = bank(prep(h, "v", n))
                    for i in range(2 * n, min(2 * n + 2, NT)):
                        for j in range(VT):
                            c = (i % 2) * GLA_DV + j * P
                            m = pe.transpose(dst[:, c:c + P], vt[:, j, i * P:(i + 1) * P], S.ident[:])
                    m.then_inc(turn_filled, 1)

                def turn_k2(h, n):
                    pe.wait_ge(k2_made, h * 2 + 2)
                    dst = bank(prep(h, "k2", n))
                    for c, i in enumerate(K2_TILES[n]):
                        m = pe.transpose(dst[:, c * P:(c + 1) * P], soft[:, i * P:(i + 1) * P], S.ident[:])
                    m.then_inc(turn_filled, 1)

                def finish(h):
                    pe.wait_ge(added, h * NT + (NT + 2))
                    dst = bank(post(h, "sums", 0))
                    for i in range(NT):
                        m = pe.matmul(dst[:, i:i + 1], acc[:, i, :], S.ones[:, :1])
                    m.then_inc(turn_filled, 1)
                    for t in range(NG):
                        pe.wait_ge(diagonal, h * NG + (t + 1))
                        dst = bank(post(h, "spread", t))
                        pe.matmul(dst[:, :GRP], S.ones[:], diag[:, t, :]).then_inc(turn_filled, 1)

                def out(h, b, i):
                    pe.wait_ge(s_masked, h * NT + (2 + i + 1))
                    if i < NTP:
                        pe.wait_ge(stepped, h * STEPS + (4 + 2 * i + 1))
                    else:
                        pe.wait_ge(st_in, h * 16 + 16)
                    pe.wait_ge(o_taken, h * NT + (i + 1))
                    slot = i % 2 if i < NTP else 2
                    for j in range(VT):
                        dst, vc = ops[:, i % 2, j * P:(j + 1) * P], slice(j * P, (j + 1) * P)
                        pe.matmul(dst, v[:, b, i, vc], sc[:, slot, :], start=True, stop=False)
                        if i < NTP:
                            for c in range(2):
                                cols = slice(c * GLA_BLOCK, (c + 1) * GLA_BLOCK)
                                m = pe.matmul(dst[:, cols], st[:, (2 * i + c) % STATES, vc],
                                              q[:, b, i * P + c * GLA_BLOCK:i * P + (c + 1) * GLA_BLOCK],
                                              start=False, stop=c == 1)
                        else:
                            for s in range(DEC_B):
                                cols = slice(s * DEC_S, (s + 1) * DEC_S)
                                m = pe.matmul(dst[:, cols], st_s[:, s, vc],
                                              q[:, b, SEQ + s * DEC_S:SEQ + (s + 1) * DEC_S],
                                              start=False, stop=s == DEC_B - 1)
                    m.then_inc(o_filled, 1)

                logits(0)
                for n in range(V_FILLS):
                    turn_v(0, n)
                for n in range(K2_FILLS):
                    turn_k2(0, n)

                def head(h, b, last):
                    pe.wait_ge(scaled, h * 2 + 2)
                    for n in (K2_FILLS - 2, K2_FILLS - 1):
                        at = prep(h, "k2", n)
                        pe.wait_ge(taken[at[0]], at[1] + 2)
                    for i in range(NT + 1):
                        if i < NT:
                            pe.wait_ge(s_masked, h * NT + (i + 1))
                            cols = slice(i * P, (i + 1) * P)
                            pe.matmul(sps[:, i % 2, :P], k[:, b, cols], q[:, b, cols]).then_inc(s_filled, 1)
                        if i < NTP:
                            pe.wait_ge(stepped, h * STEPS + (4 + 2 * i))
                            for c in range(2):
                                r = slice(c * GLA_BLOCK, (c + 1) * GLA_BLOCK)
                                m = pe.matmul(ups[:, c, :GLA_DV], k2t[r, b, i, :], v[r, b, i, :])
                            m.then_inc(u_filled, 1)
                        if i == 0 and not first(h):
                            finish(h - 1)
                        if i:
                            out(h, b, i - 1)
                        if not last:
                            if i == 1:
                                logits(h + 1)
                            if 2 <= i < 2 + V_FILLS:
                                turn_v(h + 1, i - 2)
                            if i == NT:
                                turn_k2(h + 1, 0)
                                turn_k2(h + 1, 1)
                    pe.wait_ge(spread, h + 1)
                    for n in range(DEC_B):
                        pe.wait_ge(stepped, h * STEPS + (4 + NB + n - 1))
                        pe.matmul(ups[:, n % 2, :GLA_DV], spread_k2[:, n, :], v[:, b, NTP, :]).then_inc(u_filled, 1)
                    if not last:
                        for n in range(2, K2_FILLS):
                            turn_k2(h + 1, n)

                heads(pe, head)
                finish(LAST)

            @block.scalar
            def _(act):
                def is_filled(at):
                    act.wait_ge(turn_filled, at[2] + 1)
                    return turn[:, at[0], :]

                def soft_logits(h):
                    for t in range(NG):
                        at = prep(h, "logit", t)
                        act.activation(soft[:, t * GRP:(t + 1) * GRP], is_filled(at)[:, :GRP], ACT.Identity,
                                       bias=bg[:]).then_inc(taken[at[0]], 1)
                    act.wait_ge(decay, h * 3 + 1)
                    act.activation(soft[:], soft[:], ACT.Abs).then_inc(softplus, 1)
                    act.wait_ge(softplus, h * 3 + 1)
                    act.activation(soft[:], soft[:], ACT.Exp, scale=-1.0).then_inc(softplus, 1)
                    act.wait_ge(softplus, h * 3 + 2)
                    act.activation(soft[:], soft[:], ACT.Ln, bias=1.0).then_inc(softplus, 1)

                def take_v(h, b, n):
                    at = prep(h, "v", n)
                    w = min(2, NT - 2 * n)
                    act.copy(v[:, b, 2 * n:2 * n + w, :].rearrange("p i d -> p (i d)"),
                             is_filled(at)[:, :w * GLA_DV]).then_inc(taken[at[0]], 1)

                def grow(h, b):
                    act.wait_ge(decay, h * 3 + 3)
                    act.activation(eb[:, b, :], b_sum[:], ACT.Exp, scale=1.0 / GLA_TAU).then_inc(grown, 1)
                    act.activation(least[:], b_sum[:], ACT.Exp, scale=-1.0 / GLA_TAU).then_inc(grown, 1)

                def take_k2(h, b, n):
                    at = prep(h, "k2", n)
                    lo, w = K2_TILES[n][0], len(K2_TILES[n])
                    act.copy(k2t[:, b, lo:lo + w, :].rearrange("p i d -> p (i d)"),
                             is_filled(at)[:, :w * P]).then_inc(taken[at[0]], 1)

                def finish(h):
                    at = post(h, "sums", 0)
                    act.activation(rms[:], is_filled(at)[:, :NT], ACT.Sqrt, bias=S.eps[:],
                                   scale=1.0 / GLA_DV).then_inc(taken[at[0]], 1)
                    act.wait_ge(g_in, h * 32 + 32)
                    act.activation(g[:], g[:], ACT.Silu).then_inc(gated, 1)

                soft_logits(0)
                for n in range(V_FILLS):
                    take_v(0, 0, n)
                grow(0, 0)
                for n in range(K2_FILLS):
                    take_k2(0, 0, n)

                def head(h, b, last):
                    for i in range(NT + 1):
                        if i == 0 and not first(h):
                            finish(h - 1)
                        if i:
                            act.wait_ge(o_filled, h * NT + i)
                            act.wait_ge(added, h * NT + i)
                            src = ops[:, (i - 1) % 2, :VT * P].rearrange("p (j t) -> p j t", t=P)
                            act.activation(sq[:, (i - 1) % 2, :, :], src, ACT.Square).then_inc(squared, 1)
                            act.copy(out_columns(h, None, (i - 1) * P, P), src).then_inc(o_taken, 1)
                        if not last:
                            if i == 1:
                                soft_logits(h + 1)
                            if 2 <= i < 2 + V_FILLS:
                                take_v(h + 1, 1 - b, i - 2)
                            if i == 5:
                                grow(h + 1, 1 - b)
                            if i == NT:
                                take_k2(h + 1, 1 - b, 0)
                                take_k2(h + 1, 1 - b, 1)
                    if not last:
                        for n in range(2, K2_FILLS):
                            take_k2(h + 1, 1 - b, n)
                    act.wait_ge(stepped, h * STEPS + (STEPS + 4))
                    act.dma_start(a["state_gla_prompt"][0, 0, bass.ds(h, 1), :, :].rearrange("o k v -> (o k) v"), st_fin[:]
                                  ).then_inc(st_out, 16)
                    act.dma_start(a["state_gla_sample"][0, :, bass.ds(h, 1), :, :].rearrange("b o k v -> (o k) b v"), st_s[:]
                                  ).then_inc(st_out, 16)

                heads(act, head)
                finish(LAST)
                act.wait_ge(st_out, GLA_H * 32)

            @block.gpsimd
            def _(pool):
                for i in range(2):
                    pool.sem_inc(taken[i], 1)
                pool.sem_inc(added, 2)

                def make_k2(h, b):
                    pool.wait_ge(scaled, h * 2 + 2)
                    for lo, hi, blk in ((0, SEQ, GLA_BLOCK), (SEQ, TOK, DEC_S)):
                        n = (hi - lo) // blk
                        pool.tensor_tensor(soft[:, lo:hi].rearrange("p (n t) -> p n t", t=blk),
                                           k[:, b, lo:hi].rearrange("p (n t) -> p n t", t=blk),
                                           eb[:, b, lo + blk - 1:hi:blk].unsqueeze(2).to_broadcast([P, n, blk]),
                                           ALU.mult).then_inc(k2_made, 1)

                def finish(h):
                    pool.wait_ge(gated, h + 1)
                    for t in range(NG):
                        pool.wait_ge(normed, h * (NG * VT) + (t + 1) * VT)
                        o = out_columns(h, None, t * GRP, GRP)
                        pool.tensor_tensor(o, o, g[:, :, t * GRP:(t + 1) * GRP], ALU.mult).then_inc(mixed, 1)

                make_k2(0, 0)

                def head(h, b, last):
                    if not first(h):
                        pool.wait_ge(u_filled, h * (NTP + DEC_B))
                    for n in (K2_FILLS - 2, K2_FILLS - 1):
                        at = prep(h, "k2", n)
                        pool.wait_ge(taken[at[0]], at[1] + 2)
                    pool.tensor_tensor(spread_k2[:], k2t[:, b, NTP:NT, :].to_broadcast([P, DEC_B, P]),
                                       S.stream[:].unsqueeze(2).to_broadcast([P, DEC_B, P]), ALU.mult).then_inc(spread, 1)
                    for i in range(NT + 1):
                        if i == 1 and not first(h):
                            pool.wait_ge(turn_filled, post(h - 1, "sums", 0)[2] + 1)
                            finish(h - 1)
                        if i:
                            pool.wait_ge(squared, h * NT + i)
                            pool.tensor_tensor(acc[:, i - 1, :], sq[:, (i - 1) % 2, 0, :], sq[:, (i - 1) % 2, 1, :],
                                               ALU.add).then_inc(added, 1)
                        if i == 6 and not last:
                            make_k2(h + 1, 1 - b)

                heads(pool, head)
                finish(LAST)

            @block.vector
            def _(dve):
                dve.sem_inc(s_masked, 2)
                dve.sem_inc(stepped, 4)
                dve.sem_inc(o_taken, 2)
                dve.memset(sc[:], 0.0).then_inc(zeroed, 1)
                dve.memset(reset[:], 1.0).then_inc(zeroed, 1)
                dve.wait_ge(zeroed, 2)
                dve.memset(reset[:, 0:SEQ:GLA_BLOCK], 0.0).then_inc(zeroed, 1)
                dve.memset(reset[:, SEQ::DEC_S], 0.0).then_inc(zeroed, 1)
                dve.wait_ge(zeroed, 4)

                def clip(h):
                    for n in (NG - 2, NG - 1):
                        at = prep(h, "logit", n)
                        dve.wait_ge(taken[at[0]], at[1] + 2)
                    dve.tensor_scalar(least[:], soft[:], 0.0, None, ALU.min).then_inc(decay, 1)

                def cumulate(h):
                    dve.wait_ge(softplus, h * 3 + 3)
                    dve.wait_ge(decay, h * 3 + 1)
                    dve.tensor_tensor(least[:], least[:], soft[:], ALU.subtract).then_inc(decay, 1)
                    dve.wait_ge(decay, h * 3 + 2)
                    dve.tensor_tensor_scan(b_sum[:], reset[:], least[:], 0.0, ALU.mult, ALU.add).then_inc(decay, 1)

                def scale(h, b):
                    dve.wait_ge(qk_in, h * 32 + 32)
                    dve.wait_ge(grown, h * 2 + 2)
                    dve.scalar_tensor_tensor(q[:, b, :], q[:, b, :], GLA_DK ** -0.5, eb[:, b, :], ALU.mult,
                                             ALU.mult).then_inc(scaled, 1)
                    dve.tensor_tensor(k[:, b, :], k[:, b, :], least[:], ALU.mult).then_inc(scaled, 1)

                def invert(h):
                    at = post(h, "sums", 0)
                    dve.wait_ge(taken[at[0]], at[1] + 2)
                    dve.reciprocal(rms[:], rms[:]).then_inc(inverse, 1)
                    dve.wait_ge(inverse, h + 1)
                    for t in range(NG):
                        dve.tensor_tensor(diag[:, t, :].rearrange("p (i c) -> p i c", c=P),
                                          S.ident[:].unsqueeze(1).to_broadcast([P, NG, P]),
                                          rms[:, t * NG:(t + 1) * NG].unsqueeze(2).to_broadcast([P, NG, P]),
                                          ALU.mult).then_inc(diagonal, 1)

                def finish(h):
                    dve.wait_ge(g_in, h * 32 + 32)
                    dve.wait_ge(o_taken, h * NT + (NT + 2))
                    for t in range(NG):
                        at = post(h, "spread", t)
                        dve.wait_ge(turn_filled, at[2] + 1)
                        for j in range(VT):
                            o = out_columns(h, j, t * GRP, GRP)
                            m = dve.scalar_tensor_tensor(o, o, ng[:, j:j + 1], turn[:, at[0], :GRP], ALU.mult, ALU.mult)
                            m.then_inc(normed, 1)
                        dve.wait_ge(normed, h * (NG * VT) + (t + 1) * VT)
                        dve.sem_inc(taken[at[0]], 1)

                clip(0)
                cumulate(0)
                scale(0, 0)

                def head(h, b, last):
                    if not first(h):
                        dve.wait_ge(o_filled, h * NT)
                    dve.memset(st[:, 0, :], 0.0).then_inc(zeroed, 1)
                    dve.wait_ge(zeroed, h + 5)
                    for i in range(NT):
                        dve.wait_ge(s_filled, h * NT + (i + 1))
                        if i >= 2:
                            dve.wait_ge(o_filled, h * NT + (i - 1))
                        dve.sem_inc(paced, 1)
                        dve.copy_predicated(sc[:, i % 2 if i < NTP else 2, :],
                                            S.causal[:, 0 if i < NTP else 1, :].bitcast(I32),
                                            sps[:, i % 2, :P]).then_inc(s_masked, 1)
                        if i < NTP:
                            dve.wait_ge(u_filled, h * (NTP + DEC_B) + (i + 1))
                            for c in range(2):
                                n = 2 * i + c
                                dve.wait_ge(stepped, h * STEPS + (4 + n))
                                if n + 1 >= STATES:
                                    dve.wait_ge(o_filled, h * NT + ((n + 1 - STATES) // 2 + 1))
                                if n == NB - 1 and not first(h):
                                    dve.wait_ge(st_out, h * 32)
                                last_col = n * GLA_BLOCK + GLA_BLOCK - 1
                                dst = st_fin[:] if n == NB - 1 else st[:, (n + 1) % STATES, :]
                                dve.scalar_tensor_tensor(dst, st[:, n % STATES, :], eb[:, b, last_col:last_col + 1],
                                                         ups[:, c, :GLA_DV], ALU.mult, ALU.add).then_inc(stepped, 1)
                        if i == 0 and not first(h):
                            invert(h - 1)
                            finish(h - 1)
                        if not last:
                            if i == 1:
                                clip(h + 1)
                            if i == 3:
                                cumulate(h + 1)
                            if i == 6:
                                scale(h + 1, 1 - b)
                    dve.wait_ge(o_filled, h * NT + NT)
                    for n in range(DEC_B):
                        dve.wait_ge(u_filled, h * (NTP + DEC_B) + (NTP + n + 1))
                        last_col = SEQ + n * DEC_S + DEC_S - 1
                        dve.scalar_tensor_tensor(st_s[:, n, :], st_s[:, n, :], eb[:, b, last_col:last_col + 1],
                                                 ups[:, n % 2, :GLA_DV], ALU.mult, ALU.add).then_inc(stepped, 1)

                heads(dve, head)
                invert(LAST)
                finish(LAST)


def attention_core(nc, S, a):
    with semaphores(nc) as sem:
        NTP = NT - 1
        UNITS = 2 * NTP
        GB = DEC_B // 2
        GROUPS = DEC_B // GB
        ALLU = UNITS + GROUPS
        KEPT = 5
        KT_S = PAST // P
        WIDE = BAND_T * P
        SW = PAST + P
        BANK = 512
        PREPS = 4
        AT_Q, AT_FILL = 9, 10
        AT_KEYS = (2, 7)

        def width(u):
            return P * min(u // 2 + 1, BAND_T) if u < UNITS else SW

        def parts(u):
            w = width(u)
            return [(0, w)] if w <= 3 * P else [(0, 3 * P), (3 * P, w)]

        def order(last):
            number, n = {}, PREPS
            for u in range(ALLU + 2 if last else ALLU):
                if not last and AT_FILL <= u < AT_FILL + PREPS:
                    number["prep", u - AT_FILL] = n
                    n += 1
                if u in AT_KEYS:
                    for m in range(2):
                        number["keys", AT_KEYS.index(u), m] = n
                        n += 1
                if u >= 2:
                    for m in range(len(parts(u - 2))):
                        number["probs", u - 2, m] = n
                        n += 1
            return number, n

        STEADY, end = order(False)
        FILLS = end - PREPS + GROUPS
        for g in range(GROUPS):
            STEADY["probs", UNITS + g, 0] = FILLS + PREPS - GROUPS + g
        LAST, _ = order(True)
        assert FILLS % 2 == 0

        LAST_PAIR = PAIRS - 1

        def fill(h, *key):
            n = (LAST if isinstance(h, int) and h == LAST_PAIR else STEADY)[key]
            return n % 2, h * (FILLS // 2) + n // 2, h * FILLS + n

        def prep_fill(h, n):
            return (n % 2, n // 2, n) if h is None else fill(h, "prep", n)

        def back(h, u, steps):
            v = u - steps
            if v < 0:
                return (None, None) if isinstance(h, int) and h == 0 else (h - 1, v + ALLU)
            return (h, v) if v < ALLU else (None, None)

        def pairs(engine, body):
            body(0, 0, False)
            with engine.Fori(0, (PAIRS - 2) // 2) as it:
                body(it * 2 + 1, 1, False)
                body(it * 2 + 2, 0, False)
            body(LAST_PAIR, 1, True)

        qkv_in, bias_in = sem("att_qkv_in"), sem("att_bias_in")
        kc_in, vc_in = sem("att_kcache_in"), sem("att_vcache_in")
        masked = sem("att_bias_masked")
        paced = sem("att_paced")
        q_scaled, rows_done, qz_done = sem("att_q_scaled"), sem("att_rows"), sem("att_qz")
        turn_filled = sem("att_turn_filled")
        taken = [sem(f"att_turn_taken{i}") for i in range(2)]
        s_filled, biased = sem("att_scores_filled"), sem("att_biased")
        exped, inverse, scaled = sem("att_exp"), sem("att_inverse"), sem("att_probs")
        o_filled, o_taken = sem("att_out_filled"), sem("att_out_taken")
        cached = sem("att_cache_out")
        with ExitStack() as ctx:
            def sb(name, shape, dt=F32):
                return ctx.enter_context(nc.sbuf_tensor(f"att_{name}", shape, dt))

            def pb(name, shape):
                return ctx.enter_context(nc.psum_tensor(f"att_{name}", shape, F32))

            qf, kf, vf = sb("q", [P, TOK]), sb("k", [P, 2, TOK]), sb("v", [P, TOK])
            qs = sb("q_scaled", [P, 2, TOK])
            vr, kr = sb("v_rows", [P, 2, NT, P]), sb("k_rows", [P, KEPT, P])
            probs = sb("probs", [P, 3, WIDE])
            pt = sb("p_turned", [P, 2, WIDE])
            top, total = sb("top", [P, 3]), sb("total", [P, 3])
            rec = sb("rec", [P, 3])
            bias = sb("bias", [P, 2, 2, WIDE])
            bias_s = sb("bias_s", [P, 2, GROUPS, SW])
            own = sb("own", [P, 2, DEC_S])
            kc = sb("k_cache", [P, GB, KT_S, P])
            vc = sb("v_cache", [P, GROUPS, GB, KT_S, P])
            kt = sb("k_turned", [P, GROUPS, GB, PAST])
            qz = sb("q_sample", [P, GROUPS, GB, P])
            qa = sb("q_sample_all", [P, GROUPS, P])
            sps = pb("score_ps", [P, 2, 2 * BANK])
            tps = pb("turn_ps", [P, 2, BANK])
            ops = pb("out_ps", [P, 2, BANK])
            block = ctx.enter_context(nc.Block())

            def skewed(h, head, rows, first, cols, copies=None):
                ap = [[STRIP - 1, rows], [1, cols]]
                if copies:
                    ap = [[0, copies]] + ap
                base = S.strips[bass.ds(h * 2 + head, 1), 0, first:first + 1]
                return bass.AP(tensor=base.tensor, offset=base.offset, ap=ap)

            @block.sync
            def _(sp):
                def load_qkv(h, b):
                    for n, dst in enumerate((qf[:], kf[:, b, :], vf[:])):
                        sp.dma_start(dst, S.qkv_rows[bass.ds(h * P + n * D, P), :]).then_inc(qkv_in, 16)

                def load_bias(h, b):
                    zero = STRIP_C + CLIP
                    for head in range(2):
                        sp.dma_start(bias[:, b, head, :], skewed(h, head, P, zero - (WIDE - P), WIDE)).then_inc(bias_in, 16)
                        half = slice(head * CHUNK, (head + 1) * CHUNK)
                        for g in range(GROUPS):
                            sp.dma_start(bias_s[half, b, g, :PAST],
                                         skewed(h, head, DEC_S, zero - PAST, PAST, GB)).then_inc(bias_in, 16)
                        sp.dma_start(own[half, b, :], skewed(h, head, DEC_S, zero, DEC_S, GB)).then_inc(bias_in, 16)

                def load_cache(h, g, name, dst, signal):
                    for b in range(GB):
                        src = a[name][g * GB + b].rearrange("(t p) h d -> p t (h d)", p=P)
                        sp.dma_start(dst[:, b], src[:, :, bass.ds(h * P, P)]).then_inc(signal, 16)

                load_qkv(0, 0)
                load_bias(0, 0)
                load_cache(0, 0, "cache_k", kc, kc_in)
                for g in range(GROUPS):
                    load_cache(0, g, "cache_v", vc[:, g], vc_in)

                def keep_rows(stream):
                    for nm in "kv":
                        old, new = (a[n].rearrange("b s h d -> b (s h d)")[bass.ds(stream, 1)]
                                    for n in (f"cache_{nm}", f"cache_{nm}_sample"))
                        sp.dma_start(new[:, :(PAST - DEC_S) * D], old[:, DEC_S * D:]).then_inc(S.caches_kept, 16)

                assert PAIRS == DEC_B

                def pair(h, b, last):
                    if not last:
                        sp.wait_ge(q_scaled, h + 1)
                        sp.sem_inc(paced, 1)
                        sp.wait_ge(rows_done, h + 1)
                        sp.sem_inc(paced, 1)
                        sp.wait_ge(biased, h * ALLU + 2)
                        sp.sem_inc(paced, 1)
                        load_qkv(h + 1, 1 - b)
                    sp.wait_ge(turn_filled, fill(h, "keys", 0, 1)[2] + 1)
                    sp.sem_inc(paced, 1)
                    load_cache(h, 1, "cache_k", kc, kc_in)
                    if not (isinstance(h, int) and h == 0):
                        sp.wait_ge(o_filled, h * ALLU + 1)
                        sp.sem_inc(paced, 1)
                        for g in range(GROUPS):
                            load_cache(h, g, "cache_v", vc[:, g], vc_in)
                    if not last:
                        sp.wait_ge(masked, h * (2 + GROUPS) + (2 + GROUPS))
                        sp.sem_inc(paced, 1)
                        load_bias(h + 1, 1 - b)
                        sp.wait_ge(turn_filled, fill(h, "keys", 1, 1)[2] + 1)
                        sp.sem_inc(paced, 1)
                        load_cache(h + 1, 0, "cache_k", kc, kc_in)
                    keep_rows(h)

                pairs(sp, pair)

            @block.gpsimd
            def _(pool):
                MASKS = 2 + GROUPS
                for i in range(2):
                    pool.sem_inc(taken[i], 1)
                pool.memset(qz[:], 0.0).then_inc(qz_done, 1)
                pool.memset(qa[:], 0.0).then_inc(qz_done, 1)

                def mask_bias(h, b):
                    pool.wait_ge(bias_in, h * 128 + 128)
                    pool.sem_inc(paced, 1)
                    pool.memset(bias[:CHUNK, b, :, WIDE - CHUNK:], MASKED).then_inc(masked, 1)
                    pool.wait_ge(masked, h * MASKS + 1)
                    pool.sem_inc(paced, 1)
                    pool.memset(bias[CHUNK:, b, :, :CHUNK], MASKED).then_inc(masked, 1)
                    pool.wait_ge(masked, h * MASKS + 2)
                    mask = S.own_mask[:].rearrange("p g (b s) -> p g b s", s=DEC_S)
                    for g in range(GROUPS):
                        pool.tensor_tensor(bias_s[:, b, g, PAST:].rearrange("p (b s) -> p b s", s=DEC_S),
                                           own[:, b, :].unsqueeze(1).to_broadcast([P, DEC_B, DEC_S]), mask[:, g],
                                           ALU.add).then_inc(masked, 1)

                mask_bias(0, 0)

                def pair(h, b, last):
                    pool.wait_ge(s_filled, h * ALLU + 1)
                    pool.sem_inc(paced, 1)
                    pool.wait_ge(q_scaled, h + 1)
                    pool.sem_inc(paced, 1)
                    n = 0
                    for g in range(GROUPS):
                        for head in range(2):
                            f = slice(head * DH, (head + 1) * DH)
                            dst = qz[f, g].rearrange("p b c -> p (b c)")
                            dst = bass.AP(tensor=dst.tensor, offset=dst.offset + head * DH,
                                          ap=[dst.ap[0], [P + DEC_S, GB], [1, DEC_S]])
                            src = qs[f, b, SEQ + g * GB * DEC_S:SEQ + (g + 1) * GB * DEC_S]
                            pool.wait_ge(qz_done, h * (4 * GROUPS) + (n + 2))
                            pool.sem_inc(paced, 1)
                            pool.tensor_copy(dst, src.rearrange("p (b s) -> p b s", s=DEC_S)).then_inc(qz_done, 1)
                            pool.wait_ge(qz_done, h * (4 * GROUPS) + (n + 3))
                            pool.sem_inc(paced, 1)
                            pool.tensor_copy(qa[f, g, head * DH:(head + 1) * DH], src).then_inc(qz_done, 1)
                            n += 2
                    if not last:
                        mask_bias(h + 1, 1 - b)

                pairs(pool, pair)

            @block.tensor
            def _(pe):
                def bank(at):
                    pe.wait_ge(taken[at[0]], at[1] + 1)
                    return tps[:, at[0], :]

                def is_taken(at):
                    pe.wait_ge(taken[at[0]], at[1] + 2)

                def prepare(h, b, n):
                    if n == 0:
                        pe.wait_ge(qkv_in, 48 if h is None else h * 48 + 96)
                    k = kf[:, b, :]
                    src = [(vf, i) for i in range(NTP)] + [(k, NT - KEPT + i) for i in range(KEPT)] + [(vf, NTP)]
                    dst = bank(prep_fill(h, n))
                    for i, (t, c) in enumerate(src[4 * n:4 * n + 4]):
                        m = pe.transpose(dst[:, i * P:(i + 1) * P], t[:, c * P:(c + 1) * P], S.ident[:])
                    m.then_inc(turn_filled, 1)

                def scores(h, b, u):
                    pe.wait_ge(biased, h * ALLU + (u + 1))
                    if u < UNITS:
                        j, head = divmod(u, 2)
                        f = slice(head * DH, (head + 1) * DH)
                        w = width(u)
                        first = j * P + P - w
                        for c in range(0, w, BANK):
                            n = min(BANK, w - c)
                            m = pe.matmul(sps[:, u % 2, c:c + n], qs[f, b, j * P:(j + 1) * P],
                                          kf[f, b, first + c:first + c + n])
                    else:
                        g = u - UNITS
                        pe.wait_ge(qz_done, h * (4 * GROUPS) + (4 * g + 6))
                        for m in range(2):
                            is_taken(fill(h, "keys", g, m))
                        for s in range(GB):
                            pe.matmul(sps[:, u % 2, :PAST], qz[:, g, s, :], kt[:, g, s, :], start=s == 0, stop=s == GB - 1)
                        m = pe.matmul(sps[:, u % 2, PAST:SW], qa[:, g, :], kf[:, b, SEQ:])
                    m.then_inc(s_filled, 1)

                def turn_keys(h, g):
                    pe.wait_ge(kc_in, h * (GROUPS * GB * 16) + (g + 1) * GB * 16)
                    for n in range(2):
                        dst = bank(fill(h, "keys", g, n))
                        for i in range(4):
                            m = pe.transpose(dst[:, i * P:(i + 1) * P], kc[:, 2 * n + i // 2, i % 2, :], S.ident[:])
                        m.then_inc(turn_filled, 1)

                def turn_probs(h, v):
                    pe.wait_ge(scaled, h * ALLU + (v + 1))
                    for n, (lo, hi) in enumerate(parts(v)):
                        dst = bank(fill(h, "probs", v, n))
                        for c in range(lo, hi, P):
                            m = pe.transpose(dst[:, c - lo:c - lo + P], probs[:, v % 3, c:c + P], S.ident[:])
                        m.then_inc(turn_filled, 1)

                def out(h, b, v):
                    pe.wait_ge(o_taken, h * ALLU + (v + 1))
                    dst = ops[:, v % 2, :P]
                    for n in range(len(parts(v))):
                        is_taken(fill(h, "probs", v, n))
                    if v < UNITS:
                        tiles = width(v) // P
                        for n in range(tiles):
                            i, c = v // 2 + 1 - tiles + n, slice(n * P, (n + 1) * P)
                            m = pe.matmul(dst, vr[:, b, i, :], pt[:, v % 2, c], start=n == 0, stop=n == tiles - 1)
                    else:
                        g = v - UNITS
                        pe.wait_ge(vc_in, h * (GROUPS * GB * 16) + GROUPS * GB * 16)
                        turned = lambda t: pt[:, v % 2, t * P:(t + 1) * P]
                        pe.matmul(dst, vr[:, b, NTP, :], turned(KT_S), start=True, stop=False)
                        for s in range(GB):
                            pick = lambda ap: ap.rearrange("p (h b q) -> p h b q", b=GB, q=DEC_S)[:, :, s, :]
                            for t in range(KT_S):
                                m = pe.matmul(pick(dst), vc[:, g, s, t, :], pick(turned(t)), start=False,
                                              stop=s == GB - 1 and t == KT_S - 1)
                    m.then_inc(o_filled, 1)

                for n in range(PREPS):
                    prepare(None, 0, n)

                def pair(h, b, last):
                    pe.wait_ge(q_scaled, h + 1)
                    pe.wait_ge(rows_done, h + 1)
                    for u in range(ALLU + 3 if last else ALLU):
                        if u < ALLU:
                            scores(h, b, u)
                        if not last and AT_FILL <= u < AT_FILL + PREPS:
                            prepare(h, 1 - b, u - AT_FILL)
                        if u in AT_KEYS:
                            turn_keys(h, AT_KEYS.index(u))
                        at, v = back(h, u, 2)
                        if v is not None:
                            turn_probs(at, v)
                        at, v = back(h, u, 3)
                        if v is not None:
                            out(at, b if v == u - 3 else 1 - b, v)

                pairs(pe, pair)

            @block.scalar
            def _(act):
                def is_filled(at):
                    act.wait_ge(turn_filled, at[2] + 1)
                    return tps[:, at[0], :]

                def scale_q(h, b):
                    act.wait_ge(qkv_in, h * 48 + 48)
                    act.activation(qs[:, b, :], qf[:], ACT.Copy, scale=-DH ** -0.5).then_inc(q_scaled, 1)

                def take(h, b, n, pair):
                    at = prep_fill(h, n)
                    src = is_filled(at)
                    if h is not None and n == 0:
                        act.wait_ge(cached, h * 64 + 64)
                    if n < 2:
                        act.copy(vr[:, b, 4 * n:4 * n + 4, :].rearrange("p i d -> p (i d)"), src).then_inc(taken[at[0]], 1)
                    elif n == 2:
                        act.copy(kr[:, :KEPT - 1, :].rearrange("p i d -> p (i d)"), src).then_inc(taken[at[0]], 1)
                    else:
                        act.copy(kr[:, KEPT - 1, :], src[:, :P])
                        act.copy(vr[:, b, NTP, :], src[:, P:2 * P]).then_inc(taken[at[0]], 1)
                        for m in range(2):
                            act.wait_ge(taken[m], prep_fill(h, 2 + m)[1] + 2)
                        act.sem_inc(rows_done, 1)
                        feats = bass.ds(pair * P, P)
                        for rows, nm in ((kr, "k"), (vr[:, b, NT - KEPT:], "v")):
                            act.dma_start(a[f"cache_{nm}_prompt"][0].rearrange("(i t) h d -> t i (h d)", t=P)[:, :, feats],
                                          rows[:, :KEPT - 1, :]).then_inc(cached, 16)
                            act.dma_start(a[f"cache_{nm}_sample"].rearrange("b s h d -> b s (h d)")[:, PAST - DEC_S:, feats],
                                          rows[:, KEPT - 1, :]).then_inc(cached, 16)

                def exponential(h, u):
                    w = width(u)
                    act.wait_ge(biased, h * ALLU + (u + 3))
                    act.activation(probs[:, u % 3, :w], probs[:, u % 3, :w], ACT.Exp, scale=-1.0,
                                   bias=top[:, u % 3:u % 3 + 1], accum_out=total[:, u % 3:u % 3 + 1]).then_inc(exped, 1)

                def take_probs(h, v):
                    at = fill(h, "probs", v, 0)
                    src = is_filled(at)
                    lo, hi = parts(v)[0]
                    act.copy(pt[:, v % 2, lo:hi], src[:, :hi - lo]).then_inc(taken[at[0]], 1)

                def take_out(h, v):
                    act.wait_ge(o_filled, h * ALLU + (v + 1))
                    flat = S.mixed[:].rearrange("p k t -> p (k t)")
                    if v < UNITS:
                        j, head = divmod(v, 2)
                        f = slice(head * DH, (head + 1) * DH)
                        act.copy(flat[f, bass.ds(h * TOK + j * P, P)], ops[f, v % 2, :P]).then_inc(o_taken, 1)
                    else:
                        g = v - UNITS
                        for head in range(2):
                            f = slice(head * DH, (head + 1) * DH)
                            m = act.copy(flat[f, bass.ds(h * TOK + (SEQ + g * GB * DEC_S), GB * DEC_S)],
                                         ops[f, v % 2, head * DH:(head + 1) * DH])
                        m.then_inc(o_taken, 1)

                scale_q(0, 0)
                for n in range(PREPS):
                    take(None, 0, n, 0)

                def pair(h, b, last):
                    for u in range(ALLU + 3 if last else ALLU):
                        if not last and u == AT_Q:
                            scale_q(h + 1, 1 - b)
                        if not last and AT_FILL <= u < AT_FILL + PREPS:
                            take(h, 1 - b, u - AT_FILL, h + 1)
                        if u in AT_KEYS:
                            g = AT_KEYS.index(u)
                            for n in range(2):
                                at = fill(h, "keys", g, n)
                                act.copy(kt[:, g, 2 * n:2 * n + 2, :].rearrange("p b t -> p (b t)"),
                                         is_filled(at)).then_inc(taken[at[0]], 1)
                        at, v = back(h, u, 2)
                        if v is not None:
                            take_probs(at, v)
                        if u < ALLU:
                            exponential(h, u)
                        at, v = back(h, u, 3)
                        if v is not None:
                            take_out(at, v)

                pairs(act, pair)
                act.wait_ge(cached, PAIRS * 64)

            @block.vector
            def _(dve):
                dve.sem_inc(biased, 2)
                dve.sem_inc(o_taken, 2)

                def add_bias(h, b, u):
                    w = width(u)
                    in1 = bias[:, b, u % 2, WIDE - w:] if u < UNITS else bias_s[:, b, u - UNITS, :]
                    dve.wait_ge(s_filled, h * ALLU + (u + 1))
                    at, v = back(h, u, 3)
                    if v is not None:
                        dve.wait_ge(turn_filled, fill(at, "probs", v, len(parts(v)) - 1)[2] + 1)
                    dve.sem_inc(paced, 1)
                    dve.tensor_tensor_reduce(probs[:, u % 3, :w], sps[:, u % 2, :w], in1, 1.0, 3e38, ALU.add,
                                             ALU.min, top[:, u % 3:u % 3 + 1]).then_inc(biased, 1)

                def normalise(h, v):
                    w, s = width(v), slice(v % 3, v % 3 + 1)
                    dve.wait_ge(exped, h * ALLU + (v + 1))
                    dve.reciprocal(rec[:, s], total[:, s]).then_inc(inverse, 1)
                    dve.wait_ge(inverse, h * ALLU + (v + 1))
                    dve.tensor_scalar(probs[:, v % 3, :w], probs[:, v % 3, :w], rec[:, s], None,
                                      ALU.mult).then_inc(scaled, 1)

                def take_probs(h, v):
                    if len(parts(v)) == 2:
                        at = fill(h, "probs", v, 1)
                        lo, hi = parts(v)[1]
                        dve.wait_ge(turn_filled, at[2] + 1)
                        dve.wait_ge(o_filled, h * ALLU + (v - 1))
                        dve.tensor_copy(pt[:, v % 2, lo:hi], tps[:, at[0], :hi - lo]).then_inc(taken[at[0]], 1)

                def pair(h, b, last):
                    dve.wait_ge(masked, h * (2 + GROUPS) + (2 + GROUPS))
                    for u in range(ALLU + 3 if last else ALLU):
                        if u < ALLU:
                            add_bias(h, b, u)
                        at, v = back(h, u, 1)
                        if v is not None:
                            normalise(at, v)
                        at, v = back(h, u, 2)
                        if v is not None:
                            take_probs(at, v)

                pairs(dve, pair)


def build(nc, a):
    with ExitStack() as ctx:
        def sb(name, shape, dt=F32):
            return ctx.enter_context(nc.sbuf_tensor(name, shape, dt))

        def dram(name, shape):
            return nc.dram_tensor(name, shape, F32, kind="Internal").ap()

        S = Shared()
        S.res = sb("res", [P, DK, TOK])
        S.ident, S.ones, S.eps = sb("ident", [P, P]), sb("ones", [P, P]), sb("eps", [P, 1])
        S.causal, S.stream, S.own_mask = sb("causal", [P, 2, P]), sb("stream", [P, DEC_B]), sb("own_mask", [P, 2, P])
        S.gains = sb("gains", [P, 6, DK])
        S.gla_rows, S.qkv_rows = dram("gla_rows", [GLA_IN, TOK]), dram("qkv_rows", [3 * D, TOK])
        S.strips = dram("strips", [HEADS, P, STRIP])
        S.caches_kept, S.strips_kept = nc.alloc_semaphore("caches_kept"), nc.alloc_semaphore("strips_kept")
        w_in = a["gla_w_in"][0]
        body = 2 * NQK + 2 * NV
        with nc.sbuf_tensor("bias_strip", [HEADS, STRIP], F32) as S.strip:
            constants(nc, S, a)
            load_tokens(nc, S, a)
            with ExitStack() as phase:
                operands(nc, S, phase, "in")
                project(nc, S, "in", G_MIX0, [(w_in, 0, body // P, None, S.gla_rows, 0, 0),
                                              (w_in, GLA_IN - P, 1, None, S.gla_rows, body, P - RANK)],
                        aside=keep_strips)
            with nc.sbuf_tensor("gla_mixed", [P, DK, TOK], F32) as S.mixed:
                gla_core(nc, S, a)
                add_product(nc, S, "go", a["gla_w_out"][0])
        with ExitStack() as phase:
            operands(nc, S, phase, "f0")
            ffn(nc, S, "f0", G_FFN0, a["ffn_w_gate"][0], a["ffn_w_up"][0], a["ffn_w_down"][0])
            project(nc, S, "qkv", None, [(a["attn_w_q"][0], 0, DK, G_MIX1, S.qkv_rows, 0, 0),
                                         (a["w_kv"], 0, 2 * DK, G_KV, S.qkv_rows, D, 0)])
        with nc.sbuf_tensor("att_mixed", [P, DK, TOK], F32) as S.mixed:
            attention_core(nc, S, a)
            add_product(nc, S, "ao", a["attn_w_out"][0])
        with ExitStack() as phase:
            operands(nc, S, phase, "f1")
            ffn(nc, S, "f1", G_FFN1, a["ffn_w_gate"][1], a["ffn_w_up"][1], a["ffn_w_down"][1])
        store_tokens(nc, S, a)


_INS = ["x_prompt", "x_sample", "state_gla", "cache_k", "cache_v", "norm_mix", "norm_ffn", "norm_final",
        "gla_w_in", "gla_w_gate2", "gla_b_gate", "gla_norm", "gla_w_out", "kv_norm", "w_kv", "attn_w_q",
        "attn_rel_bias", "attn_w_out", "ffn_w_gate", "ffn_w_up", "ffn_w_down"]
_OUTS = [("y_prompt", (1, SEQ, D)), ("y_sample", (DEC_B, DEC_S, D)),
         ("state_gla_prompt", (1, 1, GLA_H, GLA_DK, GLA_DV)),
         ("cache_k_prompt", (1, 512, HEADS, DH)), ("cache_v_prompt", (1, 512, HEADS, DH)),
         ("state_gla_sample", (1, DEC_B, GLA_H, GLA_DK, GLA_DV)),
         ("cache_k_sample", (DEC_B, PAST, HEADS, DH)), ("cache_v_sample", (DEC_B, PAST, HEADS, DH))]


def kernel(**inputs):
    import numpy as _np
    import concourse.bacc as _bacc
    from concourse.bass_utils import run_bass_kernel_spmd as _run

    nc = _bacc.Bacc("TRN2", target_bir_lowering=False, num_devices=1)
    arrays, args = {}, {}
    for name in _INS:
        arrays[f"in_{name}"] = _np.ascontiguousarray(inputs[name])
        args[name] = nc.dram_tensor(f"in_{name}", arrays[f"in_{name}"].shape, F32, kind="ExternalInput").ap()
    for name, shape in _OUTS:
        args[name] = nc.dram_tensor(f"out_{name}", shape, F32, kind="ExternalOutput").ap()
    build(nc, args)
    r = _run(nc, [arrays], core_ids=[0])
    return tuple(r.results[0][f"out_{name}"] for name, _ in _OUTS)
```
